# Optimizing a Trainium2 kernel written in Bass

```python
import math
import jax, jax.numpy as jnp
from jax import lax
import numpy as np

D_MODEL = 1024
BATCH = 1
SEQ = 256
DEPTH = 2

CTX_LEN = 256
GRID_W = 64
BLOCK_Q = 128
ROPE_THETA = 10000.0
NORM_EPS = 1e-6
NEG_INF = -1e30
HEAD_DIM = 64

MLA_HEADS = 8
MLA_Q_LORA = 384
MLA_KV_LORA = 256
MLA_NOPE = 64
MLA_ROPE = 32
MLA_V = 64
MLA_SCALE = (MLA_NOPE + MLA_ROPE) ** -0.5
MLA_IN_COLS = MLA_Q_LORA + MLA_KV_LORA + MLA_ROPE

DIFF_HEADS = 8
DIFF_D = 32
DIFF_V = 2 * DIFF_D
DIFF_SCALE = DIFF_D ** -0.5
EVEN_IN = MLA_IN_COLS + 2 * DIFF_HEADS * 2 * DIFF_D + DIFF_HEADS * DIFF_V
EVEN_OUT = MLA_HEADS * MLA_V + DIFF_HEADS * DIFF_V

WIN_HEADS = 8
WIN_KV_HEADS = 2
WINDOW = 128
GLB_HEADS = 8
GLB_KV_HEADS = 2
ATTN_SCALE = HEAD_DIM ** -0.5
ODD_IN = (WIN_HEADS + 2 * WIN_KV_HEADS + GLB_HEADS + 2 * GLB_KV_HEADS) * HEAD_DIM
ODD_OUT = (WIN_HEADS + GLB_HEADS) * HEAD_DIM

N_EXPERTS = 16
N_GROUPS = 4
EXPERTS_PER_GROUP = N_EXPERTS // N_GROUPS
GROUP_SCORE_TOPK = 2
TOP_K = 2
D_FF_EXPERT = 512

N_EVEN = (DEPTH + 1) // 2
N_ODD = DEPTH // 2

kernel_name = "hybrid_mla_diff_window_axial_moe_dit"

def rmsnorm(x, g):
    xf = x.astype(jnp.float32)
    y = xf * lax.rsqrt(jnp.mean(xf * xf, axis=-1, keepdims=True) + NORM_EPS)
    return (y * g.astype(jnp.float32)).astype(x.dtype)

def modulate(h, shift, scale):
    return h * (1.0 + scale) + shift

def split_heads(z, n_heads, hd):
    B, T, _ = z.shape
    return z.reshape(B, T, n_heads, hd).transpose(0, 2, 1, 3)

def merge_heads(o):
    B, H, T, hd = o.shape
    return o.transpose(0, 2, 1, 3).reshape(B, T, H * hd)

def axial_tables(rows, rot_dim):
    half = rot_dim // 2
    inv_freq = ROPE_THETA ** (-jnp.arange(0, half, 2, dtype=jnp.float32) / half)
    row = jnp.broadcast_to(jnp.arange(rows, dtype=jnp.float32)[:, None], (rows, GRID_W)).reshape(-1)
    col = jnp.broadcast_to(jnp.arange(GRID_W, dtype=jnp.float32)[None, :], (rows, GRID_W)).reshape(-1)

    def tab(pos):
        ang = pos[:, None] * inv_freq[None, :]
        ang = jnp.concatenate([ang, ang], axis=-1)
        return jnp.cos(ang), jnp.sin(ang)

    return tab(row) + tab(col)

def rotate_half(x):
    h = x.shape[-1] // 2
    return jnp.concatenate([-x[..., h:], x[..., :h]], axis=-1)

def apply_rope(x, tabs):
    cos_r, sin_r, cos_c, sin_c = tabs
    h = x.shape[-1] // 2
    xr, xc = x[..., :h], x[..., h:]
    out = jnp.concatenate([xr * cos_r + rotate_half(xr) * sin_r,
                           xc * cos_c + rotate_half(xc) * sin_c], axis=-1)
    return out.astype(x.dtype)

def softmax_with_sink(s, sink):
    if sink is None:
        return jax.nn.softmax(s, axis=-1)
    snk = sink.astype(jnp.float32).reshape((1, s.shape[1], s.shape[2]) + (1,) * (s.ndim - 3))
    m = jnp.maximum(jnp.max(s, axis=-1, keepdims=True), snk)
    e = jnp.exp(s - m)
    return e / (jnp.sum(e, axis=-1, keepdims=True) + jnp.exp(snk - m))

def dense_attend(q, k, v, scale, sink=None):
    B, Hq, T, dk = q.shape
    Hk, dv = k.shape[1], v.shape[-1]
    G = Hq // Hk
    nb = T // BLOCK_Q
    qb = q.reshape(B, Hk, G, nb, BLOCK_Q, dk).transpose(3, 0, 1, 2, 4, 5)

    def one(qi):
        s = jnp.einsum("bhgqd,bhkd->bhgqk", qi, k).astype(jnp.float32) * scale
        p = softmax_with_sink(s, sink)
        return jnp.einsum("bhgqk,bhkd->bhgqd", p.astype(v.dtype), v)

    o = lax.map(one, qb)
    return o.transpose(1, 2, 3, 0, 4, 5).reshape(B, Hq, T, dv)

def window_attend(q, k, v, k_ctx, v_ctx, sink, scale):
    B, Hq, T, d = q.shape
    Hk = k.shape[1]
    G = Hq // Hk
    nb = T // BLOCK_Q
    pad = ((0, 0), (0, 0), (BLOCK_Q, BLOCK_Q), (0, 0))
    kp, vp = jnp.pad(k, pad), jnp.pad(v, pad)
    qb = q.reshape(B, Hk, G, nb, BLOCK_Q, d).transpose(3, 0, 1, 2, 4, 5)
    band = 3 * BLOCK_Q
    offs = jnp.arange(band) - BLOCK_Q
    qoff = jnp.arange(BLOCK_Q)

    def one(args):
        i, qi = args
        start = i * BLOCK_Q
        ki = lax.dynamic_slice_in_dim(kp, start, band, axis=2)
        vi = lax.dynamic_slice_in_dim(vp, start, band, axis=2)
        kpos = start + offs
        qpos = start + qoff
        valid = ((jnp.abs(kpos[None, :] - qpos[:, None]) <= WINDOW)
                 & (kpos >= 0)[None, :] & (kpos < T)[None, :])
        s_loc = jnp.einsum("bhgqd,bhkd->bhgqk", qi, ki).astype(jnp.float32) * scale
        s_loc = jnp.where(valid, s_loc, NEG_INF)
        s_ctx = jnp.einsum("bhgqd,bhcd->bhgqc", qi, k_ctx).astype(jnp.float32) * scale
        p = softmax_with_sink(jnp.concatenate([s_loc, s_ctx], axis=-1), sink).astype(v.dtype)
        return (jnp.einsum("bhgqk,bhkd->bhgqd", p[..., :band], vi)
                + jnp.einsum("bhgqc,bhcd->bhgqd", p[..., band:], v_ctx))

    o = lax.map(one, (jnp.arange(nb), qb))
    return o.transpose(1, 2, 3, 0, 4, 5).reshape(B, Hq, T, d)

def cat_tokens(a, b):
    return jnp.concatenate([a, b], axis=2)

def mla_qkv(z, norm_q, norm_kv, w_uq, w_ukv, tabs):
    o1 = MLA_Q_LORA
    o2 = o1 + MLA_KV_LORA
    o3 = o2 + MLA_ROPE
    c_q = rmsnorm(z[..., :o1], norm_q)
    c_kv = rmsnorm(z[..., o1:o2], norm_kv)
    k_rope = z[..., o2:o3][:, None]
    q = split_heads(c_q @ w_uq, MLA_HEADS, MLA_NOPE + MLA_ROPE)
    kv = split_heads(c_kv @ w_ukv, MLA_HEADS, MLA_NOPE + MLA_V)
    q_nope, q_rope = q[..., :MLA_NOPE], q[..., MLA_NOPE:]
    k_nope, v = kv[..., :MLA_NOPE], kv[..., MLA_NOPE:]
    if tabs is not None:
        q_rope = apply_rope(q_rope, tabs)
        k_rope = apply_rope(k_rope, tabs)
    k_rope = jnp.broadcast_to(k_rope, k_nope.shape[:-1] + (MLA_ROPE,))
    return (jnp.concatenate([q_nope, q_rope], axis=-1),
            jnp.concatenate([k_nope, k_rope], axis=-1), v)

def diff_qkv(z, tabs):
    B, T, _ = z.shape
    o0 = MLA_IN_COLS
    nq = DIFF_HEADS * 2 * DIFF_D
    q = z[..., o0:o0 + nq].reshape(B, T, DIFF_HEADS, 2, DIFF_D).transpose(3, 0, 2, 1, 4)
    k = z[..., o0 + nq:o0 + 2 * nq].reshape(B, T, DIFF_HEADS, 2, DIFF_D).transpose(3, 0, 2, 1, 4)
    v = split_heads(z[..., o0 + 2 * nq:o0 + 2 * nq + DIFF_HEADS * DIFF_V], DIFF_HEADS, DIFF_V)
    if tabs is not None:
        q = apply_rope(q, tabs)
        k = apply_rope(k, tabs)
    return q[0], q[1], k[0], k[1], v

def even_mixer(h_lat, h_ctx, w_in, norm_q, norm_kv, w_uq, w_ukv, lam, subln, w_out,
               tabs_mla, tabs_diff, lam_init, with_ctx):
    z_lat, z_ctx = h_lat @ w_in, h_ctx @ w_in
    qa, ka, va = mla_qkv(z_lat, norm_q, norm_kv, w_uq, w_ukv, tabs_mla)
    qa_c, ka_c, va_c = mla_qkv(z_ctx, norm_q, norm_kv, w_uq, w_ukv, None)
    q1, q2, k1, k2, vb = diff_qkv(z_lat, tabs_diff)
    q1_c, q2_c, k1_c, k2_c, vb_c = diff_qkv(z_ctx, None)
    lam = lam.astype(jnp.float32)
    lam_full = jnp.exp(jnp.sum(lam[0] * lam[1])) - jnp.exp(jnp.sum(lam[2] * lam[3])) + lam_init

    def merge(oa, o1, o2):
        ob = rmsnorm((o1 - lam_full * o2).astype(o1.dtype), subln) * (1.0 - lam_init)
        return jnp.concatenate([merge_heads(oa), merge_heads(ob)], axis=-1) @ w_out

    vb_all = cat_tokens(vb, vb_c)
    y_lat = merge(dense_attend(qa, cat_tokens(ka, ka_c), cat_tokens(va, va_c), MLA_SCALE),
                  dense_attend(q1, cat_tokens(k1, k1_c), vb_all, DIFF_SCALE),
                  dense_attend(q2, cat_tokens(k2, k2_c), vb_all, DIFF_SCALE))
    y_ctx = None
    if with_ctx:
        y_ctx = merge(dense_attend(qa_c, ka_c, va_c, MLA_SCALE),
                      dense_attend(q1_c, k1_c, vb_c, DIFF_SCALE),
                      dense_attend(q2_c, k2_c, vb_c, DIFF_SCALE))
    return y_lat, y_ctx

def odd_mixer(h_lat, h_ctx, w_in, sink, q_norm, k_norm, w_out, tabs, with_ctx):
    sizes = (WIN_HEADS, WIN_KV_HEADS, WIN_KV_HEADS, GLB_HEADS, GLB_KV_HEADS, GLB_KV_HEADS)

    def proj(h, tb):
        z = h @ w_in
        parts, off = [], 0
        for n in sizes:
            parts.append(split_heads(z[..., off * HEAD_DIM:(off + n) * HEAD_DIM], n, HEAD_DIM))
            off += n
        qc, kc, vc, qd, kd, vd = parts
        qd, kd = rmsnorm(qd, q_norm), rmsnorm(kd, k_norm)
        if tb is not None:
            qc, kc, qd, kd = apply_rope(qc, tb), apply_rope(kc, tb), apply_rope(qd, tb), apply_rope(kd, tb)
        return qc, kc, vc, qd, kd, vd

    qc, kc, vc, qd, kd, vd = proj(h_lat, tabs)
    qc_c, kc_c, vc_c, qd_c, kd_c, vd_c = proj(h_ctx, None)

    def merge(oc, od):
        return jnp.concatenate([merge_heads(oc), merge_heads(od)], axis=-1) @ w_out

    y_lat = merge(window_attend(qc, kc, vc, kc_c, vc_c, sink, ATTN_SCALE),
                  dense_attend(qd, cat_tokens(kd, kd_c), cat_tokens(vd, vd_c), ATTN_SCALE))
    y_ctx = None
    if with_ctx:
        y_ctx = merge(dense_attend(qc_c, kc_c, vc_c, ATTN_SCALE, sink),
                      dense_attend(qd_c, kd_c, vd_c, ATTN_SCALE))
    return y_lat, y_ctx

def moe_ffn(h, w_router, b_router, w_gate, w_up, w_down):
    n = h.shape[0]
    s = jax.nn.sigmoid((h @ w_router).astype(jnp.float32))
    sel = (s + b_router.astype(jnp.float32)).reshape(n, N_GROUPS, EXPERTS_PER_GROUP)
    group_score = jnp.sum(lax.top_k(sel, GROUP_SCORE_TOPK)[0], axis=-1)
    g = jnp.argmax(group_score, axis=-1)
    in_group = jnp.take_along_axis(sel, g[:, None, None], axis=1)[:, 0]
    _, local = lax.top_k(in_group, TOP_K)
    idx = g[:, None] * EXPERTS_PER_GROUP + local
    w = jnp.take_along_axis(s, idx, axis=-1)
    w = w / jnp.sum(w, axis=-1, keepdims=True)
    combine = jnp.sum(jax.nn.one_hot(idx, N_EXPERTS, dtype=jnp.float32) * w[..., None], axis=1).astype(h.dtype)
    out = jnp.zeros_like(h)
    for e in range(N_EXPERTS):
        y = (jax.nn.silu(h @ w_gate[e]) * (h @ w_up[e])) @ w_down[e]
        out = out + combine[:, e:e + 1] * y
    return out

def setup_inputs(seed: int = 0) -> dict:
    key = jax.random.key(seed)
    ks = iter(jax.random.split(key, 32))
    f32 = jnp.float32
    D = D_MODEL

    def nrm(shape, scale):
        return jax.random.normal(next(ks), shape, f32) * scale

    def gain(shape):
        return 1.0 + nrm(shape, 0.02)

    return {
        "x": nrm((BATCH, SEQ, D), 1.0),
        "c": nrm((BATCH, D), 1.0),
        "ctx": nrm((BATCH, CTX_LEN, D), 1.0),
        "c_ctx": nrm((D,), 1.0),
        "w_mod": nrm((DEPTH, D, 6 * D), 0.5 * D ** -0.5),
        "b_mod": nrm((DEPTH, 6 * D), 0.01),
        "norm_mix": gain((DEPTH, D)),
        "norm_ffn": gain((DEPTH, D)),
        "even_w_in": nrm((N_EVEN, D, EVEN_IN), D ** -0.5),
        "even_norm_q": gain((N_EVEN, MLA_Q_LORA)),
        "even_norm_kv": gain((N_EVEN, MLA_KV_LORA)),
        "even_w_uq": nrm((N_EVEN, MLA_Q_LORA, MLA_HEADS * (MLA_NOPE + MLA_ROPE)), MLA_Q_LORA ** -0.5),
        "even_w_ukv": nrm((N_EVEN, MLA_KV_LORA, MLA_HEADS * (MLA_NOPE + MLA_V)), MLA_KV_LORA ** -0.5),
        "even_lambda": nrm((N_EVEN, 4, DIFF_D), 0.1),
        "even_subln": gain((N_EVEN, DIFF_V)),
        "even_w_out": nrm((N_EVEN, EVEN_OUT, D), EVEN_OUT ** -0.5),
        "odd_w_in": nrm((N_ODD, D, ODD_IN), D ** -0.5),
        "odd_sink": nrm((N_ODD, WIN_HEADS), 0.5),
        "odd_q_norm": gain((N_ODD, HEAD_DIM)),
        "odd_k_norm": gain((N_ODD, HEAD_DIM)),
        "odd_w_out": nrm((N_ODD, ODD_OUT, D), ODD_OUT ** -0.5),
        "w_router": nrm((D, N_EXPERTS), D ** -0.5),
        "b_router": nrm((N_EXPERTS,), 0.01),
        "w_gate": nrm((DEPTH, N_EXPERTS, D, D_FF_EXPERT), D ** -0.5),
        "w_up": nrm((DEPTH, N_EXPERTS, D, D_FF_EXPERT), D ** -0.5),
        "w_down": nrm((DEPTH, N_EXPERTS, D_FF_EXPERT, D), D_FF_EXPERT ** -0.5),
        "norm_final": gain((D,)),
    }

def reference(x, c, ctx, c_ctx, w_mod, b_mod, norm_mix, norm_ffn,
              even_w_in, even_norm_q, even_norm_kv, even_w_uq, even_w_ukv, even_lambda, even_subln, even_w_out,
              odd_w_in, odd_sink, odd_q_norm, odd_k_norm, odd_w_out,
              w_router, b_router, w_gate, w_up, w_down, norm_final):
    B, T, D = x.shape
    rows = T // GRID_W
    tabs_mla = axial_tables(rows, MLA_ROPE)
    tabs_diff = axial_tables(rows, DIFF_D)
    tabs_attn = axial_tables(rows, HEAD_DIM)
    silu_c = jax.nn.silu(c)
    silu_cc = jax.nn.silu(c_ctx)
    cx = ctx
    n_ctx_tok = B * CTX_LEN
    for l in range(DEPTH):
        with_ctx = l < DEPTH - 1
        i = l // 2
        mod = (silu_c @ w_mod[l] + b_mod[l])[:, None, :]
        mod_c = silu_cc @ w_mod[l] + b_mod[l]
        sh_a, sc_a, g_a, sh_f, sc_f, g_f = jnp.split(mod, 6, axis=-1)
        ch_a, cs_a, cg_a, ch_f, cs_f, cg_f = jnp.split(mod_c, 6, axis=-1)
        h_lat = modulate(rmsnorm(x, norm_mix[l]), sh_a, sc_a)
        h_ctx = modulate(rmsnorm(cx, norm_mix[l]), ch_a, cs_a)
        if l % 2 == 0:
            lam_init = 0.8 - 0.6 * math.exp(-0.3 * l)
            y_lat, y_ctx = even_mixer(h_lat, h_ctx, even_w_in[i], even_norm_q[i], even_norm_kv[i],
                                      even_w_uq[i], even_w_ukv[i], even_lambda[i], even_subln[i],
                                      even_w_out[i], tabs_mla, tabs_diff, lam_init, with_ctx)
        else:
            y_lat, y_ctx = odd_mixer(h_lat, h_ctx, odd_w_in[i], odd_sink[i], odd_q_norm[i],
                                     odd_k_norm[i], odd_w_out[i], tabs_attn, with_ctx)
        x = x + g_a * y_lat
        h_lat = modulate(rmsnorm(x, norm_ffn[l]), sh_f, sc_f)
        if with_ctx:
            cx = cx + cg_a * y_ctx
            h_ctx = modulate(rmsnorm(cx, norm_ffn[l]), ch_f, cs_f)
            tok = jnp.concatenate([h_ctx.reshape(-1, D), h_lat.reshape(-1, D)], axis=0)
            y = moe_ffn(tok, w_router, b_router, w_gate[l], w_up[l], w_down[l])
            cx = cx + cg_f * y[:n_ctx_tok].reshape(B, CTX_LEN, D)
            x = x + g_f * y[n_ctx_tok:].reshape(B, T, D)
        else:
            y = moe_ffn(h_lat.reshape(-1, D), w_router, b_router, w_gate[l], w_up[l], w_down[l])
            x = x + g_f * y.reshape(B, T, D)
    return rmsnorm(x, norm_final)


_drawn_inputs = setup_inputs


def setup_inputs(seed=0):
    import zlib

    import numpy as np

    out = dict(_drawn_inputs(seed))
    spreads = {}
    factors = {'norm_mix': 3.488,
     'even_norm_q': 8.0,
     'even_norm_kv': 8.0,
     'even_subln': 5.242,
     'odd_sink': 8.0,
     'odd_q_norm': 8.0,
     'odd_k_norm': 8.0,
     'norm_final': 2.801}
    for name, (base, spread) in spreads.items():
        noise = np.random.default_rng([zlib.crc32(name.encode()), seed]).standard_normal(out[name].shape)
        drawn = base * np.exp(spread * noise) if base else spread * noise
        out[name] = __import__('jax').numpy.asarray(drawn.astype(out[name].dtype))
    for name, factor in factors.items():
        out[name] = (out[name] * factor).astype(out[name].dtype)
    return out
```

```python
import math
from contextlib import ExitStack

import numpy as np

import concourse.bass as bass
from concourse import mybir

P = 128
D = 1024
KD = D // P
SEQ, CTX = 256, 256
NT = (SEQ + CTX) // P
LT = SEQ // P
NTOK = SEQ + CTX
DEPTH = 2
GRID_W = 64
EPS = 1e-6
CH = 512
SLOTS = 6
SLOT = KD * CH
MODC = 6 * D // CH
QL, KVL, RD, NOPE, MV, MH = 384, 256, 32, 64, 64, 8
QD = NOPE + RD
DH, DD, DV = 8, 32, 64
EV_IN = QL + KVL + RD + 2 * DH * 2 * DD + DH * DV
EV_CH = [(0, QL), (QL, KVL + RD), (672, 512), (1184, 512), (1696, 512)]
ZQ, ZK, ZV = 672, 1184, 1696
HD = 64
OD_IN = 1536
OD_CH = [(0, 512, LT), (512, 256, NT), (768, 512, LT), (1280, 256, NT)]
LAM_INIT = 0.8 - 0.6 * math.exp(-0.3 * 0)
MLA_SCALE, DIFF_SCALE, ATT_SCALE = QD ** -0.5, DD ** -0.5, HD ** -0.5
NE, NG, EG, FF = 16, 4, 4, 512
TL = [NT, LT]
ROUNDS = [t - 1 for t in TL]
ROWS = NTOK * NE

CONSTS = [("ident", P), ("ones", P), ("tri", P), ("cos32", LT * 32), ("sin32", LT * 32),
          ("cosT", SEQ), ("sinT", SEQ), ("rot", 32),
          ("cos64", LT * 64), ("sin64", LT * 64), ("wmask", 2 * P), ("lower", EG * EG),
          ("eidx", NE), ("tokid", NT), ("eps", 1)]


def shape_constants():
    c = {}
    p = np.arange(P)
    c["ident"] = np.eye(P)
    c["ones"] = np.ones((P, P))
    c["tri"] = (p[:, None] < p[None, :])
    t = np.arange(SEQ)

    def tables(rot):
        half = rot // 2
        inv = (np.float32(10000.0) ** (-np.arange(0, half, 2, dtype=np.float32) / np.float32(half))).astype(np.float32)
        cos, sin = [], []
        for pos in (t // GRID_W, t % GRID_W):
            ang = pos.astype(np.float32)[:, None] * inv[None, :]
            cos += [np.cos(ang), np.cos(ang)]
            sin += [-np.sin(ang), np.sin(ang)]
        return np.concatenate(cos, 1), np.concatenate(sin, 1)
    for rot in (32, 64):
        cos, sin = tables(rot)
        c[f"cos{rot}"] = cos.reshape(LT, P, rot).transpose(1, 0, 2).reshape(P, -1)
        c[f"sin{rot}"] = sin.reshape(LT, P, rot).transpose(1, 0, 2).reshape(P, -1)
    cos, sin = tables(32)
    tall = np.zeros((P, SEQ)); tall[64:96] = cos.T; c["cosT"] = tall
    tall = np.zeros((P, SEQ)); tall[64:96] = sin.T; c["sinT"] = tall
    rot = np.zeros((P, 32))
    for m in range(32):
        rot[64 + (m // 16) * 16 + (m % 16 + 8) % 16, m] = 1.0
    c["rot"] = rot
    far = np.zeros((P, 2, P))
    far[:, 0][p[None, :] > p[:, None]] = -1e30
    far[:, 1][p[None, :] < p[:, None]] = -1e30
    c["wmask"] = far.reshape(P, -1)
    i = np.arange(EG)
    c["lower"] = np.broadcast_to((i[None, :] < i[:, None]).reshape(1, -1), (P, EG * EG))
    c["eidx"] = np.broadcast_to(np.arange(NE)[None], (P, NE))
    c["tokid"] = p[:, None] + P * np.arange(NT)[None, :]
    c["eps"] = np.full((P, 1), EPS)
    return np.concatenate([np.asarray(c[n], np.float32).reshape(P, w) for n, w in CONSTS], 1)


def build(nc, a, consts_dram, out_dram, dbg=None, cap=P):
    f32, i32, bf16 = mybir.dt.float32, mybir.dt.int32, mybir.dt.bfloat16
    ALU = mybir.AluOpType
    ACT = mybir.ActivationFunctionType
    AX = mybir.AxisListType.X
    ds = bass.ds
    ctx = ExitStack()
    layer0_total = {
        "mod_row{}": MODC, "mod_cols{}": MODC, "mod_T{}": MODC, "scol{}": 4, "sumsq{}": NT, "xn_ready{}": NT,
        "xT0_{}": KD // 2, "xT1_{}": KD // 2, "hT0_{}": KD, "hT1_{}": KD,
        "z_v{}": 10, "z_a{}": 10, "z_mm{}": len(EV_CH) * (NT - 1),
        "s_ready{}": 96, "max_ready{}": 96, "p_ready{}": 96, "t_ready{}": 96, "pT_ready{}": 96, "pv_done{}": 96,
        "out_mm{}": 2 * (NT - 1), "out_v{}": 2 * NT, "x_add{}": 2 * NT,
        "sumsq_f{}": NT, "h_scaled{}": NT, "h_ready{}": NT, "h_stored{}": 16 * NT, "h_tr{}": KD, "h_v{}": KD // 2, "h_a{}": KD // 2,
        "logits{}": 1, "sig{}": 1, "mask{}": 1, "counts{}": 1, "idx{}": 2, "flag_set{}": 1, "listed{}": 32 * NT, "slots{}": 16,
        "xg_loaded{}_0": 8 * NE, "xg_loaded{}_1": 8 * NE, "xT_lo{}": NE, "xT_hi{}": NE, "xgT_v{}": NE, "xgT_a{}": NE,
        "silu_ready{}": NE, "act_ready{}": NE, "act_tr{}": NE, "actT_ready{}": NE, "y_mm{}": NE, "y_v{}": NE, "y_a{}": NE,
        "y_stored{}_0": 8 * NE, "y_stored{}_1": 8 * NE,
        "ya_loaded{}_0": 32, "ya_loaded{}_1": 32, "yb_loaded{}_0": 32, "yb_loaded{}_1": 32, "x_moe{}": NT,
    }
    sems, alias = {}, {}
    for n, total in layer0_total.items():
        for l in range(DEPTH):
            alias[n.format(l)] = (n.format(""), l * total)
    for kind, stages in (("blocks", [("dT", 8), ("oT0", 8), ("gT", 8), ("oT1", 8)]),
                         ("rows", [("bc0", 6), ("gf0", 2), ("bc1", 3), ("gf1", 1)])):
        at = 0
        for n, count in stages:
            for part, share in ((("tr", 1), ("v", 2), ("a", 2)) if kind == "blocks" else
                                (("diag", 1), ("mm", 1), ("v", 1), ("a", 1))):
                alias[f"{n}_{part}"] = (f"{kind}_{part}", at // share)
            at += count

    def sem(name):
        n = alias.get(name, (name, 0))[0]
        if n not in sems:
            sems[n] = ctx.enter_context(nc.semaphore(n))
        return sems[n]

    def at(name, value):
        return value + alias.get(name, (name, 0))[1]

    def sb(name, shape, dt=f32):
        return ctx.enter_context(nc.sbuf_tensor(name, shape, dt))

    h_dram = [nc.dram_tensor(f"h_rows{l}", [(NT if l == 0 else LT) * P, D], f32).ap() for l in range(DEPTH)]
    list_dram = [nc.dram_tensor(f"slot_list{l}", [ROWS, 1], i32).ap() for l in range(DEPTH)]
    y_dram = [nc.dram_tensor(f"y_rows{l}", [TL[l] * P * NE, D], f32).ap() for l in range(DEPTH)]

    with ctx:
        ring = sb("ring", [P, SLOTS * SLOT])
        x = sb("x", [P, NT * D])
        rh = sb("region_h", [P, 4096])
        rz = sb("region_z", [P, NT * EV_IN])
        rq = sb("region_q", [P, 4096])
        rk = sb("region_k", [P, 4096])
        NCON = sum(w for _, w in CONSTS)
        con = sb("con", [P, NCON])
        small = sb("small", [P, 1283])
        small_i = sb("small_i", [P, 96], i32)
        bank = [ctx.enter_context(nc.psum_tensor(f"bank{i}", [P, 512], f32)) for i in range(8)]

        off = {}
        o = 0
        for n, w in CONSTS:
            off[n] = (o, w)
            o += w

        def const(n):
            return con[:, off[n][0]:off[n][0] + off[n][1]]
        so = [0]

        def sm(w):
            so[0] += w
            assert so[0] <= 1283, so[0]
            return small[:, so[0] - w:so[0]]
        ident, ones, tri = const("ident"), const("ones"), const("tri")
        colv = sm(56)
        C_C, C_NM, C_NF, C_NQ, C_NKV = 0, 16, 32, 48, 51
        bmodT = sm(96)
        modT = sm(2 * 96)
        silu = sm(16)
        scols = [sm(32), sm(32)]
        stat = sm(8)
        rstd = sm(8)
        lamv = sm(4)
        nsink, nsk, nrm = sm(8), sm(16), sm(10)
        nmx = sm(64)
        roots = sm(10)
        rsum = sm(64)
        rinv = sm(64)
        tokid_i = small_i[:, 0:4]
        idx_hi = small_i[:, 4:8]
        idx_lo = small_i[:, 8:12]
        slots_i = small_i[:, 12:28]
        zeros_i = small_i[:, 32:96]
        kdup = rk[:, 2048:4096]
        flag_i = [small_i[:, 30 + l:31 + l] for l in range(DEPTH)]

        def mod(l, s, r):
            return modT.rearrange("p (l s k r) -> p l s k r", l=2, s=6, r=2)[:, l, s, :, r]
        xt = x[:, :].rearrange("p (t d) -> p t d", t=NT)
        hT = rh[:, :].rearrange("p (k n) -> p k n", k=KD)
        xn = rz[:, 0:4096].rearrange("p (t d) -> p t d", t=NT)
        slot = [ring[:, i * SLOT:(i + 1) * SLOT] for i in range(SLOTS)]
        slotk = [s.rearrange("p (k n) -> p k n", k=KD) for s in slot]
        bc = [rz[:, i * D:(i + 1) * D] for i in range(6)]
        diag = [rh[:, i * D:(i + 1) * D] for i in range(2)]

        modrow = [rk[0:2, i * CH:(i + 1) * CH] for i in range(2)]
        z = rz[:, :].rearrange("p (t n) -> p t n", t=NT)
        zo = rz[:, 0:NT * OD_IN].rearrange("p (t n) -> p t n", t=NT)
        cT = hT
        qT = rq[:, :].rearrange("p (h n) -> p h n", h=MH)
        kT = rk[:, :].rearrange("p (h n) -> p h n", h=MH)
        probs = [rh[:, i * 512:(i + 1) * 512] for i in range(4)]
        probsT = [rh[:, (4 + i) * 512:(5 + i) * 512] for i in range(2)]
        tmp = [rh[:, (6 + i) * 512:(7 + i) * 512] for i in range(2)]
        dqT = rq[:, 0:2048].rearrange("p (b n) -> p b n", b=4)
        dkT = rq[:, 2048:4096].rearrange("p (b n) -> p b n", b=4)
        oT = rq[:, :].rearrange("p (k n) -> p k n", k=KD)
        goT = rq[:, 0:KD * SEQ].rearrange("p (b n) -> p b n", b=KD)
        gkT = rk[:, 0:2048].rearrange("p (b n) -> p b n", b=4)
        htok = rq[:, :].rearrange("p (t d) -> p t d", t=NT)
        xg = [rk[:, i * D:(i + 1) * D] for i in range(2)]
        ybuf = [rk[:, (2 + i) * D:(3 + i) * D] for i in range(2)]
        xgT = [rq[:, i * D:(i + 1) * D].rearrange("p (k n) -> p k n", k=KD) for i in range(2)]
        sg = [rh[:, i * 512:(i + 1) * 512] for i in range(2)]
        act_ = [rh[:, (2 + i) * 512:(3 + i) * 512] for i in range(2)]
        actT = [rh[:, (4 + i) * 512:(5 + i) * 512].rearrange("p (j n) -> p j n", j=4) for i in range(2)]
        ya = [rq[:, i * D:(i + 1) * D] for i in range(2)]
        yb = [rq[:, (2 + i) * D:(3 + i) * D] for i in range(2)]
        ow = rz[:, 2 * D:2 * D + 4096]
        over_w = [ow.rearrange("p (k n) -> p k n", k=KD), ow.rearrange("p (k n) -> p k n", k=KD),
                  ow.rearrange("p (k n) -> p k n", k=4)]
        ro = [6 * D]

        def rt(w):
            ro[0] += w
            assert ro[0] <= NT * EV_IN
            return rz[:, ro[0] - w:ro[0]]
        r_s, r_sel, r_beat, r_eq = rt(64), rt(64), rt(256), rt(256)
        r_top, r_gs, r_mask, r_w, r_pos, r_val, r_t = rt(64), rt(16), rt(64), rt(64), rt(64), rt(64), rt(64)
        r_gb, r_hi, r_lo, r_whi, r_wlo, r_sum, r_cnt = rt(64), rt(4), rt(4), rt(4), rt(4), rt(4), rt(16)
        wr_sb, br_sb = sm(KD * NE), sm(NE)
        subln_b, lam_b = sm(64), sm(128)
        sink_b, qk_b = sm(8), sm(128)

        M0 = 0
        E0 = M0 + MODC
        M1 = E0 + len(EV_CH)
        U0 = M1 + MODC
        O0 = U0 + 2
        X0 = O0 + 2
        E1 = X0 + 3 * NE
        O1 = E1 + len(OD_CH)
        X1 = O1 + 2
        END = X1 + 3 * NE

        def view(w, cols, o=0):
            return w[:, o:o + cols].rearrange("(k p) n -> p k n", p=P)
        chunks_used = sem("chunks_used")
        full = [sem(f"slot_full{i}") for i in range(SLOTS)]

        def arrived(eng, n, it=None, step=1):
            v = 16 * (n // SLOTS + 1)
            eng.wait_ge(full[n % SLOTS], v if it is None else it * (16 * step) + v)

        def product_done(eng, name, base, tiles, i, t):
            if t == tiles[i] - 1:
                eng.wait_ge(chunks_used, base + i + 1)
            else:
                eng.wait_ge(sem(name), at(name, sum(n - 1 for n in tiles[:i]) + t + 1))

        def latent_done(eng, g):
            if g in (MH - 1, 2 * MH + NT - 1):
                eng.wait_ge(chunks_used, U0 + (1 if g < MH else 2))
            else:
                eng.wait_ge(sem("lat_mm"), at("lat_mm", g + (1 if g < MH else 0)))

        block = ctx.enter_context(nc.Block())

        @block.sync
        def _(sp):
            def load(n, dst, src, it=None, step=1):
                if n >= SLOTS or it is not None:
                    v = n - SLOTS + 1
                    sp.wait_ge(chunks_used, v if it is None else it * (SLOTS * step) + v)
                sp.dma_start(dst, src).then_inc(full[n % SLOTS], 16)

            s_v = sem("small_loaded")
            sp.dma_start(con[:, :], consts_dram).then_inc(s_v, 16)
            vecs = rq[:, 0:P]
            rows = [(a["c"].rearrange("a (k p) -> (a k) p", p=P), 8),
                    (a["c_ctx"].rearrange("(k p) -> k p", p=P), 8),
                    (a["norm_mix"].rearrange("l (k p) -> (l k) p", p=P), 16),
                    (a["norm_ffn"].rearrange("l (k p) -> (l k) p", p=P), 16),
                    (a["even_norm_q"].rearrange("l (k p) -> (l k) p", p=P), 3),
                    (a["even_norm_kv"].rearrange("l (k p) -> (l k) p", p=P), 2)]
            wide = [(subln_b, a["even_subln"][0]), (lam_b, a["even_lambda"][0].rearrange("a b -> (a b)")),
                    (sink_b, a["odd_sink"][0]), (qk_b[:, 0:64], a["odd_q_norm"][0]), (qk_b[:, 64:128], a["odd_k_norm"][0]),
                    (br_sb, a["b_router"])]
            for dst, src in wide:
                sp.dma_start(dst, src.partition_broadcast(P)).then_inc(sem("wide_loaded"), 16)
            sp.dma_start(wr_sb.rearrange("p (k e) -> p k e", k=KD), a["w_router"].rearrange("(k p) e -> p k e", p=P)).then_inc(sem("wide_loaded"), 16)
            r = 0
            for src, n in rows:
                sp.dma_start(vecs[r:r + n, :], src).then_inc(s_v, 16)
                r += n
            sp.dma_start(rq[0:96, P:2 * P], a["b_mod"].rearrange("l (k p) -> (l k) p", p=P)).then_inc(s_v, 16)
            sp.dma_start(xt[:, 0:LT, :], a["x"].rearrange("a (t p) d -> p (a t) d", p=P)).then_inc(sem("x_loaded"), 16)
            sp.dma_start(xt[:, LT:NT, :], a["ctx"].rearrange("a (t p) d -> p (a t) d", p=P)).then_inc(sem("x_loaded"), 16)

            def modulation(base, l):
                w = a["w_mod"][l]
                if base == 0:
                    for j in range(SLOTS):
                        load(j, slotk[j], view(w, CH, j * CH))
                    for j in range(SLOTS):
                        load(SLOTS + j, slotk[j], view(w, CH, (SLOTS + j) * CH))
                else:
                    with sp.Fori(0, MODC // SLOTS) as it:
                        for j in range(SLOTS):
                            n = base + j
                            load(n, slotk[n % SLOTS], w[:, ds(it * (SLOTS * CH) + j * CH, CH)].rearrange("(k p) n -> p k n", p=P), it=it)
            modulation(M0, 0)
            for i, (o, w) in enumerate(EV_CH):
                n = E0 + i
                load(n, slotk[n % SLOTS][:, :, 0:w], view(a["even_w_in"][0], w, o))
            modulation(M1, 1)
            load(U0, slot[U0 % SLOTS][:, 0:3 * 768].rearrange("p (k n) -> p k n", k=3), view(a["even_w_uq"][0], 768))
            load(U0 + 1, slot[(U0 + 1) % SLOTS][:, 0:2 * 1024].rearrange("p (k n) -> p k n", k=2), view(a["even_w_ukv"][0], 1024))
            for i in range(2):
                n = O0 + i
                load(n, slotk[n % SLOTS], view(a["even_w_out"][0], CH, i * CH))

            def experts(base, l):
                gate = a["w_gate"][l].rearrange("e (k p) f -> e p k f", p=P)
                up = a["w_up"][l].rearrange("e (k p) f -> e p k f", p=P)
                down = a["w_down"][l].rearrange("e (j p) d -> e p j d", p=P)
                with sp.Fori(0, NE // 2) as it:
                    for u in range(2):
                        e = it * 2 + u
                        for j, w in enumerate((gate, up, down)):
                            n = base + 3 * u + j
                            s = slotk[n % SLOTS] if j < 2 else slot[n % SLOTS].rearrange("p (j n) -> p j n", j=4)
                            load(n, s, w[ds(e, 1)].rearrange("e p k f -> (e p) k f"), it=it)

            def overflow(l):
                sp.wait_ge(sem(f"flag_set{l}"), at(f"flag_set{l}", 1))
                over = sp.value_load(flag_i[l][0:1, :], min_val=0, max_val=1)
                with sp.If(over > 0):
                    mats = [(a["w_gate"][l], FF), (a["w_up"][l], FF), (a["w_down"][l], D)]
                    sp.wait_ge(sem(f"y_v{l}"), at(f"y_v{l}", NE))
                    with sp.Fori(0, ROUNDS[l]) as r:
                        with sp.Fori(0, NE) as e:
                            for j in range(3):
                                if j == 0:
                                    sp.wait_ge(sem(f"over_xT{l}"), at(f"over_xT{l}", r * NE + e + 1))
                                else:
                                    sp.wait_ge(sem(f"over_used{l}"), at(f"over_used{l}", (r * NE + e) * 3 + j))
                                sp.dma_start(over_w[j], mats[j][0][ds(e, 1)].rearrange(
                                    "a (k p) n -> p (a k) n", p=P)).then_inc(sem(f"over_loaded{l}"), 16)
                sp.nop()
            experts(X0, 0)
            overflow(0)
            for i, (o, w, _) in enumerate(OD_CH):
                n = E1 + i
                load(n, slotk[n % SLOTS][:, :, 0:w], view(a["odd_w_in"][0], w, o))
            for i in range(2):
                n = O1 + i
                load(n, slotk[n % SLOTS], view(a["odd_w_out"][0], CH, i * CH))
            experts(X1, 1)
            overflow(1)
            sp.wait_ge(sem("logits1"), at("logits1", 1))
            sp.dma_start(rh[:, 3072:4096], a["norm_final"].partition_broadcast(P)).then_inc(sem("nf_loaded"), 16)
            sp.wait_ge(sem("out_stored"), at("out_stored", 16 * LT))

        SMALL_LOADS, WIDE_LOADS = 8, 7

        def even_group(gi):
            units = []
            if gi == 0:
                for h in range(MH):
                    for t in range(NT):
                        k0 = 0 if t < LT else SEQ
                        units.append((qT[0:QD, h, t * P:(t + 1) * P], kT[0:QD, h, k0:NTOK], NTOK - k0,
                                      [z[:, j, h * MV:(h + 1) * MV] for j in range(k0 // P, NT)],
                                      bank[4 + t][:, h * MV:(h + 1) * MV]))
            else:
                for h in range(DH):
                    for c in range(2):
                        for i in range(LT):
                            t = i if gi == 1 else LT + i
                            k0 = 0 if gi == 1 else SEQ
                            b, r = (2 * h + c) // 4, 32 * ((2 * h + c) % 4)
                            units.append((dqT[r:r + 32, b, t * P:(t + 1) * P], dkT[r:r + 32, b, k0:NTOK], NTOK - k0,
                                          [z[:, j, ZV + h * DV:ZV + (h + 1) * DV] for j in range(k0 // P, NT)],
                                          bank[4 + 2 * c + i][:, h * DV:(h + 1) * DV]))
            return units

        def odd_units():
            units = []
            for h in range(8):
                for kind in range(2):
                    for t in range(LT):
                        r = 64 * (h % 2)
                        v0 = 640 if kind == 0 else 1408
                        units.append((goT[r:r + 64, 4 * kind + h // 2, t * P:(t + 1) * P],
                                      gkT[r:r + 64, 2 * kind + h // 4, :], NTOK,
                                      [zo[:, j, v0 + (h // 4) * HD:v0 + (h // 4 + 1) * HD] for j in range(NT)],
                                      bank[4 + 2 * kind + t][:, h * HD:(h + 1) * HD]))
            return units
        GROUPS = [[even_group(0), even_group(1), even_group(2)], [odd_units()]]
        GBASE = [[0, 32, 64], [0]]

        def bc_list(l):
            rs = range(2) if l == 0 else range(1)
            return [(0 + r, mod(l, 2, r)) for r in rs] + [(2 + r, scols[l][:, 8 * r + 16:8 * r + 24]) for r in rs] + \
                   [(4 + r, mod(l, 3, r)) for r in rs]

        def gate_list(l):
            return [(r, mod(l, 5, r)) for r in (range(2) if l == 0 else range(1))]

        @block.tensor
        def _(pe):
            mm = nc.tensor.matmul
            tr = nc.tensor.transpose
            pe.wait_ge(sem("small_loaded"), at("small_loaded", 16 * SMALL_LOADS))
            tr(bank[0][:, 0:53], rq[0:53, 0:P], ident[0:53, 0:53])
            tr(bank[1][:, 0:96], rq[0:96, P:2 * P], ident[0:96, 0:96]).then_inc(sem("vec_cols"), 1)

            def modulation(l, base):
                row, cols = f"mod_row{l}", f"mod_T{l}"

                def to_cols(it, j):
                    pe.wait_ge(sem(row), at(row, it * SLOTS + j + 1))
                    if j >= 2:
                        pe.wait_ge(sem(cols), at(cols, it * SLOTS + j - 1))
                    for i in range(4):
                        last = mm(bank[2 + j % 2][:, 2 * i:2 * i + 2], modrow[j % 2][:, i * P:(i + 1) * P],
                                  ident[0:2, 0:2], start=True, stop=True)
                    last.then_inc(sem(f"mod_cols{l}"), 1)
                with pe.Fori(0, MODC // SLOTS) as it:
                    for j in range(SLOTS):
                        arrived(pe, base + j, it)
                        if j >= 2:
                            pe.wait_ge(sem(row), at(row, it * SLOTS + j - 1))
                        for k in range(KD):
                            last = mm(bank[j % 2][0:2, :], silu.rearrange("p (r k) -> p k r", r=2)[:, k, :],
                                      slotk[(base + j) % SLOTS][:, k, :], start=k == 0, stop=k == KD - 1)
                        last.then_inc(chunks_used, 1)
                        if j > 0:
                            to_cols(it, j - 1)
                    to_cols(it, SLOTS - 1)
                    pe.wait_ge(sem(cols), at(cols, it * SLOTS + SLOTS))

            def norm_T(l):
                for kp in range(KD // 2):
                    for grp in range(2):
                        if kp == 0:
                            pe.wait_ge(sem(f"xn_ready{l}"), at(f"xn_ready{l}", 2 * (grp + 1)))
                        if kp >= 2:
                            pe.wait_ge(sem(f"hT{grp}_{l}"), at(f"hT{grp}_{l}", 2 * (kp - 1)))
                        for kk in range(2):
                            for i in range(2):
                                k, t = 2 * kp + kk, 2 * grp + i
                                last = tr(bank[4 + 2 * grp + kp % 2][:, kk * 256 + i * P:kk * 256 + (i + 1) * P],
                                          xn[:, t, k * P:(k + 1) * P], ident)
                        last.then_inc(sem(f"xT{grp}_{l}"), 1)

            def project(l, base, chunks):
                pe.wait_ge(sem(f"hT0_{l}"), at(f"hT0_{l}", KD))
                pe.wait_ge(sem(f"hT1_{l}"), at(f"hT1_{l}", KD))
                g = 0
                for i, (o, w, tiles) in enumerate(chunks):
                    n = base + i
                    arrived(pe, n)
                    for t in range(tiles):
                        if g >= 4:
                            pe.wait_ge(sem(f"z_{'va'[g % 2]}{l}"), at(f"z_{'va'[g % 2]}{l}", (g - 4) // 2 + 1))
                        for k in range(KD):
                            last = mm(bank[g % 4][:, 0:w], hT[:, k, t * P:(t + 1) * P], slotk[n % SLOTS][:, k, 0:w],
                                      start=k == 0, stop=k == KD - 1)
                        last.then_inc(chunks_used if t == tiles - 1 else sem(f"z_mm{l}"), 1)
                        g += 1

            def attend(l, gi):
                units, b = GROUPS[l][gi], GBASE[l][gi]
                if gi > 0:
                    pe.wait_ge(sem(f"o_read{l}"), at(f"o_read{l}", 4 * gi))

                def scores(u):
                    q, k, nk, _, _ = units[u]
                    if b + u >= 3:
                        pe.wait_ge(sem(f"p_ready{l}"), at(f"p_ready{l}", b + u - 2))
                    mm(bank[(b + u) % 3][:, 0:nk], q, k, start=True, stop=True).then_inc(sem(f"s_ready{l}"), 1)
                scores(0)
                scores(1)
                for u in range(len(units) + 1):
                    if u + 2 < len(units):
                        scores(u + 2)
                    if u >= 1:
                        _, _, nk, vs, out = units[u - 1]
                        pe.wait_ge(sem(f"pT_ready{l}"), at(f"pT_ready{l}", b + u))
                        for j, v in enumerate(vs):
                            last = mm(out, probsT[(b + u - 1) % 2][:, j * P:(j + 1) * P], v, start=j == 0, stop=j == len(vs) - 1)
                        last.then_inc(sem(f"pv_done{l}"), 1)
                    if u < len(units):
                        pe.wait_ge(sem(f"p_ready{l}"), at(f"p_ready{l}", b + u + 1))
                        for j in range(units[u][2] // P):
                            last = tr(bank[3][:, j * P:(j + 1) * P], probs[(b + u) % 4][:, j * P:(j + 1) * P], ident)
                        last.then_inc(sem(f"t_ready{l}"), 1)

            def block_T(name, blocks, ready):
                for s_, v_ in ready:
                    pe.wait_ge(sem(s_), at(s_, v_))
                for g, tiles in enumerate(blocks):
                    if g >= 4:
                        pe.wait_ge(sem(f"{name}_{'va'[g % 2]}"), at(f"{name}_{'va'[g % 2]}", (g - 4) // 2 + 1))
                    for i, src in enumerate(tiles):
                        last = tr(bank[g % 4][:, i * P:(i + 1) * P], src, ident)
                    last.then_inc(sem(f"{name}_tr"), 1)

            def broadcast(name, n, first):
                for i in range(n):
                    pe.wait_ge(sem(f"{name}_diag"), at(f"{name}_diag", i + 1))
                    if i >= 2:
                        pe.wait_ge(sem(f"{name}_v"), at(f"{name}_v", i - 1))
                        pe.wait_ge(sem(f"{name}_a"), at(f"{name}_a", i - 1))
                    for h in range(2):
                        last = mm(bank[4 + 2 * (i % 2) + h][:, :], ones, diag[i % 2][:, h * 512:(h + 1) * 512], start=True, stop=True)
                    last.then_inc(sem(f"{name}_mm"), 1)

            def out_project(l, base):
                pe.wait_ge(sem(f"oT{l}_v"), at(f"oT{l}_v", 4))
                pe.wait_ge(sem(f"oT{l}_a"), at(f"oT{l}_a", 4))
                g = 0
                for i in range(2):
                    n = base + i
                    arrived(pe, n)
                    for t in range(TL[l]):
                        if g >= 4:
                            pe.wait_ge(sem(f"out_v{l}"), at(f"out_v{l}", g - 3))
                        for k in range(KD):
                            last = mm(bank[g % 4][:, :], oT[:, k, t * P:(t + 1) * P], slotk[n % SLOTS][:, k, :],
                                      start=k == 0, stop=k == KD - 1)
                        last.then_inc(chunks_used if t == TL[l] - 1 else sem(f"out_mm{l}"), 1)
                        g += 1

            def experts(l, base):
                T = TL[l]
                for k in range(KD):
                    if k == 0:
                        pe.wait_ge(sem(f"h_ready{l}"), at(f"h_ready{l}", T))
                    if k >= 4:
                        pe.wait_ge(sem(f"h_{'va'[k % 2]}{l}"), at(f"h_{'va'[k % 2]}{l}", (k - 4) // 2 + 1))
                    for t in range(T):
                        last = tr(bank[4 + k % 4][:, t * P:(t + 1) * P], htok[:, t, k * P:(k + 1) * P], ident)
                    last.then_inc(sem(f"h_tr{l}"), 1)
                pe.wait_ge(sem(f"h_v{l}"), at(f"h_v{l}", 4))
                pe.wait_ge(sem(f"h_a{l}"), at(f"h_a{l}", 4))
                pe.wait_ge(sem("wide_loaded"), at("wide_loaded", 16 * WIDE_LOADS))
                for t in range(T):
                    for k in range(KD):
                        last = mm(bank[0][:, t * NE:(t + 1) * NE], hT[:, k, t * P:(t + 1) * P],
                                  wr_sb[:, k * NE:(k + 1) * NE], start=k == 0, stop=k == KD - 1)
                last.then_inc(sem(f"logits{l}"), 1)
                broadcast(f"gf{l}", len(gate_list(l)), True)
                pe.wait_ge(sem(f"mask{l}"), at(f"mask{l}", 1))
                m = r_mask.rearrange("p (t e) -> p t e", e=NE)
                for t in range(T):
                    mm(bank[1][:, t * NE:(t + 1) * NE], tri, m[:, t, :], start=True, stop=t == 0)
                    for b in range(t):
                        mm(bank[1][:, t * NE:(t + 1) * NE], ones, m[:, b, :], start=False, stop=b == t - 1)
                for t in range(T):
                    last = mm(bank[1][:, 64:64 + NE], ones, m[:, t, :], start=t == 0, stop=t == T - 1)
                last.then_inc(sem(f"counts{l}"), 1)

                def rows_T(buf, when, loaded):
                    pe.wait_ge(sem(loaded), at(loaded, when))
                    for k in range(KD):
                        last = tr(bank[k // 4][:, (k % 4) * P:(k % 4 + 1) * P], xg[buf][:, k * P:(k + 1) * P], ident)
                        if k == 3:
                            last.then_inc(sem(f"xT_lo{l}"), 1)
                    last.then_inc(sem(f"xT_hi{l}"), 1)

                def pair(it, last_pair):
                    for u in range(2):
                        e = it * 2 + u
                        n = base + 3 * u
                        pe.wait_ge(sem(f"xgT_v{l}"), at(f"xgT_v{l}", e + 1))
                        pe.wait_ge(sem(f"xgT_a{l}"), at(f"xgT_a{l}", e + 1))
                        pe.wait_ge(sem(f"act_ready{l}"), at(f"act_ready{l}", e))
                        for j in range(2):
                            arrived(pe, n + j, it)
                            for k in range(KD):
                                last = mm(bank[2 + j][:, :], xgT[u][:, k, :], slotk[(n + j) % SLOTS][:, k, :],
                                          start=k == 0, stop=k == KD - 1)
                            last.then_inc(chunks_used, 1)
                        if not (last_pair and u == 1):
                            rows_T(1 - u, it * 16 + 16 * (1 + u), f"xg_loaded{l}_{1 - u}")
                        pe.wait_ge(sem(f"act_ready{l}"), at(f"act_ready{l}", e + 1))
                        for j in range(4):
                            last = tr(bank[4][:, j * P:(j + 1) * P], act_[u][:, j * P:(j + 1) * P], ident)
                        last.then_inc(sem(f"act_tr{l}"), 1)
                        pe.wait_ge(sem(f"actT_ready{l}"), at(f"actT_ready{l}", e + 1))
                        pe.wait_ge(sem(f"y_v{l}"), at(f"y_v{l}", e))
                        pe.wait_ge(sem(f"y_a{l}"), at(f"y_a{l}", e))
                        arrived(pe, n + 2, it)
                        w = slot[(n + 2) % SLOTS].rearrange("p (j n) -> p j n", j=4)
                        for h in range(2):
                            for j in range(4):
                                last = mm(bank[5 + h][:, :], actT[u][:, j, :], w[:, j, h * 512:(h + 1) * 512],
                                          start=j == 0, stop=j == 3)
                            last.then_inc(sem(f"y_mm{l}") if h == 0 else chunks_used, 1)
                pe.wait_ge(sem(f"flag_set{l}"), at(f"flag_set{l}", 1))
                rows_T(0, 16, f"xg_loaded{l}_0")
                pair(0, False)
                with pe.Fori(1, NE // 2 - 1) as it:
                    pair(it, False)
                pair(NE // 2 - 1, True)

                pe.wait_ge(sem(f"flag_set{l}"), at(f"flag_set{l}", 1))
                over = pe.value_load(flag_i[l][0:1, :], min_val=0, max_val=1)
                with pe.If(over > 0):
                    pe.wait_ge(sem(f"y_v{l}"), at(f"y_v{l}", NE))
                    pe.wait_ge(sem(f"y_a{l}"), at(f"y_a{l}", NE))
                    with pe.Fori(0, ROUNDS[l] * NE) as i:
                        loaded, used = sem(f"over_loaded{l}"), sem(f"over_used{l}")
                        pe.wait_ge(sem(f"over_xg{l}"), at(f"over_xg{l}", i * 16 + 16))
                        for k in range(KD):
                            last = tr(bank[k // 4][:, (k % 4) * P:(k % 4 + 1) * P], xg[0][:, k * P:(k + 1) * P], ident)
                        last.then_inc(sem(f"over_xT{l}"), 1)
                        pe.wait_ge(sem(f"over_xgT{l}"), at(f"over_xgT{l}", i * 2 + 2))
                        for j in range(2):
                            pe.wait_ge(loaded, i * 48 + 16 * (j + 1))
                            for k in range(KD):
                                last = mm(bank[2 + j][:, :], xgT[0][:, k, :], over_w[j][:, k, :], start=k == 0, stop=k == KD - 1)
                            last.then_inc(used, 1)
                        pe.wait_ge(sem(f"over_act{l}"), at(f"over_act{l}", i + 1))
                        for j in range(4):
                            last = tr(bank[4][:, j * P:(j + 1) * P], act_[0][:, j * P:(j + 1) * P], ident)
                        last.then_inc(sem(f"over_act_tr{l}"), 1)
                        pe.wait_ge(sem(f"over_actT{l}"), at(f"over_actT{l}", i + 1))
                        pe.wait_ge(loaded, i * 48 + 48)
                        for h in range(2):
                            for j in range(4):
                                last = mm(bank[5 + h][:, :], actT[0][:, j, :], over_w[2][:, j, h * 512:(h + 1) * 512],
                                          start=j == 0, stop=j == 3)
                        last.then_inc(used, 1)
                pe.nop()

            pe.wait_ge(sem("silu_c"), at("silu_c", 1))
            modulation(0, M0)
            norm_T(0)
            project(0, E0, [(o, w, NT) for o, w in EV_CH])
            pe.wait_ge(sem("z_v0"), at("z_v0", 10))
            pe.wait_ge(sem("z_a0"), at("z_a0", 10))
            modulation(1, M1)

            pe.wait_ge(sem("cn_ready"), at("cn_ready", NT))
            for b in range(5):
                if b == 4:
                    pe.wait_ge(sem("ct_ready"), at("ct_ready", 1))
                for t in range(NT):
                    last = tr(bank[4 + b % 4][:, t * P:(t + 1) * P], z[:, t, b * P:(b + 1) * P], ident)
                last.then_inc(sem("ct_tr"), 1)
            pe.wait_ge(sem("ct_ready"), at("ct_ready", 5))
            pe.wait_ge(sem("krope_done"), at("krope_done", LT))
            for t in range(NT):
                last = mm(bank[5][64:96, t * P:(t + 1) * P], z[:, t, QL + KVL:QL + KVL + RD], ident, start=True, stop=True)
            last.then_inc(sem("kr_mm"), 1)
            uq = slot[U0 % SLOTS][:, 0:3 * 768].rearrange("p (k n) -> p k n", k=3)
            ukv = slot[(U0 + 1) % SLOTS][:, 0:2 * 1024].rearrange("p (k n) -> p k n", k=2)
            arrived(pe, U0)
            for g in range(20):
                if g >= 4:
                    pe.wait_ge(sem(f"lat_{'va'[g % 2]}"), at(f"lat_{'va'[g % 2]}", (g - 4) // 2 + 1))
                if g == MH:
                    arrived(pe, U0 + 1)
                if g < MH:
                    for k in range(3):
                        last = mm(bank[g % 4][0:QD, :], uq[:, k, g * QD:(g + 1) * QD], cT[:, k, :], start=k == 0, stop=k == 2)
                elif g < 2 * MH:
                    h = g - MH
                    for k in range(2):
                        last = mm(bank[g % 4][0:NOPE, :], ukv[:, k, h * P:h * P + NOPE], cT[:, 3 + k, :], start=k == 0, stop=k == 1)
                else:
                    t = g - 2 * MH
                    for k in range(2):
                        last = mm(bank[g % 4][:, :], cT[:, 3 + k, t * P:(t + 1) * P],
                                  ukv[:, k, :].rearrange("p (h c) -> p h c", h=MH)[:, :, NOPE:P], start=k == 0, stop=k == 1)
                last.then_inc(chunks_used if g in (MH - 1, 2 * MH + NT - 1) else sem("lat_mm"), 1)
            pe.wait_ge(sem("lat_v"), at("lat_v", 10))
            pe.wait_ge(sem("lat_a"), at("lat_a", 10))
            pe.wait_ge(sem("kT_rope"), at("kT_rope", 1))
            for i in range(4):
                if i >= 2:
                    pe.wait_ge(sem("qrot_read"), at("qrot_read", i - 1))
                mm(bank[6 + i % 2][64:96, :], const("rot")[64:96, :], qT[64:96, 2 * i:2 * i + 2, 0:SEQ],
                   start=True, stop=True).then_inc(sem("qrot_mm"), 1)
            pe.wait_ge(sem("qT_ready"), at("qT_ready", 4))
            pe.wait_ge(sem("kT_ready"), at("kT_ready", 1))
            attend(0, 0)
            block_T("dT", [[z[:, t, ZQ + b * P:ZQ + (b + 1) * P] for t in range(NT)] for b in range(4)] +
                    [[z[:, t, ZK + b * P:ZK + (b + 1) * P] for t in range(NT)] for b in range(4)], [("diff_rope", NT)])
            pe.wait_ge(sem("dT_v"), at("dT_v", 4))
            pe.wait_ge(sem("dT_a"), at("dT_a", 4))
            attend(0, 1)
            attend(0, 2)

            def o_src(l, t, k):
                if l == 1:
                    return zo[:, t, k * P:(k + 1) * P]
                return z[:, t, k * P:(k + 1) * P] if k < 4 else z[:, t, ZQ + (k - 4) * P:ZQ + (k - 3) * P]
            block_T("oT0", [[o_src(0, t, k) for t in range(NT)] for k in range(KD)], [("o_ready0", 8)])
            broadcast("bc0", len(bc_list(0)), True)
            out_project(0, O0)
            experts(0, X0)

            norm_T(1)
            project(1, E1, OD_CH)
            block_T("gT", [[zo[:, t, b * P:(b + 1) * P] for t in range(LT)] for b in range(4)] +
                    [[zo[:, t, 768 + b * P:768 + (b + 1) * P] for t in range(LT)] for b in range(4)],
                    [("odd_rope_w", 1), ("odd_rope_d", 1)])
            for g in range(4):
                pe.wait_ge(sem(f"gT_{'va'[g % 2]}"), at(f"gT_{'va'[g % 2]}", 3 + g // 2))
                o = (512 if g < 2 else 1280) + (g % 2) * HD
                for t in range(NT):
                    src = kdup[:, (g * NT + t) * P:(g * NT + t + 1) * P]
                    last = tr(bank[g % 4][:, t * P:(t + 1) * P], src, ident)
                last.then_inc(sem("gk_tr"), 1)
            pe.wait_ge(sem("gk_v"), at("gk_v", 2))
            pe.wait_ge(sem("gk_a"), at("gk_a", 2))
            pe.wait_ge(sem("gT_v"), at("gT_v", 4))
            pe.wait_ge(sem("gT_a"), at("gT_a", 4))
            attend(1, 0)
            block_T("oT1", [[o_src(1, t, k) for t in range(LT)] for k in range(KD)], [("o_ready1", 4)])
            broadcast("bc1", len(bc_list(1)), True)
            out_project(1, O1)
            experts(1, X1)

        @block.vector
        def _(ve):
            V = nc.vector
            done = [0]

            def link(ins):
                done[0] += 1
                ins.then_inc(sem("v_chain"), 1)
                ve.wait_ge(sem("v_chain"), at("v_chain", done[0]))

            sums_n, roots_n = [0], [0]

            def sums_done(ins):
                sums_n[0] += 1
                ins.then_inc(sem("sums_ready"), 1)
                ve.wait_ge(sem("sums_ready"), at("sums_ready", sums_n[0]))

            def rms(out, n, o=0):
                roots_n[0] += 1
                ve.wait_ge(sem("root_ready"), at("root_ready", roots_n[0]))
                link(V.reciprocal(out, roots[:, o:o + n]))

            ve.wait_ge(sem("vec_cols"), at("vec_cols", 1))
            V.tensor_copy(colv[:, 0:53], bank[0][:, 0:53]).then_inc(sem("vec_sb"), 1)
            V.tensor_copy(bmodT, bank[1][:, 0:96]).then_inc(sem("vec_sb"), 1)
            ve.wait_ge(sem("vec_sb"), at("vec_sb", 2))
            link(V.tensor_copy(tokid_i, const("tokid")))
            ve.wait_ge(sem("wide_loaded"), at("wide_loaded", 16 * WIDE_LOADS))
            lq = lam_b.rearrange("p (a b c) -> p a b c", a=2, b=2)
            link(V.tensor_tensor(lq[:, :, 0, :], lq[:, :, 0, :], lq[:, :, 1, :], ALU.mult))
            V.tensor_reduce(lamv[:, 0:2], lq[:, :, 0, :], AX, ALU.add).then_inc(sem("lam_sums"), 1)
            link(V.tensor_scalar(subln_b, subln_b, 1.0 - LAM_INIT, None, ALU.mult))

            def modulation(l):
                row = sem(f"mod_row{l}")
                mT = modT.rearrange("p (l b r) -> p l b r", l=2, r=2)[:, l]
                base = M0 if l == 0 else M1
                with ve.Fori(0, MODC // SLOTS) as it:
                    def to_T(j):
                        ve.wait_ge(sem(f"mod_cols{l}"), at(f"mod_cols{l}", it * SLOTS + j + 1))
                        c = it * (SLOTS * 4) + 4 * j
                        V.tensor_tensor(mT[:, ds(c, 4), :], bank[2 + j % 2][:, 0:8].rearrange("p (b r) -> p b r", r=2),
                                        bmodT.rearrange("p (l b) -> p l b", l=2)[:, l, ds(c, 4)].unsqueeze(2).to_broadcast([P, 4, 2]),
                                        ALU.add).then_inc(sem(f"mod_T{l}"), 1)
                    for j in range(SLOTS):
                        ve.wait_ge(chunks_used, it * SLOTS + base + j + 1)
                        V.tensor_copy(modrow[j % 2], bank[j % 2][0:2, :]).then_inc(row, 1)
                        if j > 0:
                            to_T(j - 1)
                    to_T(SLOTS - 1)
                ve.wait_ge(sem(f"mod_T{l}"), at(f"mod_T{l}", MODC))
                for r in range(2):
                    V.scalar_tensor_tensor(scols[l][:, 8 * r:8 * r + 8], mod(l, 1, r), 1.0,
                                           colv[:, C_NM + 8 * l:C_NM + 8 * l + 8], ALU.add, ALU.mult).then_inc(sem(f"scol{l}"), 1)
                    V.scalar_tensor_tensor(scols[l][:, 16 + 8 * r:24 + 8 * r], mod(l, 4, r), 1.0,
                                           colv[:, C_NF + 8 * l:C_NF + 8 * l + 8], ALU.add, ALU.mult).then_inc(sem(f"scol{l}"), 1)
                ve.wait_ge(sem(f"scol{l}"), at(f"scol{l}", 4))

            def norm(l):
                rms(rstd[:, 0:NT], NT)
                for t in range(NT):
                    V.tensor_scalar(xn[:, t, :], xt[:, t, :], rstd[:, t:t + 1], None, ALU.mult).then_inc(sem(f"xn_ready{l}"), 1)
                for k in range(KD):
                    ve.wait_ge(sem(f"xT0_{l}"), at(f"xT0_{l}", k // 2 + 1))
                    V.tensor_scalar(hT[:, k, 0:SEQ], bank[4 + (k // 2) % 2][:, (k % 2) * 256:(k % 2 + 1) * 256],
                                    scols[l][:, k:k + 1], mod(l, 0, 0)[:, k:k + 1], ALU.mult, ALU.add).then_inc(sem(f"hT0_{l}"), 1)

            def projected(l, chunks, zz):
                g = 0
                for i, (o, w, tiles) in enumerate(chunks):
                    for t in range(tiles):
                        if g % 2 == 0:
                            product_done(ve, f"z_mm{l}", E0 if l == 0 else E1, [c[2] for c in chunks], i, t)
                            V.tensor_copy(zz[:, t, o:o + w], bank[g % 4][:, 0:w]).then_inc(sem(f"z_v{l}"), 1)
                        g += 1

            def rope(src, cos, sin, heads, d, t1, t2):
                q = d // 4
                s4 = src.rearrange("p (h x a q) -> p h x a q", h=heads, x=2, a=2)
                t4 = t1.rearrange("p (h x a q) -> p h x a q", h=heads, x=2, a=2)
                n4 = sin.rearrange("p (x a q) -> p x a q", x=2, a=2)
                for i in range(2):
                    V.tensor_tensor(t4[:, :, :, i, :], s4[:, :, :, 1 - i, :],
                                    n4[:, :, i, :].unsqueeze(1).to_broadcast([P, heads, 2, q]), ALU.mult)\
                     .then_inc(sem("v_rope"), 1)
                    rope_n[0] += 1
                ve.wait_ge(sem("v_rope"), at("v_rope", rope_n[0]))
                s2 = src.rearrange("p (h d) -> p h d", h=heads)
                link(V.tensor_tensor(s2, s2, cos.unsqueeze(1).to_broadcast([P, heads, d]), ALU.mult))
                return V.tensor_tensor(src, src, t1, ALU.add)
            rope_n = [0]

            def attend(l, gi):
                units, b = GROUPS[l][gi], GBASE[l][gi]

                def maxima(u):
                    nk = units[u][2]
                    ve.wait_ge(sem(f"s_ready{l}"), at(f"s_ready{l}", b + u + 1))
                    s = bank[(b + u) % 3]
                    m = nmx[:, (b + u) % 64:(b + u) % 64 + 1]
                    if l == 1 and (u // 2) % 2 == 0:
                        t = u % 2
                        far = s[:, P:2 * P] if t == 0 else s[:, 0:P]
                        link(V.tensor_tensor(far, far, const("wmask")[:, t * P:(t + 1) * P], ALU.add))
                        link(V.tensor_reduce(m, s[:, 0:nk], AX, ALU.max, negate=True))
                        V.tensor_tensor(m, m, nsink[:, u // 4:u // 4 + 1], ALU.min).then_inc(sem(f"max_ready{l}"), 1)
                    else:
                        V.tensor_reduce(m, s[:, 0:nk], AX, ALU.max, negate=True).then_inc(sem(f"max_ready{l}"), 1)
                maxima(0)
                maxima(1)
                for u in range(len(units)):
                    if u + 2 < len(units):
                        maxima(u + 2)
                    ve.wait_ge(sem(f"t_ready{l}"), at(f"t_ready{l}", b + u + 1))
                    if b + u >= 2:
                        ve.wait_ge(sem(f"pv_done{l}"), at(f"pv_done{l}", b + u - 1))
                    nk = units[u][2]
                    V.tensor_copy(probsT[(b + u) % 2][:, 0:nk], bank[3][:, 0:nk]).then_inc(sem(f"pT_ready{l}"), 1)
                ve.wait_ge(sem(f"pv_done{l}"), at(f"pv_done{l}", b + len(units)))
                ve.wait_ge(sem(f"p_ready{l}"), at(f"p_ready{l}", b + len(units)))

            def heads(ap):
                return ap.rearrange("p (h d) -> p h d", h=8)

            def per_head(v):
                return v.unsqueeze(2).to_broadcast([P, 8, 64])

            def transposed(name, blocks, dst, n):
                for g in range(0, blocks, 2):
                    ve.wait_ge(sem(f"{name}_tr"), at(f"{name}_tr", g + 1))
                    V.tensor_copy(dst(g), bank[g % 4][:, 0:n]).then_inc(sem(f"{name}_v"), 1)

            def broadcast(name, cols):
                def diagonal(i):
                    if i >= 2:
                        ve.wait_ge(sem(f"{name}_mm"), at(f"{name}_mm", i - 1))
                    V.tensor_tensor(diag[i % 2].rearrange("p (k n) -> p k n", k=KD), ident.unsqueeze(1).to_broadcast([P, KD, P]),
                                    cols[i][1].unsqueeze(2).to_broadcast([P, KD, P]), ALU.mult).then_inc(sem(f"{name}_diag"), 1)
                diagonal(0)
                for i in range(len(cols)):
                    if i + 1 < len(cols):
                        diagonal(i + 1)
                    ve.wait_ge(sem(f"{name}_mm"), at(f"{name}_mm", i + 1))
                    V.tensor_copy(bc[cols[i][0]][:, 0:512], bank[4 + 2 * (i % 2)][:, :]).then_inc(sem(f"{name}_v"), 1)
                ve.wait_ge(sem(f"{name}_v"), at(f"{name}_v", len(cols)))
                ve.wait_ge(sem(f"{name}_a"), at(f"{name}_a", len(cols)))

            def out_project(l):
                g = 0
                T = TL[l]
                for i in range(2):
                    for t in range(T):
                        product_done(ve, f"out_mm{l}", O0 if l == 0 else O1, [T, T], i, t)
                        if g >= 4:
                            ve.wait_ge(sem(f"x_add{l}"), at(f"x_add{l}", g - 3))
                        V.tensor_tensor(rk[:, (g % 4) * 512:(g % 4 + 1) * 512], bank[g % 4][:, :],
                                        bc[t // LT][:, i * 512:(i + 1) * 512], ALU.mult).then_inc(sem(f"out_v{l}"), 1)
                        g += 1

            def experts(l):
                T = TL[l]
                rms(rstd[:, 0:T], T)
                for t in range(T):
                    V.scalar_tensor_tensor(htok[:, t, :], xt[:, t, :], rstd[:, t:t + 1], bc[2 + t // LT], ALU.mult, ALU.mult)\
                     .then_inc(sem(f"h_scaled{l}"), 1)
                for k in range(0, KD, 2):
                    ve.wait_ge(sem(f"h_tr{l}"), at(f"h_tr{l}", k + 1))
                    V.tensor_copy(hT[:, k, 0:T * P], bank[4 + k % 4][:, 0:T * P]).then_inc(sem(f"h_v{l}"), 1)
                ve.wait_ge(sem(f"logits{l}"), at(f"logits{l}", 1))
                broadcast(f"gf{l}", gate_list(l))

                W = T * NE
                G = T * NG
                s, sel, top, mask, w = r_s[:, 0:W], r_sel[:, 0:W], r_top[:, 0:W], r_mask[:, 0:W], r_w[:, 0:W]
                te = lambda v: v.rearrange("p (t e) -> p t e", e=NE)
                ge = lambda v: v.rearrange("p (g e) -> p g e", e=EG)
                ve.wait_ge(sem(f"sig{l}"), at(f"sig{l}", 1))
                link(V.tensor_tensor(te(sel), te(s), br_sb.unsqueeze(1).to_broadcast([P, T, NE]), ALU.add))

                def outranked(v, groups, n):
                    vv = v.rearrange("p (g e) -> p g e", e=n)
                    by, of = vv.unsqueeze(2).to_broadcast([P, groups, n, n]), vv.unsqueeze(3).to_broadcast([P, groups, n, n])
                    beat = r_beat[:, 0:groups * n * n].rearrange("p (g i j) -> p g i j", i=n, j=n)
                    eq = r_eq[:, 0:groups * n * n].rearrange("p (g i j) -> p g i j", i=n, j=n)
                    V.tensor_tensor(beat, by, of, ALU.is_gt)
                    link(V.tensor_tensor(eq, by, of, ALU.is_equal))
                    eqf = r_eq[:, 0:groups * n * n].rearrange("p (g m) -> p g m", m=n * n)
                    link(V.tensor_tensor(eqf, eqf, const("lower").unsqueeze(1).to_broadcast([P, groups, n * n]), ALU.mult))
                    link(V.tensor_tensor(r_beat[:, 0:groups * n * n], r_beat[:, 0:groups * n * n], r_eq[:, 0:groups * n * n], ALU.add))
                    return beat
                beat = outranked(sel, G, EG)
                link(V.tensor_reduce(top, beat, AX, ALU.add))
                link(V.tensor_scalar(top, top, 1.5, None, ALU.is_lt))
                link(V.tensor_tensor(r_t[:, 0:W], sel, top, ALU.mult))
                link(V.tensor_reduce(r_gs[:, 0:G], ge(r_t[:, 0:W]), AX, ALU.add))
                beat = outranked(r_gs[:, 0:G], T, NG)
                link(V.tensor_reduce(r_gb[:, 0:G], beat, AX, ALU.add))
                link(V.tensor_scalar(r_gb[:, 0:G], r_gb[:, 0:G], 0.5, None, ALU.is_lt))
                V.tensor_tensor(ge(mask), ge(top), r_gb[:, 0:G].unsqueeze(2).to_broadcast([P, G, EG]), ALU.mult)\
                 .then_inc(sem(f"mask{l}"), 1)
                ve.wait_ge(sem(f"mask{l}"), at(f"mask{l}", 1))
                link(V.tensor_tensor(w, s, mask, ALU.mult))
                link(V.tensor_reduce(r_sum[:, 0:T], te(w), AX, ALU.add))
                link(V.reciprocal(r_sum[:, 0:T], r_sum[:, 0:T]))
                link(V.tensor_tensor(te(w), te(w), r_sum[:, 0:T].unsqueeze(2).to_broadcast([P, T, NE]), ALU.mult))
                ve.wait_ge(sem(f"counts{l}"), at(f"counts{l}", 1))
                val = r_val[:, 0:W]
                link(V.tensor_scalar(r_pos[:, 0:W], bank[1][:, 0:W], float(NE), None, ALU.mult))
                link(V.tensor_tensor(te(val), te(r_pos[:, 0:W]), const("eidx").unsqueeze(1).to_broadcast([P, T, NE]), ALU.add))
                link(V.tensor_scalar(r_t[:, 0:W], val, 1.0, None, ALU.add))
                link(V.tensor_tensor(r_t[:, 0:W], r_t[:, 0:W], mask, ALU.mult))
                link(V.tensor_reduce(r_hi[:, 0:T], te(r_t[:, 0:W]), AX, ALU.max))
                link(V.tensor_scalar(r_hi[:, 0:T], r_hi[:, 0:T], -1.0, None, ALU.add))
                link(V.tensor_scalar(r_t[:, 0:W], val, -1.0, float(ROWS), ALU.mult, ALU.add))
                link(V.tensor_tensor(r_t[:, 0:W], r_t[:, 0:W], mask, ALU.mult))
                link(V.tensor_reduce(r_lo[:, 0:T], te(r_t[:, 0:W]), AX, ALU.max))
                link(V.tensor_scalar(r_lo[:, 0:T], r_lo[:, 0:T], -1.0, float(ROWS), ALU.mult, ALU.add))
                V.tensor_copy(idx_hi[:, 0:T], r_hi[:, 0:T]).then_inc(sem(f"idx{l}"), 1)
                V.tensor_copy(idx_lo[:, 0:T], r_lo[:, 0:T]).then_inc(sem(f"idx{l}"), 1)
                link(V.tensor_reduce(r_cnt[:, 0:1], bank[1][:, 64:64 + NE], AX, ALU.max))
                V.tensor_scalar(flag_i[l], r_cnt[:, 0:1], cap + 0.5, None, ALU.is_gt).then_inc(sem(f"flag_set{l}"), 1)
                for sel_idx, wsel in ((r_hi, r_whi), (r_lo, r_wlo)):
                    link(V.tensor_tensor(te(r_t[:, 0:W]), te(val), sel_idx[:, 0:T].unsqueeze(2).to_broadcast([P, T, NE]), ALU.is_equal))
                    link(V.tensor_tensor(r_t[:, 0:W], r_t[:, 0:W], w, ALU.mult))
                    link(V.tensor_reduce(wsel[:, 0:T], te(r_t[:, 0:W]), AX, ALU.add))

                def rows_T(buf, when):
                    ve.wait_ge(sem(f"xT_lo{l}"), at(f"xT_lo{l}", when))
                    V.tensor_copy(xgT[buf][:, 0:4, :], bank[0][:, :].rearrange("p (k n) -> p k n", k=4)).then_inc(sem(f"xgT_v{l}"), 1)

                def pair(it, last_pair):
                    for u in range(2):
                        e = it * 2 + u
                        ve.wait_ge(sem(f"silu_ready{l}"), at(f"silu_ready{l}", e + 1))
                        V.tensor_tensor(act_[u], sg[u], bank[3][:, :], ALU.mult).then_inc(sem(f"act_ready{l}"), 1)
                        if not (last_pair and u == 1):
                            rows_T(1 - u, e + 2)
                        ve.wait_ge(sem(f"y_mm{l}"), at(f"y_mm{l}", e + 1))
                        ve.wait_ge(sem(f"y_stored{l}_{u}"), at(f"y_stored{l}_{u}", it * 16))
                        V.tensor_copy(ybuf[u][:, 0:512], bank[5][:, :]).then_inc(sem(f"y_v{l}"), 1)
                ve.wait_ge(sem(f"h_stored{l}"), at(f"h_stored{l}", 16 * T))
                rows_T(0, 1)
                pair(0, False)
                with ve.Fori(1, NE // 2 - 1) as it:
                    pair(it, False)
                pair(NE // 2 - 1, True)

                over = ve.value_load(flag_i[l][0:1, :], min_val=0, max_val=1)
                with ve.If(over > 0):
                    ve.wait_ge(sem(f"y_stored{l}_0"), at(f"y_stored{l}_0", 8 * NE))
                    with ve.Fori(0, ROUNDS[l] * NE) as i:
                        ve.wait_ge(sem(f"over_xT{l}"), at(f"over_xT{l}", i + 1))
                        for h in range(2):
                            V.tensor_copy(xgT[0][:, 4 * h:4 * h + 4, :], bank[h][:, :].rearrange("p (k n) -> p k n", k=4))\
                             .then_inc(sem(f"over_xgT{l}"), 1)
                        ve.wait_ge(sem(f"over_silu{l}"), at(f"over_silu{l}", i + 1))
                        V.tensor_tensor(act_[0], sg[0], bank[3][:, :], ALU.mult).then_inc(sem(f"over_act{l}"), 1)
                        ve.wait_ge(sem(f"over_used{l}"), at(f"over_used{l}", i * 3 + 3))
                        for h in range(2):
                            V.tensor_copy(ybuf[0][:, 512 * h:512 * h + 512], bank[5 + h][:, :]).then_inc(sem(f"over_y{l}"), 1)
                ve.nop()

                for t in range(T):
                    b = t % 2
                    ve.wait_ge(sem(f"ya_loaded{l}_{b}"), at(f"ya_loaded{l}_{b}", 16 * (t // 2 + 1)))
                    ve.wait_ge(sem(f"yb_loaded{l}_{b}"), at(f"yb_loaded{l}_{b}", 16 * (t // 2 + 1)))
                    link(V.tensor_scalar(ya[b], ya[b], r_whi[:, t:t + 1], None, ALU.mult))
                    link(V.scalar_tensor_tensor(ya[b], yb[b], r_wlo[:, t:t + 1], ya[b], ALU.mult, ALU.add))
                    link(V.tensor_tensor(ya[b], ya[b], bc[t // LT], ALU.mult))
                    V.tensor_tensor(xt[:, t, :], xt[:, t, :], ya[b], ALU.add).then_inc(sem(f"x_moe{l}"), 1)

            modulation(0)
            norm(0)
            projected(0, [(o, w, NT) for o, w in EV_CH], z)
            modulation(1)

            rms(rstd[:, 0:4], 4)
            rms(rstd[:, 4:8], 4, 4)
            for t in range(NT):
                V.tensor_scalar(z[:, t, 0:QL], z[:, t, 0:QL], rstd[:, t:t + 1], None, ALU.mult)
                V.tensor_scalar(z[:, t, QL:QL + KVL], z[:, t, QL:QL + KVL], rstd[:, 4 + t:5 + t], None, ALU.mult)\
                 .then_inc(sem("cn_ready"), 1)
            for t in range(LT):
                rope(z[:, t, QL + KVL:QL + KVL + RD], const("cos32")[:, t * RD:(t + 1) * RD], const("sin32")[:, t * RD:(t + 1) * RD],
                     1, RD, rh[:, 3584 + 32 * t:3616 + 32 * t], None).then_inc(sem("krope_done"), 1)
            ve.wait_ge(sem("kr_mm"), at("kr_mm", 1))
            V.tensor_copy(kT[64:96, 0, :], bank[5][64:96, :]).then_inc(sem("kT_rope"), 1)
            for g in range(0, 20, 2):
                latent_done(ve, g)
                if g < MH:
                    V.tensor_scalar(qT[0:QD, g, :], bank[g % 4][0:QD, :], MLA_SCALE, None, ALU.mult).then_inc(sem("lat_v"), 1)
                elif g < 2 * MH:
                    V.tensor_copy(kT[0:NOPE, g - MH, :], bank[g % 4][0:NOPE, :]).then_inc(sem("lat_v"), 1)
                else:
                    V.tensor_copy(z[:, g - 2 * MH, 0:MH * MV], bank[g % 4][:, :]).then_inc(sem("lat_v"), 1)
            ve.wait_ge(sem("lat_v"), at("lat_v", 10))
            ve.wait_ge(sem("lat_a"), at("lat_a", 10))
            ve.wait_ge(sem("krope_done"), at("krope_done", LT))
            for i in range(4):
                ve.wait_ge(sem("qrot_mm"), at("qrot_mm", i + 1))
                t1 = rh[64:96, 3584:4096].rearrange("p (h n) -> p h n", h=2)
                if i:
                    ve.wait_ge(sem("qT_ready"), at("qT_ready", i))
                V.tensor_tensor(t1, bank[6 + i % 2][64:96, :].rearrange("p (h n) -> p h n", h=2),
                                const("sinT")[64:96, :].unsqueeze(1).to_broadcast([32, 2, SEQ]), ALU.mult).then_inc(sem("qrot_read"), 1)
                ve.wait_ge(sem("qrot_read"), at("qrot_read", i + 1))
                qr = qT[64:96, 2 * i:2 * i + 2, 0:SEQ]
                link(V.tensor_tensor(qr, qr, const("cosT")[64:96, :].unsqueeze(1).to_broadcast([32, 2, SEQ]), ALU.mult))
                V.tensor_tensor(qr, qr, t1, ALU.add).then_inc(sem("qT_ready"), 1)
            ve.wait_ge(sem("lam_exp"), at("lam_exp", 1))
            link(V.tensor_scalar(lamv[:, 3:4], lamv[:, 1:2], -1.0, LAM_INIT, ALU.mult, ALU.add))
            link(V.tensor_tensor(lamv[:, 2:3], lamv[:, 0:1], lamv[:, 3:4], ALU.add))

            attend(0, 0)
            link(V.reciprocal(rinv[:, 0:32], rsum[:, 0:32]))
            rv = rinv[:, 0:32].rearrange("p (h t) -> p t h", t=NT)
            for t in range(NT):
                V.tensor_tensor(heads(z[:, t, 0:512]), heads(bank[4 + t][:, :]), per_head(rv[:, t, :]), ALU.mult)\
                 .then_inc(sem("o_mla"), 1)
            ve.wait_ge(sem("o_mla"), at("o_mla", NT))
            V.tensor_copy(rstd[:, 0:1], rstd[:, 1:2]).then_inc(sem("o_read0"), 4)
            transposed("dT", 8, lambda g: (dqT if g < 4 else dkT)[:, g % 4, :], NTOK)
            for gi in (1, 2):
                attend(0, gi)
                c0 = (gi % 2) * 32
                link(V.reciprocal(rinv[:, c0:c0 + 32], rsum[:, c0:c0 + 32]))
                rv = rinv[:, c0:c0 + 32].rearrange("p (h c i) -> p c i h", c=2, i=2)
                for i in range(2):
                    t = i if gi == 1 else LT + i
                    link(V.tensor_scalar(rv[:, 1, i, :], rv[:, 1, i, :], lamv[:, 2:3], None, ALU.mult))
                    V.tensor_tensor(heads(tmp[0]), heads(bank[4 + i][:, :]), per_head(rv[:, 0, i, :]), ALU.mult)
                    link(V.tensor_tensor(heads(tmp[1]), heads(bank[6 + i][:, :]), per_head(rv[:, 1, i, :]), ALU.mult))
                    ob = z[:, t, ZQ:ZQ + 512]
                    V.tensor_tensor(ob, tmp[0], tmp[1], ALU.subtract).then_inc(sem("o_read0"), 2)
                    ve.wait_ge(sem("o_read0"), at("o_read0", 4 * gi + 2 * (i + 1)))
                    link(V.tensor_tensor(tmp[0], ob, ob, ALU.mult))
                    sums_done(V.tensor_reduce(stat[:, 0:8], heads(tmp[0]), AX, ALU.add))
                    rms(rstd[:, 0:8], 8)
                    link(V.tensor_tensor(heads(ob), heads(ob), per_head(rstd[:, 0:8]), ALU.mult))
                    V.tensor_tensor(heads(ob), heads(ob), subln_b.unsqueeze(1).to_broadcast([P, 8, DV]), ALU.mult)\
                     .then_inc(sem("o_ready0"), 2)
            transposed("oT0", KD, lambda g: oT[:, g, :], NTOK)
            broadcast("bc0", bc_list(0))
            out_project(0)
            experts(0)

            norm(1)
            projected(1, OD_CH, zo)
            ve.wait_ge(sem("z_v1"), at("z_v1", 6))
            ve.wait_ge(sem("z_a1"), at("z_a1", 6))
            t1, t2 = rq[:, 2048:2048 + 640], rq[:, 2688:2688 + 640]
            for t in range(NT):
                h0, nh = (0, 10) if t < LT else (8, 2)
                src = zo[:, t, 768 + 64 * h0:768 + 640]
                n = 64 * nh
                sv = src.rearrange("p (h d) -> p h d", h=nh)
                link(V.tensor_tensor(t1[:, 0:n], src, src, ALU.mult))
                sums_done(V.tensor_reduce(nrm[:, 0:nh], t1[:, 0:n].rearrange("p (h d) -> p h d", h=nh), AX, ALU.add))
                rms(nrm[:, 0:nh], nh)
                link(V.tensor_tensor(sv, sv, nrm[:, 0:nh].unsqueeze(2).to_broadcast([P, nh, HD]), ALU.mult))
                if t < LT:
                    qv = src[:, 0:512].rearrange("p (h d) -> p h d", h=8)
                    link(V.tensor_tensor(qv, qv, qk_b[:, 0:64].unsqueeze(1).to_broadcast([P, 8, HD]), ALU.mult))
                kv = zo[:, t, 1280:1408].rearrange("p (h d) -> p h d", h=2)
                link(V.tensor_tensor(kv, kv, qk_b[:, 64:128].unsqueeze(1).to_broadcast([P, 2, HD]), ALU.mult))
                if t < LT:
                    link(rope(src, const("cos64")[:, t * 64:(t + 1) * 64], const("sin64")[:, t * 64:(t + 1) * 64], 10, 64, t1, t2))
            V.tensor_scalar(nsink, sink_b, -1.0, None, ALU.mult).then_inc(sem("odd_rope_d"), 1)
            ve.wait_ge(sem("odd_rope_d"), at("odd_rope_d", 1))
            for g in range(0, 8, 2):
                ve.wait_ge(sem("gT_tr"), at("gT_tr", g + 1))
                V.tensor_scalar(goT[:, g, :], bank[g % 4][:, 0:SEQ], ATT_SCALE, None, ALU.mult).then_inc(sem("gT_v"), 1)
            for g in (0, 2):
                ve.wait_ge(sem("gk_tr"), at("gk_tr", g + 1))
                V.tensor_copy(gkT[:, g, :], bank[g][:, :]).then_inc(sem("gk_v"), 1)
            attend(1, 0)
            nw = nmx[:, 0:32].rearrange("p (h c) -> p h c", c=4)[:, :, 0:2]
            sk = nsk.rearrange("p (h c) -> p h c", c=2)
            V.tensor_tensor(sk, nw, sink_b.unsqueeze(2).to_broadcast([P, 8, 2]), ALU.add).then_inc(sem("sink_arg"), 1)
            ve.wait_ge(sem("sink_exp"), at("sink_exp", 1))
            rw = rsum[:, 0:32].rearrange("p (h c) -> p h c", c=4)[:, :, 0:2]
            link(V.tensor_tensor(rw, rw, sk, ALU.add))
            link(V.reciprocal(rinv[:, 0:32], rsum[:, 0:32]))
            rv = rinv[:, 0:32].rearrange("p (h c t) -> p c t h", c=2, t=2)
            for c in range(2):
                for t in range(2):
                    V.tensor_tensor(heads(zo[:, t, 512 * c:512 * c + 512]), heads(bank[4 + 2 * c + t][:, :]), per_head(rv[:, c, t, :]),
                                    ALU.mult).then_inc(sem("o_ready1"), 1)
            transposed("oT1", KD, lambda g: oT[:, g, 0:SEQ], SEQ)
            broadcast("bc1", bc_list(1))
            out_project(1)
            experts(1)

            rms(rstd[:, 0:LT], LT)
            ve.wait_ge(sem("nf_loaded"), at("nf_loaded", 16))
            for t in range(LT):
                V.scalar_tensor_tensor(ya[t], xt[:, t, :], rstd[:, t:t + 1], rh[:, 3072:4096], ALU.mult, ALU.mult)\
                 .then_inc(sem("out_ready"), 1)

        @block.scalar
        def _(ac):
            A = nc.scalar.activation
            ac.wait_ge(sem("zero_list"), at("zero_list", 1))
            for l in range(DEPTH):
                ac.dma_start(list_dram[l].rearrange("(p n) o -> p (n o)", p=P), zeros_i).then_inc(sem("list_zeroed"), 16)
            ac.wait_ge(sem("vec_sb"), at("vec_sb", 2))
            A(silu, colv[:, 0:16], ACT.Silu).then_inc(sem("silu_c"), 1)
            ac.wait_ge(sem("lam_sums"), at("lam_sums", 1))
            A(lamv[:, 0:2], lamv[:, 0:2], ACT.Exp).then_inc(sem("lam_exp"), 1)

            def sumsq(tiles, name, junk, waits):
                for t in range(tiles):
                    s_, v_ = waits(t)
                    ac.wait_ge(sem(s_), at(s_, v_))
                    if t:
                        ac.wait_ge(sem(name), at(name, t))
                    A(junk, xt[:, t, :], ACT.Square, accum_out=stat[:, t:t + 1]).then_inc(sem(name), 1)

            def root(sums, n, of):
                A(roots[:, 0:n], sums, ACT.Sqrt, scale=1.0 / of, bias=const("eps")).then_inc(sem("root_ready"), 1)

            sums_n = [0]

            def root_of_sums(sums, n, of):
                sums_n[0] += 1
                ac.wait_ge(sem("sums_ready"), at("sums_ready", sums_n[0]))
                root(sums, n, of)

            def norm(l):
                ac.wait_ge(sem(f"sumsq{l}"), at(f"sumsq{l}", NT))
                root(stat[:, 0:NT], NT, D)
                for k in range(KD):
                    ac.wait_ge(sem(f"xT1_{l}"), at(f"xT1_{l}", k // 2 + 1))
                    ac.wait_ge(sem(f"scol{l}"), at(f"scol{l}", 4))
                    A(hT[:, k, SEQ:NTOK], bank[6 + (k // 2) % 2][:, (k % 2) * 256:(k % 2 + 1) * 256], ACT.Identity,
                      scale=scols[l][:, 8 + k:9 + k], bias=mod(l, 0, 1)[:, k:k + 1]).then_inc(sem(f"hT1_{l}"), 1)

            def projected(l, chunks, zz):
                g = 0
                for i, (o, w, tiles) in enumerate(chunks):
                    for t in range(tiles):
                        if g % 2 == 1:
                            product_done(ac, f"z_mm{l}", E0 if l == 0 else E1, [c[2] for c in chunks], i, t)
                            A(zz[:, t, o:o + w], bank[g % 4][:, 0:w], ACT.Copy).then_inc(sem(f"z_a{l}"), 1)
                        g += 1

            def attend(l, gi):
                units, b = GROUPS[l][gi], GBASE[l][gi]
                for u in range(len(units)):
                    n = b + u
                    ac.wait_ge(sem(f"max_ready{l}"), at(f"max_ready{l}", n + 1))
                    if n >= 4:
                        ac.wait_ge(sem(f"t_ready{l}"), at(f"t_ready{l}", n - 3))
                    nk = units[u][2]
                    c = (gi % 2) * 32 + u
                    A(probs[n % 4][:, 0:nk], bank[n % 3][:, 0:nk], ACT.Exp, bias=nmx[:, n % 64:n % 64 + 1],
                      accum_out=rsum[:, c:c + 1]).then_inc(sem(f"p_ready{l}"), 1)

            def transposed(name, blocks, dst, n, scale=1.0):
                for g in range(1, blocks, 2):
                    ac.wait_ge(sem(f"{name}_tr"), at(f"{name}_tr", g + 1))
                    A(dst(g), bank[g % 4][:, 0:n], ACT.Copy, scale=scale).then_inc(sem(f"{name}_a"), 1)

            def broadcast(name, cols):
                for i in range(len(cols)):
                    ac.wait_ge(sem(f"{name}_mm"), at(f"{name}_mm", i + 1))
                    A(bc[cols[i][0]][:, 512:1024], bank[5 + 2 * (i % 2)][:, :], ACT.Copy).then_inc(sem(f"{name}_a"), 1)

            def experts(l):
                T = TL[l]
                sumsq(T, f"sumsq_f{l}", rh[:, 0:D], lambda t: (f"x_add{l}", T + t + 1))
                ac.wait_ge(sem(f"sumsq_f{l}"), at(f"sumsq_f{l}", T))
                root(stat[:, 0:T], T, D)
                for t in range(T):
                    ac.wait_ge(sem(f"h_ready{l}"), at(f"h_ready{l}", t + 1))
                    ac.dma_start(h_dram[l][t * P:(t + 1) * P, :], htok[:, t, :]).then_inc(sem(f"h_stored{l}"), 16)
                for k in range(1, KD, 2):
                    ac.wait_ge(sem(f"h_tr{l}"), at(f"h_tr{l}", k + 1))
                    A(hT[:, k, 0:T * P], bank[4 + k % 4][:, 0:T * P], ACT.Copy).then_inc(sem(f"h_a{l}"), 1)
                ac.wait_ge(sem(f"logits{l}"), at(f"logits{l}", 1))
                A(r_s[:, 0:T * NE], bank[0][:, 0:T * NE], ACT.Sigmoid).then_inc(sem(f"sig{l}"), 1)
                broadcast(f"gf{l}", gate_list(l))

                def rows_T(buf, when):
                    ac.wait_ge(sem(f"xT_hi{l}"), at(f"xT_hi{l}", when))
                    A(xgT[buf][:, 4:8, :], bank[1][:, :].rearrange("p (k n) -> p k n", k=4), ACT.Copy).then_inc(sem(f"xgT_a{l}"), 1)

                def pair(it, last_pair):
                    for u in range(2):
                        e = it * 2 + u
                        ac.wait_ge(chunks_used, e * 3 + (X0 if l == 0 else X1) + 2)
                        A(sg[u], bank[2][:, :], ACT.Silu).then_inc(sem(f"silu_ready{l}"), 1)
                        if not (last_pair and u == 1):
                            rows_T(1 - u, e + 2)
                        ac.wait_ge(sem(f"act_tr{l}"), at(f"act_tr{l}", e + 1))
                        A(actT[u], bank[4][:, :].rearrange("p (j n) -> p j n", j=4), ACT.Copy).then_inc(sem(f"actT_ready{l}"), 1)
                        ac.wait_ge(chunks_used, e * 3 + (X0 if l == 0 else X1) + 3)
                        ac.wait_ge(sem(f"y_stored{l}_{u}"), at(f"y_stored{l}_{u}", it * 16))
                        A(ybuf[u][:, 512:1024], bank[6][:, :], ACT.Copy).then_inc(sem(f"y_a{l}"), 1)
                        ac.wait_ge(sem(f"y_v{l}"), at(f"y_v{l}", e + 1))
                        ac.wait_ge(sem(f"y_a{l}"), at(f"y_a{l}", e + 1))
                        dst = y_dram[l][0:P * NE, :].rearrange("(s e) d -> s e d", e=NE)
                        if isinstance(e, int):
                            dst = dst[:, e, :]
                        else:
                            dst = dst[:, ds(e, 1), :].rearrange("s e d -> s (e d)")
                        ac.dma_start(dst, ybuf[u]).then_inc(sem(f"y_stored{l}_{u}"), 16)
                rows_T(0, 1)
                pair(0, False)
                with ac.Fori(1, NE // 2 - 1) as it:
                    pair(it, False)
                pair(NE // 2 - 1, True)

                ac.wait_ge(sem(f"flag_set{l}"), at(f"flag_set{l}", 1))
                over = ac.value_load(flag_i[l][0:1, :], min_val=0, max_val=1)
                with ac.If(over > 0):
                    with ac.Fori(0, ROUNDS[l]) as r:
                        with ac.Fori(0, NE) as e:
                            i = r * NE + e
                            ac.wait_ge(sem(f"over_used{l}"), at(f"over_used{l}", i * 3 + 2))
                            A(sg[0], bank[2][:, :], ACT.Silu).then_inc(sem(f"over_silu{l}"), 1)
                            ac.wait_ge(sem(f"over_act_tr{l}"), at(f"over_act_tr{l}", i + 1))
                            A(actT[0], bank[4][:, :].rearrange("p (j n) -> p j n", j=4), ACT.Copy).then_inc(sem(f"over_actT{l}"), 1)
                            ac.wait_ge(sem(f"over_y{l}"), at(f"over_y{l}", i * 2 + 2))
                            dst = y_dram[l][ds(r * (P * NE) + P * NE, P * NE), :].rearrange("(s e) d -> s e d", e=NE)
                            ac.dma_start(dst[:, ds(e, 1), :].rearrange("s e d -> s (e d)"), ybuf[0]).then_inc(sem(f"over_stored{l}"), 16)
                ac.nop()

            ac.wait_ge(sem("x_loaded"), at("x_loaded", 32))
            sumsq(NT, "sumsq0", rh[:, 0:D], lambda t: ("x_loaded", 32))
            norm(0)
            projected(0, [(o, w, NT) for o, w in EV_CH], z)
            ac.wait_ge(chunks_used, M1)
            ac.wait_ge(sem("z_v0"), at("z_v0", 10))
            ac.wait_ge(sem("z_a0"), at("z_a0", 10))
            for t in range(NT):
                if t:
                    ac.wait_ge(sem("lat_sums"), at("lat_sums", 2 * t))
                A(rh[:, 0:QL], z[:, t, 0:QL], ACT.Square, accum_out=stat[:, t:t + 1]).then_inc(sem("lat_sums"), 1)
                A(rh[:, QL:QL + KVL], z[:, t, QL:QL + KVL], ACT.Square, accum_out=stat[:, 4 + t:5 + t]).then_inc(sem("lat_sums"), 1)
            ac.wait_ge(sem("lat_sums"), at("lat_sums", 2 * NT))
            root(stat[:, 0:4], 4, QL)
            A(roots[:, 4:8], stat[:, 4:8], ACT.Sqrt, scale=1.0 / KVL, bias=const("eps")).then_inc(sem("root_ready"), 1)
            for b in range(5):
                ac.wait_ge(sem("ct_tr"), at("ct_tr", b + 1))
                A(cT[:, b, :], bank[4 + b % 4][:, :], ACT.Copy, scale=colv[:, C_NQ + b:C_NQ + b + 1]).then_inc(sem("ct_ready"), 1)
            for g in range(1, 20, 2):
                latent_done(ac, g)
                if g < MH:
                    ins = A(qT[0:QD, g, :], bank[g % 4][0:QD, :], ACT.Copy, scale=MLA_SCALE)
                elif g < 2 * MH:
                    ins = A(kT[0:NOPE, g - MH, :], bank[g % 4][0:NOPE, :], ACT.Copy)
                else:
                    ins = A(z[:, g - 2 * MH, 0:MH * MV], bank[g % 4][:, :], ACT.Copy)
                ins.then_inc(sem("lat_a"), 1)
            attend(0, 0)
            transposed("dT", 8, lambda g: (dqT if g < 4 else dkT)[:, g % 4, :], NTOK)
            for gi in (1, 2):
                attend(0, gi)
                for i in range(2):
                    root_of_sums(stat[:, 0:8], 8, DV)
            transposed("oT0", KD, lambda g: oT[:, g, :], NTOK)
            broadcast("bc0", bc_list(0))
            experts(0)
            sumsq(NT, "sumsq1", rh[:, 0:D], lambda t: ("x_moe0", NT))
            norm(1)
            projected(1, OD_CH, zo)
            for t in range(NT):
                root_of_sums(nrm[:, 0:10 if t < LT else 2], 10 if t < LT else 2, HD)
            transposed("gT", 8, lambda g: goT[:, g, :], SEQ, ATT_SCALE)
            for g in (1, 3):
                ac.wait_ge(sem("gk_tr"), at("gk_tr", g + 1))
                A(gkT[:, g, :], bank[g][:, :], ACT.Copy).then_inc(sem("gk_a"), 1)
            attend(1, 0)
            ac.wait_ge(sem("sink_arg"), at("sink_arg", 1))
            A(nsk, nsk, ACT.Exp).then_inc(sem("sink_exp"), 1)
            transposed("oT1", KD, lambda g: oT[:, g, 0:SEQ], SEQ)
            broadcast("bc1", bc_list(1))
            experts(1)
            sumsq(LT, "sumsq_out", rh[:, 0:D], lambda t: ("x_moe1", t + 1))
            ac.wait_ge(sem("sumsq_out"), at("sumsq_out", LT))
            root(stat[:, 0:LT], LT, D)
            for t in range(LT):
                ac.wait_ge(sem("out_ready"), at("out_ready", t + 1))
                ac.dma_start(out_dram[0, t * P:(t + 1) * P, :], ya[t]).then_inc(sem("out_stored"), 16)
            ac.wait_ge(sem("out_stored"), at("out_stored", 16 * LT))

        @block.gpsimd
        def _(gp):
            G = nc.gpsimd
            n_done = [0]

            def link(ins):
                n_done[0] += 1
                ins.then_inc(sem("g_chain"), 1)
                gp.wait_ge(sem("g_chain"), at("g_chain", n_done[0]))
            G.memset(zeros_i, 0).then_inc(sem("zero_list"), 1)

            def rope(src, cos, sin, heads, d, t1):
                q = d // 4
                s4 = src.rearrange("p (h x a q) -> p h x a q", h=heads, x=2, a=2)
                t4 = t1.rearrange("p (h x a q) -> p h x a q", h=heads, x=2, a=2)
                n4 = sin.rearrange("p (x a q) -> p x a q", x=2, a=2)
                for i in range(2):
                    link(G.tensor_tensor(t4[:, :, :, i, :], s4[:, :, :, 1 - i, :],
                                         n4[:, :, i, :].unsqueeze(1).to_broadcast([P, heads, 2, q]), ALU.mult))
                s2 = src.rearrange("p (h d) -> p h d", h=heads)
                link(G.tensor_tensor(s2, s2, cos.unsqueeze(1).to_broadcast([P, heads, d]), ALU.mult))
                return G.tensor_tensor(src, src, t1, ALU.add)

            def add_x(l):
                g = 0
                for i in range(2):
                    for t in range(TL[l]):
                        gp.wait_ge(sem(f"out_v{l}"), at(f"out_v{l}", g + 1))
                        xs = xt[:, t, i * 512:(i + 1) * 512]
                        G.tensor_tensor(xs, xs, rk[:, (g % 4) * 512:(g % 4 + 1) * 512], ALU.add).then_inc(sem(f"x_add{l}"), 1)
                        g += 1

            def experts(l):
                T = TL[l]
                for t in range(T):
                    gp.wait_ge(sem(f"h_scaled{l}"), at(f"h_scaled{l}", t + 1))
                    G.tensor_tensor(htok[:, t, :], htok[:, t, :], bc[4 + t // LT], ALU.add).then_inc(sem(f"h_ready{l}"), 1)
                gp.wait_ge(sem(f"idx{l}"), at(f"idx{l}", 2))
                gp.wait_ge(sem("list_zeroed"), at("list_zeroed", 32))
                for t in range(T):
                    for idx in (idx_hi, idx_lo):
                        gp.indirect_dma_start(out=list_dram[l], out_offset=bass.IndirectOffsetOnAxis(idx[:, t:t + 1], 0),
                                              in_=tokid_i[:, t:t + 1], in_offset=None).then_inc(sem(f"listed{l}"), 16)
                gp.wait_ge(sem(f"listed{l}"), at(f"listed{l}", 32 * T))
                gp.dma_start(slots_i, list_dram[l][0:P * NE, :].rearrange("(s e) o -> s (e o)", e=NE)).then_inc(sem(f"slots{l}"), 16)
                gp.wait_ge(sem(f"slots{l}"), at(f"slots{l}", 16))
                gp.wait_ge(sem(f"h_stored{l}"), at(f"h_stored{l}", 16 * T))
                for e in range(NE):
                    if e >= 2:
                        gp.wait_ge(sem(f"xT_hi{l}"), at(f"xT_hi{l}", e - 1))
                    gp.indirect_dma_start(out=xg[e % 2], out_offset=None, in_=h_dram[l],
                                          in_offset=bass.IndirectOffsetOnAxis(slots_i[:, e:e + 1], 0)).then_inc(sem(f"xg_loaded{l}_{e % 2}"), 16)
                over = gp.value_load(flag_i[l][0:1, :], min_val=0, max_val=1)
                with gp.If(over > 0):
                    gp.wait_ge(sem(f"xT_hi{l}"), at(f"xT_hi{l}", NE))
                    for i in range(ROUNDS[l] * NE):
                        r, e = i // NE + 1, i % NE
                        if i:
                            gp.wait_ge(sem(f"over_stored{l}"), at(f"over_stored{l}", 16 * i))
                        if e == 0:
                            gp.dma_start(slots_i, list_dram[l][r * P * NE:(r + 1) * P * NE, :].rearrange("(s e) o -> s (e o)", e=NE))\
                              .then_inc(sem(f"over_idx{l}"), 16)
                            gp.wait_ge(sem(f"over_idx{l}"), at(f"over_idx{l}", 16 * r))
                        gp.indirect_dma_start(out=xg[0], out_offset=None, in_=h_dram[l],
                                              in_offset=bass.IndirectOffsetOnAxis(slots_i[:, e:e + 1], 0)).then_inc(sem(f"over_xg{l}"), 16)
                    gp.wait_ge(sem(f"over_stored{l}"), at(f"over_stored{l}", 16 * ROUNDS[l] * NE))
                gp.nop()
                for b in range(2):
                    gp.wait_ge(sem(f"y_stored{l}_{b}"), at(f"y_stored{l}_{b}", 8 * NE))

                def result_rows(rows):
                    for t in range(T):
                        if t >= 2:
                            gp.wait_ge(sem(f"x_moe{l}"), at(f"x_moe{l}", t - 1))
                        for buf, idx, name in ((ya, idx_hi, "ya"), (yb, idx_lo, "yb")):
                            gp.indirect_dma_start(out=buf[t % 2], out_offset=None, in_=rows,
                                                  in_offset=bass.IndirectOffsetOnAxis(idx[:, t:t + 1], 0))\
                              .then_inc(sem(f"{name}_loaded{l}_{t % 2}"), 16)
                with gp.If(over > 0):
                    result_rows(y_dram[l])
                gp.nop()
                with gp.If(over < 1):
                    result_rows(y_dram[l][0:P * NE, :])
                gp.nop()

            gp.wait_ge(chunks_used, M1)
            gp.wait_ge(sem("z_v0"), at("z_v0", 10))
            gp.wait_ge(sem("z_a0"), at("z_a0", 10))
            gp.wait_ge(sem("small_loaded"), at("small_loaded", 16 * SMALL_LOADS))
            for t in range(LT):
                ins = rope(z[:, t, ZQ:ZQ + 1024], const("cos32")[:, t * RD:(t + 1) * RD], const("sin32")[:, t * RD:(t + 1) * RD],
                           32, 32, rh[:, 2560:3584])
                link(ins)
            for t in range(NT):
                G.tensor_scalar(z[:, t, ZQ:ZQ + 512], z[:, t, ZQ:ZQ + 512], DIFF_SCALE, None, ALU.mult)\
                 .then_inc(sem("diff_rope"), 1)
            gp.wait_ge(sem("kT_rope"), at("kT_rope", 1))
            gp.wait_ge(sem("diff_rope"), at("diff_rope", NT))
            G.tensor_copy(kT[64:96, 1:MH, :], kT[64:96, 0:1, :].to_broadcast([32, MH - 1, NTOK])).then_inc(sem("kT_ready"), 1)
            add_x(0)
            experts(0)
            gp.wait_ge(sem("z_v1"), at("z_v1", 6))
            gp.wait_ge(sem("z_a1"), at("z_a1", 6))
            for t in range(LT):
                ins = rope(zo[:, t, 0:640], const("cos64")[:, t * 64:(t + 1) * 64], const("sin64")[:, t * 64:(t + 1) * 64],
                           10, 64, rq[:, 3328:3968])
                link(ins)
            gp.wait_ge(sem("odd_rope_d"), at("odd_rope_d", 1))
            for g in range(4):
                o = (512 if g < 2 else 1280) + (g % 2) * HD
                for t in range(NT):
                    kd = kdup[:, (g * NT + t) * P:(g * NT + t + 1) * P].rearrange("p (c d) -> p c d", c=2)
                    ins = G.tensor_copy(kd, zo[:, t, o:o + HD].unsqueeze(1).to_broadcast([P, 2, HD]))
            ins.then_inc(sem("odd_rope_w"), 1)
            add_x(1)
            experts(1)


_INS = ["x", "c", "ctx", "c_ctx", "w_mod", "b_mod", "norm_mix", "norm_ffn", "even_w_in", "even_norm_q", "even_norm_kv",
        "even_w_uq", "even_w_ukv", "even_lambda", "even_subln", "even_w_out", "odd_w_in", "odd_sink", "odd_q_norm",
        "odd_k_norm", "odd_w_out", "w_router", "b_router", "w_gate", "w_up", "w_down", "norm_final"]


def kernel(**inputs):
    import concourse.bacc as bacc
    from concourse.bass_utils import run_bass_kernel_spmd

    nc = bacc.Bacc("TRN2", target_bir_lowering=False, num_devices=1)
    arrays = {f"in_{n}": np.ascontiguousarray(inputs[n]) for n in _INS}
    arrays["shape_consts"] = shape_constants()
    aps = {n: nc.dram_tensor(n, v.shape, mybir.dt.from_np(v.dtype), kind="ExternalInput").ap() for n, v in arrays.items()}
    out = nc.dram_tensor("out", (1, SEQ, D), mybir.dt.float32, kind="ExternalOutput").ap()
    build(nc, {n: aps[f"in_{n}"] for n in _INS}, aps["shape_consts"], out)
    r = run_bass_kernel_spmd(nc, [arrays], core_ids=[0])
    return r.results[0]["out"]
```

```python
import math
from contextlib import ExitStack

import numpy as np

import concourse.bass as bass
from concourse import mybir

P = 128
D = 1024
KD = D // P
SEQ, CTX = 256, 256
NT = (SEQ + CTX) // P
LT = SEQ // P
NTOK = SEQ + CTX
DEPTH = 2
GRID_W = 64
EPS = 1e-6
CH = 512
SLOTS = 6
SLOT = KD * CH
MODC = 6 * D // CH
PARTS = [(0, 4), (4, 6), (10, 2)]
QL, KVL, RD, NOPE, MV, MH = 384, 256, 32, 64, 64, 8
QD = NOPE + RD
DH, DD, DV = 8, 32, 64
EV_IN = QL + KVL + RD + 2 * DH * 2 * DD + DH * DV
EV_CH = [(0, QL, NT), (QL, KVL + RD, NT), (672, 512, NT), (1184, 512, NT), (1696, 512, NT)]
ZQ, ZK, ZV = 672, 1184, 1696
HD = 64
OD_IN = 1536
OD_CH = [(0, 512, LT), (512, 256, NT), (768, 512, LT), (1280, 256, NT)]
LAM_INIT = 0.8 - 0.6 * math.exp(-0.3 * 0)
MLA_SCALE, DIFF_SCALE, ATT_SCALE = QD ** -0.5, DD ** -0.5, HD ** -0.5
NE, NG, EG, FF = 16, 4, 4, 512
TL = [NT, LT]
ROUNDS = [t - 1 for t in TL]
ROWS = NTOK * NE

CONSTS = [("ident", P), ("ones", P), ("tri", P), ("cos32", LT * 32), ("sin32", LT * 32),
          ("cosT", SEQ), ("sinT", SEQ), ("rot", 32),
          ("cos64", LT * 64), ("sin64", LT * 64), ("wmask", 2 * P), ("lower", EG * EG),
          ("eidx", NE), ("tokid", NT), ("eps", 1)]


def shape_constants():
    c = {}
    p = np.arange(P)
    c["ident"] = np.eye(P)
    c["ones"] = np.ones((P, P))
    c["tri"] = (p[:, None] < p[None, :])
    t = np.arange(SEQ)

    def tables(rot):
        half = rot // 2
        inv = (np.float32(10000.0) ** (-np.arange(0, half, 2, dtype=np.float32) / np.float32(half))).astype(np.float32)
        cos, sin = [], []
        for pos in (t // GRID_W, t % GRID_W):
            ang = pos.astype(np.float32)[:, None] * inv[None, :]
            cos += [np.cos(ang), np.cos(ang)]
            sin += [-np.sin(ang), np.sin(ang)]
        return np.concatenate(cos, 1), np.concatenate(sin, 1)
    for rot in (32, 64):
        cos, sin = tables(rot)
        c[f"cos{rot}"] = cos.reshape(LT, P, rot).transpose(1, 0, 2).reshape(P, -1)
        c[f"sin{rot}"] = sin.reshape(LT, P, rot).transpose(1, 0, 2).reshape(P, -1)
    cos, sin = tables(32)
    tall = np.zeros((P, SEQ)); tall[64:96] = cos.T; c["cosT"] = tall
    tall = np.zeros((P, SEQ)); tall[64:96] = sin.T; c["sinT"] = tall
    rot = np.zeros((P, 32))
    for m in range(32):
        rot[64 + (m // 16) * 16 + (m % 16 + 8) % 16, m] = 1.0
    c["rot"] = rot
    far = np.zeros((P, 2, P))
    far[:, 0][p[None, :] > p[:, None]] = -1e30
    far[:, 1][p[None, :] < p[:, None]] = -1e30
    c["wmask"] = far.reshape(P, -1)
    i = np.arange(EG)
    c["lower"] = np.broadcast_to((i[None, :] < i[:, None]).reshape(1, -1), (P, EG * EG))
    c["eidx"] = np.broadcast_to(np.arange(NE)[None], (P, NE))
    c["tokid"] = p[:, None] + P * np.arange(NT)[None, :]
    c["eps"] = np.full((P, 1), EPS)
    sel = np.zeros((P, 2, 2, 4, P))
    for kind, rows in enumerate(((0, 0, 1, 1), (0, 1, 0, 1))):
        for q, part in enumerate(rows):
            for j in range(4):
                for i in range(32):
                    sel[32 * j + i, kind, part, j, 32 * q + i] = 1.0
    return np.concatenate([np.asarray(c[n], np.float32).reshape(P, w) for n, w in CONSTS] +
                          [sel.reshape(P, 2048).astype(np.float32)], 1)


def build(nc, a, consts_dram, out_dram, dbg=None, cap=P):
    f32, i32, f32r = mybir.dt.float32, mybir.dt.int32, mybir.dt.float32r
    ALU = mybir.AluOpType
    ACT = mybir.ActivationFunctionType
    AX = mybir.AxisListType.X
    ds = bass.ds
    ctx = ExitStack()
    layer0_total = {
        "scol{}": 4, "sumsq{}": NT, "xn_ready{}": NT,
        "xT0_{}": KD // 2, "xT1_{}": KD // 2, "hT0_{}": KD, "hT1_{}": KD,
        "h_part{}": KD, "h_split{}": KD, "w_half{}": len(EV_CH), "w_hi{}": 2 * len(EV_CH), "w_lo{}": 2 * len(EV_CH),
        "z_v{}": 10, "z_a{}": 10, "z_mm{}": len(EV_CH) * (NT - 1),
        "s_ready{}": 96, "max_ready{}": 96, "p_ready{}": 96, "t_ready{}": 96, "pT_ready{}": 96, "pv_done{}": 96,
        "out_mm{}": 2 * (NT - 1), "out_v{}": 2 * NT, "x_add{}": 2 * NT,
        "sumsq_f{}": NT, "h_ready{}": NT, "h_stored{}_0": 8 * NT, "h_stored{}_1": 8 * NT,
        "h_lo{}": NT, "h_hi{}": NT, "h_v{}": NT, "h_a{}": NT,
        "logits{}": 1, "sig{}": 1, "mask{}": 1, "counts{}": 1, "idx{}": 2, "flag_set{}": 1, "listed{}": 32 * NT, "slots{}": 16,
        "xg_loaded{}_0": 8 * NE, "xg_loaded{}_1": 8 * NE, "xT_lo{}": NE, "xT_hi{}": NE, "xgT_v{}": 2 * NE, "xgT_a{}": 2 * NE,
        "ex_hi{}": 4 * NE, "ex_lo{}": 4 * NE, "gate_half{}": NE,
        "silu_ready{}": NE, "act_ready{}": NE, "act_tr{}": NE, "actT_ready{}": NE, "y_mm{}": NE, "y_v{}": NE, "y_a{}": NE,
        "y_stored{}_0": 8 * NE, "y_stored{}_1": 8 * NE,
        "ya_loaded{}_0": 32, "ya_loaded{}_1": 32, "yb_loaded{}_0": 32, "yb_loaded{}_1": 32, "x_moe{}": NT,
    }
    sems, alias = {}, {}
    for n, total in layer0_total.items():
        for l in range(DEPTH):
            alias[n.format(l)] = (n.format(""), l * total)
    for kind, stages in (("blocks", [("dT", 32), ("oT0", 8), ("gT", 8), ("oT1", 8)]),
                         ("rows", [("bc0", 6), ("gf0", 2), ("bc1", 3), ("gf1", 1)])):
        at = 0
        for n, count in stages:
            for part, share in ((("tr", 1), ("v", 2), ("a", 2)) if kind == "blocks" else
                                (("diag", 1), ("mm", 1), ("v", 1), ("a", 1))):
                alias[f"{n}_{part}"] = (f"{kind}_{part}", at // share)
            at += count

    def sem(name):
        n = alias.get(name, (name, 0))[0]
        if n not in sems:
            sems[n] = ctx.enter_context(nc.semaphore(n))
        return sems[n]

    def at(name, value):
        return value + alias.get(name, (name, 0))[1]

    def sb(name, shape, dt=f32):
        return ctx.enter_context(nc.sbuf_tensor(name, shape, dt))

    h_dram = [nc.dram_tensor(f"h_rows{l}", [(NT if l == 0 else LT) * P, D], f32).ap() for l in range(DEPTH)]
    list_dram = [nc.dram_tensor(f"slot_list{l}", [ROWS, 1], i32).ap() for l in range(DEPTH)]
    y_dram = [nc.dram_tensor(f"y_rows{l}", [TL[l] * P * NE, D], f32).ap() for l in range(DEPTH)]

    with ctx:
        with ExitStack() as first_names:
            def named(name, cols):
                return first_names.enter_context(nc.sbuf_tensor(name, [P, cols], f32))
            ring = [named(f"ring{i}", SLOT) for i in range(SLOTS)]
            rq, rk, rh, rz = (named(f"region_{n}", cols) for n, cols in (("q", 4096), ("k", 4096), ("h", 4096), ("z", NT * EV_IN)))
        ring_r = [sb(f"ring{i}_r", [P, SLOT], f32r) for i in range(SLOTS)]
        rq_r = sb("region_q_r", [P, 4096], f32r)
        rk_r = sb("region_k_r", [P, 4096], f32r)
        rh_r = sb("region_h_r", [P, 4096], f32r)
        rz_r = sb("region_z_r", [P, NT * EV_IN], f32r)
        x = sb("x", [P, NT * D])
        NCON = sum(w for _, w in CONSTS)
        con = sb("con", [P, NCON])
        small = sb("small", [P, 1283])
        small_i = sb("small_i", [P, 96], i32)
        bank = [ctx.enter_context(nc.psum_tensor(f"bank{i}", [P, 512], f32)) for i in range(8)]

        off = {}
        o = 0
        for n, w in CONSTS:
            off[n] = (o, w)
            o += w

        def const(n):
            return con[:, off[n][0]:off[n][0] + off[n][1]]
        so = [0]

        def sm(w):
            so[0] += w
            assert so[0] <= 1283, so[0]
            return small[:, so[0] - w:so[0]]
        ident, ones, tri = const("ident"), const("ones"), const("tri")
        colv = sm(56)
        C_C, C_NM, C_NF, C_NQ, C_NKV = 0, 16, 32, 48, 51
        bmodT = sm(96)
        modT = sm(2 * 96)
        silu = sm(16)
        scols = [sm(32), sm(32)]
        stat = sm(8)
        rstd = sm(8)
        lamv = sm(4)
        nsink, nsk, nrm = sm(8), sm(16), sm(10)
        nmx = sm(64)
        roots = sm(10)
        rsum = sm(64)
        rinv = sm(64)
        tokid_i = small_i[:, 0:4]
        idx_hi = small_i[:, 4:8]
        idx_lo = small_i[:, 8:12]
        slots_i = small_i[:, 12:28]
        zeros_i = small_i[:, 32:96]
        kdup = rk[:, 2048:4096]
        flag_i = [small_i[:, 30 + l:31 + l] for l in range(DEPTH)]

        def mod(l, s, r):
            return modT.rearrange("p (l s k r) -> p l s k r", l=2, s=6, r=2)[:, l, s, :, r]
        xt = x[:, :].rearrange("p (t d) -> p t d", t=NT)
        hT = rh[:, :].rearrange("p (k n) -> p k n", k=KD)
        xn = rz[:, 0:4096].rearrange("p (t d) -> p t d", t=NT)
        slot = [r[:, :] for r in ring]
        slotk = [s.rearrange("p (k n) -> p k n", k=KD) for s in slot]
        bc = [rz[:, i * D:(i + 1) * D] for i in range(6)]
        diag = [rh[:, i * D:(i + 1) * D] for i in range(2)]

        modrow = [rk[0:2, i * CH:(i + 1) * CH] for i in range(2)]
        z = rz[:, :].rearrange("p (t n) -> p t n", t=NT)
        zo = rz[:, 0:NT * OD_IN].rearrange("p (t n) -> p t n", t=NT)
        cT = hT
        qT = rq[:, :].rearrange("p (h n) -> p h n", h=MH)
        kT = rk[:, :].rearrange("p (h n) -> p h n", h=MH)
        probs = [rh[:, i * 512:(i + 1) * 512] for i in range(4)]
        probsT = [rh[:, (4 + i) * 512:(5 + i) * 512] for i in range(2)]
        tmp = [rh[:, (6 + i) * 512:(7 + i) * 512] for i in range(2)]
        d_hi, d_lo = (r[:, :].rearrange("p (b n) -> p b n", b=8) for r in (rq_r, rk_r))
        hT_hi, hT_lo = (r[:, :].rearrange("p (k n) -> p k n", k=KD) for r in (rq_r, rh_r))
        w_hi = rk_r[:, :].rearrange("p (k n) -> p k n", k=KD)
        slot_r = [r[:, :] for r in ring_r]
        oT = rq[:, :].rearrange("p (k n) -> p k n", k=KD)
        goT = rq[:, 0:KD * SEQ].rearrange("p (b n) -> p b n", b=KD)
        gkT = rk[:, 0:2048].rearrange("p (b n) -> p b n", b=4)
        htok = [rk[:, (2 + i) * D:(3 + i) * D] for i in range(2)]
        junk = rz[:, 6 * D:7 * D]
        modrow1 = [rz[0:2, 8832 - (2 - i) * CH:8832 - (1 - i) * CH] for i in range(2)]
        xg = [rk[:, i * D:(i + 1) * D] for i in range(2)]
        ybuf = [rk[:, (2 + i) * D:(3 + i) * D] for i in range(2)]
        xgT = [rq[:, i * D:(i + 1) * D].rearrange("p (k n) -> p k n", k=KD) for i in range(2)]
        sg = [rh[:, i * 512:(i + 1) * 512] for i in range(2)]
        act_ = [rh[:, (2 + i) * 512:(3 + i) * 512] for i in range(2)]
        actT = [rh[:, (4 + i) * 512:(5 + i) * 512].rearrange("p (j n) -> p j n", j=4) for i in range(2)]
        ya = [rq[:, i * D:(i + 1) * D] for i in range(2)]
        yb = [rq[:, (2 + i) * D:(3 + i) * D] for i in range(2)]
        ow = rz[:, 2 * D:2 * D + 4096]
        over_w = [ow.rearrange("p (k n) -> p k n", k=KD), ow.rearrange("p (k n) -> p k n", k=KD),
                  ow.rearrange("p (k n) -> p k n", k=4)]
        xg_hi, xg_lo = ([rq_r[:, (2 * j + i) * D:(2 * j + i + 1) * D].rearrange("p (k n) -> p k n", k=KD) for i in range(2)]
                        for j in range(2))

        def blocks_of(region, o, n):
            return region[:, o:o + n * CH].rearrange("p (k n) -> p k n", k=n)
        quarter = [[blocks_of(rz_r, 2 * D, 4)], [blocks_of(rz_r, 4 * D, 4)],
                   [blocks_of(rz_r, NT * EV_IN - 2 * CH, 2), blocks_of(rh_r, 3 * D, 2)]]
        quarter.append(quarter[0])
        ro = [6 * D]

        def rt(w):
            ro[0] += w
            assert ro[0] <= NT * EV_IN - 2 * CH
            return rz[:, ro[0] - w:ro[0]]
        r_s, r_sel, r_beat, r_eq = rt(64), rt(64), rt(256), rt(256)
        r_top, r_gs, r_mask, r_w, r_pos, r_val, r_t = rt(64), rt(16), rt(64), rt(64), rt(64), rt(64), rt(64)
        r_gb, r_hi, r_lo, r_whi, r_wlo, r_sum, r_cnt = rt(64), rt(4), rt(4), rt(4), rt(4), rt(4), rt(16)
        wr_sb, br_sb = sm(KD * NE), sm(NE)
        subln_b, lam_b = sm(64), sm(128)
        sink_b, qk_b = sm(8), sm(128)

        dops = []
        for kind in range(2):
            dops.append([slot_r[(19 + 2 * kind + c // 8) % SLOTS][:, (c % 8) * NTOK:(c % 8 + 1) * NTOK] for c in range(16)])

        slotk_r = [s.rearrange("p (k n) -> p k n", k=KD) for s in slot_r]

        M0 = 0
        E0 = M0 + MODC
        U0 = E0 + len(EV_CH)
        S0 = U0 + 2
        SEL = S0 + 4
        O0 = SEL + 1
        MA = O0 + 2
        X0 = MA + PARTS[0][1]
        MB = X0 + 3 * NE
        E1 = MB + PARTS[1][1]
        MC_ = E1 + len(OD_CH)
        O1 = MC_ + PARTS[2][1]
        X1 = O1 + 2
        END = X1 + 3 * NE

        def view(w, cols, o=0):
            return w[:, o:o + cols].rearrange("(k p) n -> p k n", p=P)
        assert S0 == 19
        chunks_used = sem("chunks_used")
        full = [sem(f"slot_full{i}") for i in range(SLOTS)]

        def arrived(eng, n, it=None, step=1):
            v = 16 * (n // SLOTS + 1)
            if n > SEL and n % SLOTS in [c % SLOTS for c in range(S0, SEL)]:
                v -= 16
            eng.wait_ge(full[n % SLOTS], v if it is None else it * (16 * step) + v)

        def product_done(eng, name, base, tiles, i, t):
            if t == tiles[i] - 1:
                eng.wait_ge(chunks_used, base + i + 1)
            else:
                eng.wait_ge(sem(name), at(name, sum(n - 1 for n in tiles[:i]) + t + 1))

        def latent_done(eng, g):
            if g in (MH - 1, 2 * MH + NT - 1):
                eng.wait_ge(chunks_used, U0 + (1 if g < MH else 2))
            else:
                eng.wait_ge(sem("lat_mm"), at("lat_mm", g + (1 if g < MH else 0)))

        block = ctx.enter_context(nc.Block())

        @block.sync
        def _(sp):
            def load(n, dst, src, it=None, step=1):
                if n >= SLOTS or it is not None:
                    v = n - SLOTS + 1
                    sp.wait_ge(chunks_used, v if it is None else it * (SLOTS * step) + v)
                sp.dma_start(dst, src).then_inc(full[n % SLOTS], 16)

            s_v = sem("small_loaded")
            sp.dma_start(con[:, :], consts_dram[:, 0:NCON]).then_inc(s_v, 16)
            vecs = rq[:, 0:P]
            rows = [(a["c"].rearrange("a (k p) -> (a k) p", p=P), 8),
                    (a["c_ctx"].rearrange("(k p) -> k p", p=P), 8),
                    (a["norm_mix"].rearrange("l (k p) -> (l k) p", p=P), 16),
                    (a["norm_ffn"].rearrange("l (k p) -> (l k) p", p=P), 16),
                    (a["even_norm_q"].rearrange("l (k p) -> (l k) p", p=P), 3),
                    (a["even_norm_kv"].rearrange("l (k p) -> (l k) p", p=P), 2)]
            wide = [(subln_b, a["even_subln"][0]), (lam_b, a["even_lambda"][0].rearrange("a b -> (a b)")),
                    (sink_b, a["odd_sink"][0]), (qk_b[:, 0:64], a["odd_q_norm"][0]), (qk_b[:, 64:128], a["odd_k_norm"][0]),
                    (br_sb, a["b_router"])]
            r = 0
            for src, n in rows:
                sp.dma_start(vecs[r:r + n, :], src).then_inc(s_v, 16)
                r += n
            sp.dma_start(rq[0:96, P:2 * P], a["b_mod"].rearrange("l (k p) -> (l k) p", p=P)).then_inc(s_v, 16)

            def modulation(base, l, c0, n):
                for j in range(n):
                    load(base + j, slotk[(base + j) % SLOTS], view(a["w_mod"][l], CH, (c0 + j) * CH))
            modulation(M0, 0, 0, 3)
            for dst, src in wide:
                sp.dma_start(dst, src.partition_broadcast(P)).then_inc(sem("wide_loaded"), 16)
            sp.dma_start(wr_sb.rearrange("p (k e) -> p k e", k=KD), a["w_router"].rearrange("(k p) e -> p k e", p=P)).then_inc(sem("wide_loaded"), 16)
            sp.dma_start(xt[:, 0:LT, :], a["x"].rearrange("a (t p) d -> p (a t) d", p=P)).then_inc(sem("x_loaded"), 16)
            sp.dma_start(xt[:, LT:NT, :], a["ctx"].rearrange("a (t p) d -> p (a t) d", p=P)).then_inc(sem("x_loaded"), 16)
            modulation(M0 + 3, 0, 3, MODC - 3)
            for i, (o, w, _) in enumerate(EV_CH):
                n = E0 + i
                load(n, slotk[n % SLOTS][:, :, 0:w], view(a["even_w_in"][0], w, o))
            load(U0, slot[U0 % SLOTS][:, 0:3 * 768].rearrange("p (k n) -> p k n", k=3), view(a["even_w_uq"][0], 768))
            load(U0 + 1, slot[(U0 + 1) % SLOTS][:, 0:2 * 1024].rearrange("p (k n) -> p k n", k=2), view(a["even_w_ukv"][0], 1024))
            load(SEL, slot[SEL % SLOTS][:, 0:2048], consts_dram[:, NCON:NCON + 2048])
            for i in range(2):
                n = O0 + i
                load(n, slotk[n % SLOTS], view(a["even_w_out"][0], CH, i * CH))

            def experts(base, l):
                gate = a["w_gate"][l].rearrange("e (k p) f -> e p k f", p=P)
                up = a["w_up"][l].rearrange("e (k p) f -> e p k f", p=P)
                down = a["w_down"][l].rearrange("e (j p) d -> e p j d", p=P)
                with sp.Fori(0, NE // 2) as it:
                    for u in range(2):
                        e = it * 2 + u
                        for j, w in enumerate((gate, up, down)):
                            n = base + 3 * u + j
                            s = slotk[n % SLOTS] if j < 2 else slot[n % SLOTS].rearrange("p (j n) -> p j n", j=4)
                            load(n, s, w[ds(e, 1)].rearrange("e p k f -> (e p) k f"), it=it)

            def overflow(l):
                sp.wait_ge(sem(f"flag_set{l}"), at(f"flag_set{l}", 1))
                over = sp.value_load(flag_i[l][0:1, :], min_val=0, max_val=1)
                with sp.If(over > 0):
                    mats = [(a["w_gate"][l], FF), (a["w_up"][l], FF), (a["w_down"][l], D)]
                    sp.wait_ge(sem(f"y_v{l}"), at(f"y_v{l}", NE))
                    with sp.Fori(0, ROUNDS[l]) as r:
                        with sp.Fori(0, NE) as e:
                            for j in range(3):
                                if j == 0:
                                    sp.wait_ge(sem(f"over_xT{l}"), at(f"over_xT{l}", r * NE + e + 1))
                                else:
                                    sp.wait_ge(sem(f"over_used{l}"), at(f"over_used{l}", (r * NE + e) * 3 + j))
                                sp.dma_start(over_w[j], mats[j][0][ds(e, 1)].rearrange(
                                    "a (k p) n -> p (a k) n", p=P)).then_inc(sem(f"over_loaded{l}"), 16)
                sp.nop()
            modulation(MA, 1, *PARTS[0])
            experts(X0, 0)
            overflow(0)
            modulation(MB, 1, *PARTS[1])
            for i, (o, w, _) in enumerate(OD_CH):
                n = E1 + i
                load(n, slotk[n % SLOTS][:, :, 0:w], view(a["odd_w_in"][0], w, o))
            modulation(MC_, 1, *PARTS[2])
            for i in range(2):
                n = O1 + i
                load(n, slotk[n % SLOTS], view(a["odd_w_out"][0], CH, i * CH))
            experts(X1, 1)
            overflow(1)
            sp.wait_ge(sem("sumsq1"), at("sumsq1", NT))
            sp.wait_ge(sem("xn_ready1"), at("xn_ready1", NT))
            sp.dma_start(xt[:, LT, :], a["norm_final"].partition_broadcast(P)).then_inc(sem("nf_loaded"), 16)
            sp.wait_ge(sem("out_stored"), at("out_stored", 16 * LT))

        SMALL_LOADS, WIDE_LOADS = 8, 7

        def even_group(gi):
            units = []
            if gi == 0:
                for h in range(MH):
                    for t in range(NT):
                        k0 = 0 if t < LT else SEQ
                        units.append((qT[0:QD, h, t * P:(t + 1) * P], kT[0:QD, h, k0:NTOK], NTOK - k0,
                                      [z[:, j, h * MV:(h + 1) * MV] for j in range(k0 // P, NT)],
                                      bank[4 + t][:, h * MV:(h + 1) * MV]))
            else:
                for h in range(DH):
                    for c in range(2):
                        for i in range(LT):
                            t = i if gi == 1 else LT + i
                            k0 = 0 if gi == 1 else SEQ
                            units.append((dops[0][2 * h + c][:, t * P:(t + 1) * P], dops[1][2 * h + c][:, k0:NTOK], NTOK - k0,
                                          [z[:, j, ZV + h * DV:ZV + (h + 1) * DV] for j in range(k0 // P, NT)],
                                          bank[4 + 2 * c + i][:, h * DV:(h + 1) * DV]))
            return units

        def odd_units():
            units = []
            for h in range(8):
                for kind in range(2):
                    for t in range(LT):
                        r = 64 * (h % 2)
                        v0 = 640 if kind == 0 else 1408
                        units.append((goT[r:r + 64, 4 * kind + h // 2, t * P:(t + 1) * P],
                                      gkT[r:r + 64, 2 * kind + h // 4, :], NTOK,
                                      [zo[:, j, v0 + (h // 4) * HD:v0 + (h // 4 + 1) * HD] for j in range(NT)],
                                      bank[4 + 2 * kind + t][:, h * HD:(h + 1) * HD]))
            return units
        GROUPS = [[even_group(0), even_group(1), even_group(2)], [odd_units()]]
        GBASE = [[0, 32, 64], [0]]

        def bc_list(l):
            rs = range(2) if l == 0 else range(1)
            return [(0 + r, mod(l, 2, r)) for r in rs] + [(2 + r, scols[l][:, 8 * r + 16:8 * r + 24]) for r in rs] + \
                   [(4 + r, mod(l, 3, r)) for r in rs]

        def gate_list(l):
            return [(r, mod(l, 5, r)) for r in (range(2) if l == 0 else range(1))]

        @block.tensor
        def _(pe):
            mm = nc.tensor.matmul
            tr = nc.tensor.transpose
            pe.wait_ge(sem("small_loaded"), at("small_loaded", 16 * SMALL_LOADS))
            tr(bank[0][:, 0:53], rq[0:53, 0:P], ident[0:53, 0:53])
            tr(bank[1][:, 0:96], rq[0:96, P:2 * P], ident[0:96, 0:96]).then_inc(sem("vec_cols"), 1)

            def modulation0():
                def to_cols(it, j):
                    pe.wait_ge(sem("mod_row"), it * SLOTS + j + 1)
                    if j >= 2:
                        pe.wait_ge(sem("mod_T"), it * SLOTS + j - 1)
                    for i in range(4):
                        last = mm(bank[2 + j % 2][:, 2 * i:2 * i + 2], modrow[j % 2][:, i * P:(i + 1) * P],
                                  ident[0:2, 0:2], start=True, stop=True)
                    last.then_inc(sem("mod_cols"), 1)
                with pe.Fori(0, MODC // SLOTS) as it:
                    for j in range(SLOTS):
                        arrived(pe, M0 + j, it)
                        if j >= 2:
                            pe.wait_ge(sem("mod_row"), it * SLOTS + j - 1)
                        for k in range(KD):
                            last = mm(bank[j % 2][0:2, :], silu.rearrange("p (r k) -> p k r", r=2)[:, k, :],
                                      slotk[(M0 + j) % SLOTS][:, k, :], start=k == 0, stop=k == KD - 1)
                        last.then_inc(chunks_used, 1)
                        if j > 0:
                            to_cols(it, j - 1)
                    to_cols(it, SLOTS - 1)
                    pe.wait_ge(sem("mod_T"), it * SLOTS + SLOTS)

            def modulation1(part, base, between):
                c0, n = PARTS[part]

                def to_cols(j):
                    pe.wait_ge(sem("mod1_row"), c0 + j + 1)
                    for i in range(4):
                        last = mm(bank[0][:, 8 * j + 2 * i:8 * j + 2 * i + 2], modrow1[(c0 + j) % 2][:, i * P:(i + 1) * P],
                                  ident[0:2, 0:2], start=True, stop=True)
                    last.then_inc(sem("mod1_cols"), 1)
                for j in range(n):
                    arrived(pe, base + j)
                    if j >= 2:
                        pe.wait_ge(sem("mod1_row"), c0 + j - 1)
                    for k in range(KD):
                        last = mm(bank[2 + j % 2][0:2, :], silu.rearrange("p (r k) -> p k r", r=2)[:, k, :],
                                  slotk[(base + j) % SLOTS][:, k, :], start=k == 0, stop=k == KD - 1)
                    last.then_inc(chunks_used, 1)
                    if j > 0:
                        to_cols(j - 1)
                    if j in between:
                        between[j]()
                to_cols(n - 1)

            def norm_T(l):
                for kp in range(KD // 2):
                    for grp in range(2):
                        if kp == 0:
                            pe.wait_ge(sem(f"xn_ready{l}"), at(f"xn_ready{l}", 2 * (grp + 1)))
                        if kp >= 2:
                            pe.wait_ge(sem(f"hT{grp}_{l}"), at(f"hT{grp}_{l}", 2 * (kp - 1)))
                        for kk in range(2):
                            for i in range(2):
                                k, t = 2 * kp + kk, 2 * grp + i
                                last = tr(bank[4 + 2 * grp + kp % 2][:, kk * 256 + i * P:kk * 256 + (i + 1) * P],
                                          xn[:, t, k * P:(k + 1) * P], ident)
                        last.then_inc(sem(f"xT{grp}_{l}"), 1)

            def project(l, base, chunks):
                first = [sum(c[2] for c in chunks[:i]) for i in range(len(chunks))]
                for i, (o, w, tiles) in enumerate(chunks):
                    n = base + i
                    for half in range(2):
                        pe.wait_ge(sem(f"w_lo{l}"), at(f"w_lo{l}", 2 * i + half + 1))
                        for t in range(tiles):
                            if half == 0 and i >= 2:
                                g = first[i - 2] + t
                                if t < chunks[i - 2][2]:
                                    pe.wait_ge(sem(f"z_{'va'[g % 2]}{l}"), at(f"z_{'va'[g % 2]}{l}", g // 2 + 1))
                            for k in range(4 * half, 4 * half + 4):
                                if i == 0 and t == 0:
                                    pe.wait_ge(sem(f"h_split{l}"), at(f"h_split{l}", k + 1))
                                hh, hl = hT_hi[:, k, t * P:(t + 1) * P], hT_lo[:, k, t * P:(t + 1) * P]
                                wh, wl = w_hi[:, k, 0:w], slotk_r[n % SLOTS][:, k, 0:w]
                                out = bank[4 * (i % 2) + t][:, 0:w]
                                mm(out, hh, wh, start=k == 0, stop=False)
                                mm(out, hh, wl, start=False, stop=False)
                                last = mm(out, hl, wh, start=False, stop=k == KD - 1)
                            if half == 1:
                                last.then_inc(chunks_used if t == tiles - 1 else sem(f"z_mm{l}"), 1)
                            elif t == tiles - 1:
                                last.then_inc(sem(f"w_half{l}"), 1)

            def attend(l, gi):
                units, b = GROUPS[l][gi], GBASE[l][gi]
                if gi > 0:
                    pe.wait_ge(sem(f"o_read{l}"), at(f"o_read{l}", 4 * gi))

                def scores(u):
                    q, k, nk, _, _ = units[u]
                    if b + u >= 2:
                        pe.wait_ge(sem(f"p_ready{l}"), at(f"p_ready{l}", b + u - 1))
                    mm(bank[(b + u) % 2][:, 0:nk], q, k, start=True, stop=True).then_inc(sem(f"s_ready{l}"), 1)
                scores(0)
                scores(1)
                for u in range(len(units) + 1):
                    if u < len(units):
                        pe.wait_ge(sem(f"p_ready{l}"), at(f"p_ready{l}", b + u + 1))
                        if b + u >= 2:
                            pe.wait_ge(sem(f"pT_ready{l}"), at(f"pT_ready{l}", b + u - 1))
                        for j in range(units[u][2] // P):
                            last = tr(bank[2 + (b + u) % 2][:, j * P:(j + 1) * P], probs[(b + u) % 4][:, j * P:(j + 1) * P], ident)
                        last.then_inc(sem(f"t_ready{l}"), 1)
                    if u + 2 < len(units):
                        scores(u + 2)
                    if u >= 1:
                        _, _, nk, vs, out = units[u - 1]
                        pe.wait_ge(sem(f"pT_ready{l}"), at(f"pT_ready{l}", b + u))
                        for j, v in enumerate(vs):
                            last = mm(out, probsT[(b + u - 1) % 2][:, j * P:(j + 1) * P], v, start=j == 0, stop=j == len(vs) - 1)
                            if (l, gi, u, j) == (0, 2, len(units), 0):
                                last.then_inc(chunks_used, 5)
                        last.then_inc(sem(f"pv_done{l}"), 1)

            def block_T(name, blocks, ready):
                for s_, v_ in ready:
                    pe.wait_ge(sem(s_), at(s_, v_))
                for g, tiles in enumerate(blocks):
                    if g >= 4:
                        pe.wait_ge(sem(f"{name}_{'va'[g % 2]}"), at(f"{name}_{'va'[g % 2]}", (g - 4) // 2 + 1))
                    for i, src in enumerate(tiles):
                        last = tr(bank[g % 4][:, i * P:(i + 1) * P], src, ident)
                    last.then_inc(sem(f"{name}_tr"), 1)

            def broadcast(name, n, first):
                for i in range(n):
                    pe.wait_ge(sem(f"{name}_diag"), at(f"{name}_diag", i + 1))
                    if i >= 2:
                        pe.wait_ge(sem(f"{name}_v"), at(f"{name}_v", i - 1))
                        pe.wait_ge(sem(f"{name}_a"), at(f"{name}_a", i - 1))
                    for h in range(2):
                        last = mm(bank[4 + 2 * (i % 2) + h][:, :], ones, diag[i % 2][:, h * 512:(h + 1) * 512], start=True, stop=True)
                    last.then_inc(sem(f"{name}_mm"), 1)

            def out_project(l, base):
                T = TL[l]

                def token_T(t):
                    pe.wait_ge(sem(f"h_ready{l}"), at(f"h_ready{l}", t + 1))
                    if t >= 2:
                        pe.wait_ge(sem(f"h_v{l}"), at(f"h_v{l}", t - 1))
                        pe.wait_ge(sem(f"h_a{l}"), at(f"h_a{l}", t - 1))
                    for k in range(KD):
                        ins = tr(bank[4 + 2 * (t % 2) + k // 4][:, (k % 4) * P:(k % 4 + 1) * P], htok[t % 2][:, k * P:(k + 1) * P], ident)
                        if k % 4 == 3:
                            ins.then_inc(sem(f"h_lo{l}") if k == 3 else sem(f"h_hi{l}"), 1)

                def router(t):
                    pe.wait_ge(sem(f"h_v{l}"), at(f"h_v{l}", t + 1))
                    pe.wait_ge(sem(f"h_a{l}"), at(f"h_a{l}", t + 1))
                    for k in range(KD):
                        last = mm(bank[0][:, t * NE:(t + 1) * NE], hT[:, k, t * P:(t + 1) * P],
                                  wr_sb[:, k * NE:(k + 1) * NE], start=k == 0, stop=k == KD - 1)
                    if t == T - 1:
                        last.then_inc(sem(f"logits{l}"), 1)
                pe.wait_ge(sem("wide_loaded"), 16 * WIDE_LOADS)
                pe.wait_ge(sem(f"oT{l}_v"), at(f"oT{l}_v", 4))
                pe.wait_ge(sem(f"oT{l}_a"), at(f"oT{l}_a", 4))
                g = 0
                for i in range(2):
                    n = base + i
                    arrived(pe, n)
                    for t in range(T):
                        if g >= 4:
                            pe.wait_ge(sem(f"out_v{l}"), at(f"out_v{l}", g - 3))
                        for k in range(KD):
                            last = mm(bank[g % 4][:, :], oT[:, k, t * P:(t + 1) * P], slotk[n % SLOTS][:, k, :],
                                      start=k == 0, stop=k == KD - 1)
                        last.then_inc(chunks_used if t == T - 1 else sem(f"out_mm{l}"), 1)
                        g += 1
                        if i == 1 and t >= 2:
                            token_T(t - 2)
                for t in range(T - 2, T):
                    if t >= 1:
                        if t == T - 2:
                            router(t - 2) if t >= 2 else None
                    token_T(t)
                    if t >= 1:
                        router(t - 1)
                router(T - 1)

            def experts(l, base):
                T = TL[l]
                m = r_mask.rearrange("p (t e) -> p t e", e=NE)

                def counts():
                    pe.wait_ge(sem(f"mask{l}"), at(f"mask{l}", 1))
                    later = lambda b: m[:, b:b + 1, :].to_broadcast([P, T - b, NE])
                    out = lambda b: bank[1][:, b * NE:(T + 1) * NE].rearrange("p (t e) -> p t e", e=NE)
                    mm(bank[1][:, 0:NE], tri, m[:, 0, :], start=True, stop=True)
                    mm(out(1), ones, later(0), start=True, stop=False)
                    mm(bank[1][:, NE:T * NE], tri, r_mask[:, NE:T * NE], start=False, stop=False)
                    for b in range(1, T):
                        last = mm(out(b + 1), ones, later(b), start=False, stop=b == T - 1)
                    last.then_inc(sem(f"counts{l}"), 1)

                def gates():
                    broadcast(f"gf{l}", len(gate_list(l)), True)
                if l == 0:
                    pe.wait_ge(sem(f"sig{l}"), at(f"sig{l}", 1))
                    modulation1(0, MA, {0: counts, 1: gates})
                else:
                    counts()
                    gates()

                def rows_T(buf, when, loaded):
                    pe.wait_ge(sem(loaded), at(loaded, when))
                    for k in range(KD):
                        last = tr(bank[k // 4][:, (k % 4) * P:(k % 4 + 1) * P], xg[buf][:, k * P:(k + 1) * P], ident)
                        if k == 3:
                            last.then_inc(sem(f"xT_lo{l}"), 1)
                    last.then_inc(sem(f"xT_hi{l}"), 1)

                def pair(it, last_pair):
                    for u in range(2):
                        e = it * 2 + u
                        n = base + 3 * u
                        pe.wait_ge(sem(f"xgT_v{l}"), at(f"xgT_v{l}", e * 2 + 2))
                        pe.wait_ge(sem(f"act_ready{l}"), at(f"act_ready{l}", e))
                        for q in range(4):
                            j = q // 2
                            pe.wait_ge(sem(f"ex_lo{l}"), at(f"ex_lo{l}", e * 4 + q + 1))
                            k = 4 * (q % 2)
                            for part in quarter[q]:
                                for kk in range(part.shape[1]):
                                    wh, wl = part[:, kk, :], slotk_r[(n + j) % SLOTS][:, k, :]
                                    mm(bank[2 + j][:, :], xg_hi[u][:, k, :], wh, start=k == 0, stop=False)
                                    mm(bank[2 + j][:, :], xg_hi[u][:, k, :], wl, start=False, stop=False)
                                    last = mm(bank[2 + j][:, :], xg_lo[u][:, k, :], wh, start=False, stop=k == KD - 1)
                                    k += 1
                            if q == 0:
                                last.then_inc(sem(f"gate_half{l}"), 1)
                            elif q % 2:
                                last.then_inc(chunks_used, 1)
                        if not (last_pair and u == 1):
                            rows_T(1 - u, it * 16 + 16 * (1 + u), f"xg_loaded{l}_{1 - u}")
                        pe.wait_ge(sem(f"act_ready{l}"), at(f"act_ready{l}", e + 1))
                        for j in range(4):
                            last = tr(bank[4][:, j * P:(j + 1) * P], act_[u][:, j * P:(j + 1) * P], ident)
                        last.then_inc(sem(f"act_tr{l}"), 1)
                        pe.wait_ge(sem(f"actT_ready{l}"), at(f"actT_ready{l}", e + 1))
                        pe.wait_ge(sem(f"y_v{l}"), at(f"y_v{l}", e))
                        pe.wait_ge(sem(f"y_a{l}"), at(f"y_a{l}", e))
                        arrived(pe, n + 2, it)
                        w = slot[(n + 2) % SLOTS].rearrange("p (j n) -> p j n", j=4)
                        for h in range(2):
                            for j in range(4):
                                last = mm(bank[5 + h][:, :], actT[u][:, j, :], w[:, j, h * 512:(h + 1) * 512],
                                          start=j == 0, stop=j == 3)
                            last.then_inc(sem(f"y_mm{l}") if h == 0 else chunks_used, 1)
                pe.wait_ge(sem(f"flag_set{l}"), at(f"flag_set{l}", 1))
                if l == 0:
                    pe.wait_ge(sem("mod1_T"), 1)
                rows_T(0, 16, f"xg_loaded{l}_0")
                pair(0, False)
                with pe.Fori(1, NE // 2 - 1) as it:
                    pair(it, False)
                pair(NE // 2 - 1, True)

                pe.wait_ge(sem(f"flag_set{l}"), at(f"flag_set{l}", 1))
                over = pe.value_load(flag_i[l][0:1, :], min_val=0, max_val=1)
                with pe.If(over > 0):
                    pe.wait_ge(sem(f"y_v{l}"), at(f"y_v{l}", NE))
                    pe.wait_ge(sem(f"y_a{l}"), at(f"y_a{l}", NE))
                    with pe.Fori(0, ROUNDS[l] * NE) as i:
                        loaded, used = sem(f"over_loaded{l}"), sem(f"over_used{l}")
                        pe.wait_ge(sem(f"over_xg{l}"), at(f"over_xg{l}", i * 16 + 16))
                        for k in range(KD):
                            last = tr(bank[k // 4][:, (k % 4) * P:(k % 4 + 1) * P], xg[0][:, k * P:(k + 1) * P], ident)
                        last.then_inc(sem(f"over_xT{l}"), 1)
                        pe.wait_ge(sem(f"over_xgT{l}"), at(f"over_xgT{l}", i * 2 + 2))
                        for j in range(2):
                            pe.wait_ge(loaded, i * 48 + 16 * (j + 1))
                            for k in range(KD):
                                last = mm(bank[2 + j][:, :], xgT[0][:, k, :], over_w[j][:, k, :], start=k == 0, stop=k == KD - 1)
                            last.then_inc(used, 1)
                        pe.wait_ge(sem(f"over_act{l}"), at(f"over_act{l}", i + 1))
                        for j in range(4):
                            last = tr(bank[4][:, j * P:(j + 1) * P], act_[0][:, j * P:(j + 1) * P], ident)
                        last.then_inc(sem(f"over_act_tr{l}"), 1)
                        pe.wait_ge(sem(f"over_actT{l}"), at(f"over_actT{l}", i + 1))
                        pe.wait_ge(loaded, i * 48 + 48)
                        for h in range(2):
                            for j in range(4):
                                last = mm(bank[5 + h][:, :], actT[0][:, j, :], over_w[2][:, j, h * 512:(h + 1) * 512],
                                          start=j == 0, stop=j == 3)
                        last.then_inc(used, 1)
                pe.nop()

            pe.wait_ge(sem("silu_c"), at("silu_c", 1))
            modulation0()
            norm_T(0)
            project(0, E0, EV_CH)
            pe.wait_ge(sem("z_v0"), at("z_v0", 10))
            pe.wait_ge(sem("z_a0"), at("z_a0", 10))

            pe.wait_ge(sem("cn_ready"), at("cn_ready", NT))
            for b in range(5):
                if b == 4:
                    pe.wait_ge(sem("ct_ready"), at("ct_ready", 1))
                for t in range(NT):
                    last = tr(bank[4 + b % 4][:, t * P:(t + 1) * P], z[:, t, b * P:(b + 1) * P], ident)
                last.then_inc(sem("ct_tr"), 1)
            pe.wait_ge(sem("ct_ready"), at("ct_ready", 5))
            pe.wait_ge(sem("krope_done"), at("krope_done", LT))
            for t in range(NT):
                last = mm(bank[5][64:96, t * P:(t + 1) * P], z[:, t, QL + KVL:QL + KVL + RD], ident, start=True, stop=True)
            last.then_inc(sem("kr_mm"), 1)
            uq = slot[U0 % SLOTS][:, 0:3 * 768].rearrange("p (k n) -> p k n", k=3)
            ukv = slot[(U0 + 1) % SLOTS][:, 0:2 * 1024].rearrange("p (k n) -> p k n", k=2)
            arrived(pe, U0)
            for g in range(20):
                if g >= 4:
                    pe.wait_ge(sem(f"lat_{'va'[g % 2]}"), at(f"lat_{'va'[g % 2]}", (g - 4) // 2 + 1))
                if g == MH:
                    arrived(pe, U0 + 1)
                if g < MH:
                    for k in range(3):
                        last = mm(bank[g % 4][0:QD, :], uq[:, k, g * QD:(g + 1) * QD], cT[:, k, :], start=k == 0, stop=k == 2)
                elif g < 2 * MH:
                    h = g - MH
                    for k in range(2):
                        last = mm(bank[g % 4][0:NOPE, :], ukv[:, k, h * P:h * P + NOPE], cT[:, 3 + k, :], start=k == 0, stop=k == 1)
                else:
                    t = g - 2 * MH
                    for k in range(2):
                        last = mm(bank[g % 4][:, :], cT[:, 3 + k, t * P:(t + 1) * P],
                                  ukv[:, k, :].rearrange("p (h c) -> p h c", h=MH)[:, :, NOPE:P], start=k == 0, stop=k == 1)
                last.then_inc(chunks_used if g in (MH - 1, 2 * MH + NT - 1) else sem("lat_mm"), 1)
            pe.wait_ge(sem("lat_v"), at("lat_v", 10))
            pe.wait_ge(sem("lat_a"), at("lat_a", 10))
            pe.wait_ge(sem("kT_rope"), at("kT_rope", 1))
            for i in range(4):
                if i >= 2:
                    pe.wait_ge(sem("qrot_read"), at("qrot_read", i - 1))
                mm(bank[6 + i % 2][64:96, :], const("rot")[64:96, :], qT[64:96, 2 * i:2 * i + 2, 0:SEQ],
                   start=True, stop=True).then_inc(sem("qrot_mm"), 1)
            pe.wait_ge(sem("qT_ready"), at("qT_ready", 4))
            pe.wait_ge(sem("kT_ready"), at("kT_ready", 1))
            attend(0, 0)
            pe.wait_ge(sem("diff_rope"), at("diff_rope", NT))
            pe.wait_ge(sem("o_read0"), at("o_read0", 4))
            sel = slot_r[SEL % SLOTS][:, 2048:4096].rearrange("p (k s j m) -> p k s j m", k=2, s=2, j=4)

            def diff_T(i):
                if i >= 2:
                    pe.wait_ge(sem("split_lo"), i - 1)
                for t in range(NT):
                    o = (ZQ, ZK)[i // 4] + (i % 4) * P
                    last = tr(bank[4 + i % 2][:, t * P:(t + 1) * P], z[:, t, o:o + P], ident)
                last.then_inc(sem("diff_tr"), 1)
            diff_T(0)
            diff_T(1)
            pe.wait_ge(sem("sel_ready"), 1)
            for g in range(32):
                if g % 4 == 0:
                    pe.wait_ge(sem("split_lo"), g // 4 + 1)
                if g >= 4:
                    pe.wait_ge(sem(f"dT_{'va'[g % 2]}"), at(f"dT_{'va'[g % 2]}", (g - 4) // 2 + 1))
                mm(bank[g % 4][:, :], sel[:, g // 16, 0, g % 4, :], d_hi[:, g // 4, :], start=True, stop=False)
                last = mm(bank[g % 4][:, :], sel[:, g // 16, 1, g % 4, :], d_lo[:, g // 4, :], start=False, stop=True)
                last.then_inc(sem("dT_tr"), 1)
                if g % 4 == 3 and g // 4 + 2 < 8:
                    diff_T(g // 4 + 2)
            pe.wait_ge(sem("dT_v"), at("dT_v", 16))
            pe.wait_ge(sem("dT_a"), at("dT_a", 16))
            attend(0, 1)
            attend(0, 2)

            def o_src(l, t, k):
                if l == 1:
                    return zo[:, t, k * P:(k + 1) * P]
                return z[:, t, k * P:(k + 1) * P] if k < 4 else z[:, t, ZQ + (k - 4) * P:ZQ + (k - 3) * P]
            block_T("oT0", [[o_src(0, t, k) for t in range(NT)] for k in range(KD)], [("o_ready0", 8)])
            broadcast("bc0", len(bc_list(0)), True)
            out_project(0, O0)
            experts(0, X0)
            modulation1(1, MB, {})
            norm_T(1)
            pe.wait_ge(sem("mod1_T"), 2)
            project(1, E1, OD_CH)
            pe.wait_ge(sem("z_v1"), at("z_v1", 6))
            pe.wait_ge(sem("z_a1"), at("z_a1", 6))
            modulation1(2, MC_, {})
            pe.wait_ge(sem("mod1_T"), 3)
            block_T("gT", [[zo[:, t, b * P:(b + 1) * P] for t in range(LT)] for b in range(4)] +
                    [[zo[:, t, 768 + b * P:768 + (b + 1) * P] for t in range(LT)] for b in range(4)],
                    [("odd_rope_w", 1), ("odd_rope_d", 1)])
            for g in range(4):
                pe.wait_ge(sem(f"gT_{'va'[g % 2]}"), at(f"gT_{'va'[g % 2]}", 3 + g // 2))
                o = (512 if g < 2 else 1280) + (g % 2) * HD
                for t in range(NT):
                    src = kdup[:, (g * NT + t) * P:(g * NT + t + 1) * P]
                    last = tr(bank[g % 4][:, t * P:(t + 1) * P], src, ident)
                last.then_inc(sem("gk_tr"), 1)
            pe.wait_ge(sem("gk_v"), at("gk_v", 2))
            pe.wait_ge(sem("gk_a"), at("gk_a", 2))
            pe.wait_ge(sem("gT_v"), at("gT_v", 4))
            pe.wait_ge(sem("gT_a"), at("gT_a", 4))
            attend(1, 0)
            block_T("oT1", [[o_src(1, t, k) for t in range(LT)] for k in range(KD)], [("o_ready1", 4)])
            broadcast("bc1", len(bc_list(1)), True)
            out_project(1, O1)
            experts(1, X1)

        @block.vector
        def _(ve):
            V = nc.vector
            done = [0]

            def link(ins):
                done[0] += 1
                ins.then_inc(sem("v_chain"), 1)
                ve.wait_ge(sem("v_chain"), at("v_chain", done[0]))

            sums_n, roots_n = [0], [0]

            def sums_done(ins):
                sums_n[0] += 1
                ins.then_inc(sem("sums_ready"), 1)
                ve.wait_ge(sem("sums_ready"), at("sums_ready", sums_n[0]))

            def rms(out, n, o=0):
                roots_n[0] += 1
                ve.wait_ge(sem("root_ready"), at("root_ready", roots_n[0]))
                link(V.reciprocal(out, roots[:, o:o + n]))

            ve.wait_ge(sem("vec_cols"), at("vec_cols", 1))
            V.tensor_copy(colv[:, 0:53], bank[0][:, 0:53]).then_inc(sem("vec_sb"), 1)
            V.tensor_copy(bmodT, bank[1][:, 0:96]).then_inc(sem("vec_sb"), 1)
            ve.wait_ge(sem("vec_sb"), at("vec_sb", 2))
            link(V.tensor_copy(tokid_i, const("tokid")))
            ve.wait_ge(sem("wide_loaded"), at("wide_loaded", 16 * WIDE_LOADS))
            lq = lam_b.rearrange("p (a b c) -> p a b c", a=2, b=2)
            link(V.tensor_tensor(lq[:, :, 0, :], lq[:, :, 0, :], lq[:, :, 1, :], ALU.mult))
            V.tensor_reduce(lamv[:, 0:2], lq[:, :, 0, :], AX, ALU.add).then_inc(sem("lam_sums"), 1)
            link(V.tensor_scalar(subln_b, subln_b, 1.0 - LAM_INIT, None, ALU.mult))

            def scale_cols(l, section, gain, o):
                for r in range(2):
                    V.scalar_tensor_tensor(scols[l][:, o + 8 * r:o + 8 * r + 8], mod(l, section, r), 1.0,
                                           colv[:, gain + 8 * l:gain + 8 * l + 8], ALU.add, ALU.mult).then_inc(sem(f"scol{l}"), 1)
                ve.wait_ge(sem(f"scol{l}"), at(f"scol{l}", 2 if section == 1 else 4))

            def modulation0():
                mT = modT.rearrange("p (l b r) -> p l b r", l=2, r=2)[:, 0]
                with ve.Fori(0, MODC // SLOTS) as it:
                    def to_T(j):
                        ve.wait_ge(sem("mod_cols"), it * SLOTS + j + 1)
                        c = it * (SLOTS * 4) + 4 * j
                        V.tensor_tensor(mT[:, ds(c, 4), :], bank[2 + j % 2][:, 0:8].rearrange("p (b r) -> p b r", r=2),
                                        bmodT[:, ds(c, 4)].unsqueeze(2).to_broadcast([P, 4, 2]), ALU.add).then_inc(sem("mod_T"), 1)
                    for j in range(SLOTS):
                        ve.wait_ge(chunks_used, it * SLOTS + M0 + j + 1)
                        V.tensor_copy(modrow[j % 2], bank[j % 2][0:2, :]).then_inc(sem("mod_row"), 1)
                        if j > 0:
                            to_T(j - 1)
                    to_T(SLOTS - 1)
                ve.wait_ge(sem("mod_T"), MODC)
                scale_cols(0, 1, C_NM, 0)
                scale_cols(0, 4, C_NF, 16)

            def modulation1(part):
                c0, n = PARTS[part]
                ve.wait_ge(sem("mod1_cols"), c0 + n)
                V.tensor_tensor(modT[:, 96 + 8 * c0:96 + 8 * (c0 + n)].rearrange("p (b r) -> p b r", r=2),
                                bank[0][:, 0:8 * n].rearrange("p (b r) -> p b r", r=2),
                                bmodT[:, 48 + 4 * c0:48 + 4 * (c0 + n)].unsqueeze(2).to_broadcast([P, 4 * n, 2]),
                                ALU.add).then_inc(sem("mod1_T"), 1)
                ve.wait_ge(sem("mod1_T"), part + 1)

            def weight_lo(l, base, chunks, i, half):
                n, w, k = base + i, chunks[i][1], slice(4 * half, 4 * half + 4)
                ve.wait_ge(sem(f"w_hi{l}"), at(f"w_hi{l}", 2 * i + half + 1))
                V.tensor_tensor(slotk_r[n % SLOTS][:, k, 0:w], slotk[n % SLOTS][:, k, 0:w], w_hi[:, k, 0:w].bitcast(f32),
                                ALU.subtract).then_inc(sem(f"w_lo{l}"), 1)

            def norm(l):
                rms(rstd[:, 0:NT], NT)
                for t in range(NT):
                    V.tensor_scalar(xn[:, t, :], xt[:, t, :], rstd[:, t:t + 1], None, ALU.mult).then_inc(sem(f"xn_ready{l}"), 1)
                weight_lo(l, E0 if l == 0 else E1, EV_CH if l == 0 else OD_CH, 0, 0)
                if l == 1:
                    modulation1(1)
                    scale_cols(1, 4, C_NF, 16)
                for k in range(KD):
                    ve.wait_ge(sem(f"xT0_{l}"), at(f"xT0_{l}", k // 2 + 1))
                    V.tensor_scalar(hT[:, k, 0:SEQ], bank[4 + (k // 2) % 2][:, (k % 2) * 256:(k % 2 + 1) * 256],
                                    scols[l][:, k:k + 1], mod(l, 0, 0)[:, k:k + 1], ALU.mult, ALU.add).then_inc(sem(f"hT0_{l}"), 1)
                    if k >= 1:
                        token_lo(l, k - 1)
                token_lo(l, KD - 1)
                weight_lo(l, E0 if l == 0 else E1, EV_CH if l == 0 else OD_CH, 0, 1)

            def token_lo(l, k):
                ve.wait_ge(sem(f"h_part{l}"), at(f"h_part{l}", k + 1))
                V.tensor_tensor(hT_lo[:, k, :], hT[:, k, :], hT_hi[:, k, :].bitcast(f32), ALU.subtract).then_inc(sem(f"h_split{l}"), 1)

            def projected(l, base, chunks, zz):
                g = 0
                for i, (o, w, tiles) in enumerate(chunks):
                    if i + 1 < len(chunks):
                        weight_lo(l, base, chunks, i + 1, 0)
                    for t in range(tiles):
                        if g % 2 == 0:
                            product_done(ve, f"z_mm{l}", base, [c[2] for c in chunks], i, t)
                            V.tensor_copy(zz[:, t, o:o + w], bank[4 * (i % 2) + t][:, 0:w]).then_inc(sem(f"z_v{l}"), 1)
                        g += 1
                    if i + 1 < len(chunks):
                        weight_lo(l, base, chunks, i + 1, 1)

            def rope(src, cos, sin, heads, d, t1, t2):
                q = d // 4
                s4 = src.rearrange("p (h x a q) -> p h x a q", h=heads, x=2, a=2)
                t4 = t1.rearrange("p (h x a q) -> p h x a q", h=heads, x=2, a=2)
                n4 = sin.rearrange("p (x a q) -> p x a q", x=2, a=2)
                for i in range(2):
                    V.tensor_tensor(t4[:, :, :, i, :], s4[:, :, :, 1 - i, :],
                                    n4[:, :, i, :].unsqueeze(1).to_broadcast([P, heads, 2, q]), ALU.mult)\
                     .then_inc(sem("v_rope"), 1)
                    rope_n[0] += 1
                ve.wait_ge(sem("v_rope"), at("v_rope", rope_n[0]))
                s2 = src.rearrange("p (h d) -> p h d", h=heads)
                link(V.tensor_tensor(s2, s2, cos.unsqueeze(1).to_broadcast([P, heads, d]), ALU.mult))
                return V.tensor_tensor(src, src, t1, ALU.add)
            rope_n = [0]

            def attend(l, gi):
                units, b = GROUPS[l][gi], GBASE[l][gi]

                def maxima(u):
                    nk = units[u][2]
                    ve.wait_ge(sem(f"s_ready{l}"), at(f"s_ready{l}", b + u + 1))
                    s = bank[(b + u) % 2]
                    m = nmx[:, (b + u) % 64:(b + u) % 64 + 1]
                    if l == 1 and (u // 2) % 2 == 0:
                        t = u % 2
                        far = s[:, P:2 * P] if t == 0 else s[:, 0:P]
                        link(V.tensor_tensor(far, far, const("wmask")[:, t * P:(t + 1) * P], ALU.add))
                        link(V.tensor_reduce(m, s[:, 0:nk], AX, ALU.max, negate=True))
                        V.tensor_tensor(m, m, nsink[:, u // 4:u // 4 + 1], ALU.min).then_inc(sem(f"max_ready{l}"), 1)
                    else:
                        V.tensor_reduce(m, s[:, 0:nk], AX, ALU.max, negate=True).then_inc(sem(f"max_ready{l}"), 1)
                maxima(0)
                maxima(1)
                for u in range(len(units)):
                    ve.wait_ge(sem(f"t_ready{l}"), at(f"t_ready{l}", b + u + 1))
                    if b + u >= 2:
                        ve.wait_ge(sem(f"pv_done{l}"), at(f"pv_done{l}", b + u - 1))
                    nk = units[u][2]
                    V.tensor_copy(probsT[(b + u) % 2][:, 0:nk], bank[2 + (b + u) % 2][:, 0:nk]).then_inc(sem(f"pT_ready{l}"), 1)
                    if u + 2 < len(units):
                        maxima(u + 2)
                ve.wait_ge(sem(f"pv_done{l}"), at(f"pv_done{l}", b + len(units)))
                ve.wait_ge(sem(f"p_ready{l}"), at(f"p_ready{l}", b + len(units)))

            def heads(ap):
                return ap.rearrange("p (h d) -> p h d", h=8)

            def per_head(v):
                return v.unsqueeze(2).to_broadcast([P, 8, 64])

            def transposed(name, blocks, dst, n):
                for g in range(0, blocks, 2):
                    ve.wait_ge(sem(f"{name}_tr"), at(f"{name}_tr", g + 1))
                    V.tensor_copy(dst(g), bank[g % 4][:, 0:n]).then_inc(sem(f"{name}_v"), 1)

            def broadcast(name, cols):
                def diagonal(i):
                    if i >= 2:
                        ve.wait_ge(sem(f"{name}_mm"), at(f"{name}_mm", i - 1))
                    V.tensor_tensor(diag[i % 2].rearrange("p (k n) -> p k n", k=KD), ident.unsqueeze(1).to_broadcast([P, KD, P]),
                                    cols[i][1].unsqueeze(2).to_broadcast([P, KD, P]), ALU.mult).then_inc(sem(f"{name}_diag"), 1)
                diagonal(0)
                for i in range(len(cols)):
                    if i + 1 < len(cols):
                        diagonal(i + 1)
                    ve.wait_ge(sem(f"{name}_mm"), at(f"{name}_mm", i + 1))
                    V.tensor_copy(bc[cols[i][0]][:, 0:512], bank[4 + 2 * (i % 2)][:, :]).then_inc(sem(f"{name}_v"), 1)
                ve.wait_ge(sem(f"{name}_v"), at(f"{name}_v", len(cols)))
                ve.wait_ge(sem(f"{name}_a"), at(f"{name}_a", len(cols)))

            def out_project(l):
                g = 0
                T = TL[l]

                def token_rows(t):
                    rms(rstd[:, t:t + 1], 1, t)
                    if t >= 2:
                        ve.wait_ge(sem(f"h_hi{l}"), at(f"h_hi{l}", t - 1))
                        ve.wait_ge(sem(f"h_stored{l}_{t % 2}"), at(f"h_stored{l}_{t % 2}", 16 * (t // 2)))
                    link(V.scalar_tensor_tensor(htok[t % 2], xt[:, t, :], rstd[:, t:t + 1], bc[2 + t // LT], ALU.mult, ALU.mult))
                    V.tensor_tensor(htok[t % 2], htok[t % 2], bc[4 + t // LT], ALU.add).then_inc(sem(f"h_ready{l}"), 1)

                def token_cols(t):
                    ve.wait_ge(sem(f"h_lo{l}"), at(f"h_lo{l}", t + 1))
                    V.tensor_copy(hT[:, 0:4, t * P:(t + 1) * P], bank[4 + 2 * (t % 2)][:, :].rearrange("p (k n) -> p k n", k=4))\
                     .then_inc(sem(f"h_v{l}"), 1)
                for i in range(2):
                    for t in range(T):
                        product_done(ve, f"out_mm{l}", O0 if l == 0 else O1, [T, T], i, t)
                        tm = rk[:, (g % 4) * 512:(g % 4 + 1) * 512]
                        ins = V.tensor_tensor(tm, bank[g % 4][:, :], bc[t // LT][:, i * 512:(i + 1) * 512], ALU.mult)
                        ins.then_inc(sem(f"out_v{l}"), 1)
                        g += 1
                        ve.wait_ge(sem(f"out_v{l}"), at(f"out_v{l}", g))
                        xs = xt[:, t, i * 512:(i + 1) * 512]
                        V.tensor_tensor(xs, xs, tm, ALU.add).then_inc(sem(f"x_add{l}"), 1)
                        if i == 1 and t >= 1:
                            token_rows(t - 1)
                            if t >= 3:
                                token_cols(t - 3)
                token_rows(T - 1)
                for t in range(max(0, T - 3), T):
                    token_cols(t)

            def experts(l):
                T = TL[l]
                W = T * NE
                G = T * NG
                s, sel, top, mask, w = r_s[:, 0:W], r_sel[:, 0:W], r_top[:, 0:W], r_mask[:, 0:W], r_w[:, 0:W]
                te = lambda v: v.rearrange("p (t e) -> p t e", e=NE)
                ge = lambda v: v.rearrange("p (g e) -> p g e", e=EG)
                ve.wait_ge(sem(f"sig{l}"), at(f"sig{l}", 1))
                link(V.tensor_tensor(te(sel), te(s), br_sb.unsqueeze(1).to_broadcast([P, T, NE]), ALU.add))

                def outranked(v, groups, n):
                    vv = v.rearrange("p (g e) -> p g e", e=n)
                    by, of = vv.unsqueeze(2).to_broadcast([P, groups, n, n]), vv.unsqueeze(3).to_broadcast([P, groups, n, n])
                    beat = r_beat[:, 0:groups * n * n].rearrange("p (g i j) -> p g i j", i=n, j=n)
                    eq = r_eq[:, 0:groups * n * n].rearrange("p (g i j) -> p g i j", i=n, j=n)
                    V.tensor_tensor(beat, by, of, ALU.is_gt)
                    link(V.tensor_tensor(eq, by, of, ALU.is_equal))
                    eqf = r_eq[:, 0:groups * n * n].rearrange("p (g m) -> p g m", m=n * n)
                    link(V.tensor_tensor(eqf, eqf, const("lower").unsqueeze(1).to_broadcast([P, groups, n * n]), ALU.mult))
                    link(V.tensor_tensor(r_beat[:, 0:groups * n * n], r_beat[:, 0:groups * n * n], r_eq[:, 0:groups * n * n], ALU.add))
                    return beat
                beat = outranked(sel, G, EG)
                link(V.tensor_reduce(top, beat, AX, ALU.add))
                link(V.tensor_scalar(top, top, 1.5, None, ALU.is_lt))
                link(V.tensor_tensor(r_t[:, 0:W], sel, top, ALU.mult))
                link(V.tensor_reduce(r_gs[:, 0:G], ge(r_t[:, 0:W]), AX, ALU.add))
                beat = outranked(r_gs[:, 0:G], T, NG)
                link(V.tensor_reduce(r_gb[:, 0:G], beat, AX, ALU.add))
                link(V.tensor_scalar(r_gb[:, 0:G], r_gb[:, 0:G], 0.5, None, ALU.is_lt))
                V.tensor_tensor(ge(mask), ge(top), r_gb[:, 0:G].unsqueeze(2).to_broadcast([P, G, EG]), ALU.mult)\
                 .then_inc(sem(f"mask{l}"), 1)
                ve.wait_ge(sem(f"mask{l}"), at(f"mask{l}", 1))
                link(V.tensor_tensor(w, s, mask, ALU.mult))
                link(V.tensor_reduce(r_sum[:, 0:T], te(w), AX, ALU.add))
                link(V.reciprocal(r_sum[:, 0:T], r_sum[:, 0:T]))
                link(V.tensor_tensor(te(w), te(w), r_sum[:, 0:T].unsqueeze(2).to_broadcast([P, T, NE]), ALU.mult))
                ve.wait_ge(sem(f"counts{l}"), at(f"counts{l}", 1))
                val = r_val[:, 0:W]
                link(V.tensor_scalar(r_pos[:, 0:W], bank[1][:, 0:W], float(NE), None, ALU.mult))
                link(V.tensor_tensor(te(val), te(r_pos[:, 0:W]), const("eidx").unsqueeze(1).to_broadcast([P, T, NE]), ALU.add))
                link(V.tensor_scalar(r_t[:, 0:W], val, 1.0, None, ALU.add))
                link(V.tensor_tensor(r_t[:, 0:W], r_t[:, 0:W], mask, ALU.mult))
                link(V.tensor_reduce(r_hi[:, 0:T], te(r_t[:, 0:W]), AX, ALU.max))
                link(V.tensor_scalar(r_hi[:, 0:T], r_hi[:, 0:T], -1.0, None, ALU.add))
                link(V.tensor_scalar(r_t[:, 0:W], val, -1.0, float(ROWS), ALU.mult, ALU.add))
                link(V.tensor_tensor(r_t[:, 0:W], r_t[:, 0:W], mask, ALU.mult))
                link(V.tensor_reduce(r_lo[:, 0:T], te(r_t[:, 0:W]), AX, ALU.max))
                link(V.tensor_scalar(r_lo[:, 0:T], r_lo[:, 0:T], -1.0, float(ROWS), ALU.mult, ALU.add))
                V.tensor_copy(idx_hi[:, 0:T], r_hi[:, 0:T]).then_inc(sem(f"idx{l}"), 1)
                V.tensor_copy(idx_lo[:, 0:T], r_lo[:, 0:T]).then_inc(sem(f"idx{l}"), 1)
                link(V.tensor_reduce(r_cnt[:, 0:1], bank[1][:, W:W + NE], AX, ALU.max))
                V.tensor_scalar(flag_i[l], r_cnt[:, 0:1], cap + 0.5, None, ALU.is_gt).then_inc(sem(f"flag_set{l}"), 1)
                for sel_idx, wsel in ((r_hi, r_whi), (r_lo, r_wlo)):
                    link(V.tensor_tensor(te(r_t[:, 0:W]), te(val), sel_idx[:, 0:T].unsqueeze(2).to_broadcast([P, T, NE]), ALU.is_equal))
                    link(V.tensor_tensor(r_t[:, 0:W], r_t[:, 0:W], w, ALU.mult))
                    link(V.tensor_reduce(wsel[:, 0:T], te(r_t[:, 0:W]), AX, ALU.add))

                broadcast(f"gf{l}", gate_list(l))
                if l == 0:
                    modulation1(0)
                    scale_cols(1, 1, C_NM, 0)

                def rows_lo(buf, e):
                    for h in range(2):
                        ve.wait_ge(sem(f"xgT_a{l}"), at(f"xgT_a{l}", e * 2 + h + 1))
                        V.tensor_tensor(xg_lo[buf][:, 4 * h:4 * h + 4, :], bank[h][:, :].rearrange("p (k n) -> p k n", k=4),
                                        xg_hi[buf][:, 4 * h:4 * h + 4, :].bitcast(f32), ALU.subtract).then_inc(sem(f"xgT_v{l}"), 1)

                def quarter_lo(u, e, q):
                    ve.wait_ge(sem(f"ex_hi{l}"), at(f"ex_hi{l}", e * 4 + q + 1))
                    k, s_ = 4 * (q % 2), ((X0 if l == 0 else X1) + 3 * u + q // 2) % SLOTS
                    for part in quarter[q]:
                        n = part.shape[1]
                        ins = V.tensor_tensor(slotk_r[s_][:, k:k + n, :], slotk[s_][:, k:k + n, :], part.bitcast(f32), ALU.subtract)
                        k += n
                    ins.then_inc(sem(f"ex_lo{l}"), 1)

                def pair(it, last_pair):
                    for u in range(2):
                        e = it * 2 + u
                        quarter_lo(u, e, 3)
                        ve.wait_ge(sem(f"silu_ready{l}"), at(f"silu_ready{l}", e + 1))
                        ve.wait_ge(chunks_used, e * 3 + (X0 if l == 0 else X1) + 2)
                        V.tensor_tensor(act_[u], sg[u], bank[3][:, :], ALU.mult).then_inc(sem(f"act_ready{l}"), 1)
                        if not (last_pair and u == 1):
                            rows_lo(1 - u, e + 1)
                            for q in range(3):
                                quarter_lo(1 - u, e + 1, q)
                        ve.wait_ge(sem(f"y_mm{l}"), at(f"y_mm{l}", e + 1))
                        ve.wait_ge(sem(f"y_stored{l}_{u}"), at(f"y_stored{l}_{u}", it * 16))
                        V.tensor_copy(ybuf[u][:, 0:512], bank[5][:, :]).then_inc(sem(f"y_v{l}"), 1)
                for b in range(2):
                    ve.wait_ge(sem(f"h_stored{l}_{b}"), at(f"h_stored{l}_{b}", 8 * T))
                rows_lo(0, 0)
                for q in range(3):
                    quarter_lo(0, 0, q)
                pair(0, False)
                with ve.Fori(1, NE // 2 - 1) as it:
                    pair(it, False)
                pair(NE // 2 - 1, True)

                over = ve.value_load(flag_i[l][0:1, :], min_val=0, max_val=1)
                with ve.If(over > 0):
                    ve.wait_ge(sem(f"y_stored{l}_0"), at(f"y_stored{l}_0", 8 * NE))
                    with ve.Fori(0, ROUNDS[l] * NE) as i:
                        ve.wait_ge(sem(f"over_xT{l}"), at(f"over_xT{l}", i + 1))
                        for h in range(2):
                            V.tensor_copy(xgT[0][:, 4 * h:4 * h + 4, :], bank[h][:, :].rearrange("p (k n) -> p k n", k=4))\
                             .then_inc(sem(f"over_xgT{l}"), 1)
                        ve.wait_ge(sem(f"over_silu{l}"), at(f"over_silu{l}", i + 1))
                        V.tensor_tensor(act_[0], sg[0], bank[3][:, :], ALU.mult).then_inc(sem(f"over_act{l}"), 1)
                        ve.wait_ge(sem(f"over_used{l}"), at(f"over_used{l}", i * 3 + 3))
                        for h in range(2):
                            V.tensor_copy(ybuf[0][:, 512 * h:512 * h + 512], bank[5 + h][:, :]).then_inc(sem(f"over_y{l}"), 1)
                ve.nop()

                for t in range(T):
                    b = t % 2
                    ve.wait_ge(sem(f"ya_loaded{l}_{b}"), at(f"ya_loaded{l}_{b}", 16 * (t // 2 + 1)))
                    ve.wait_ge(sem(f"yb_loaded{l}_{b}"), at(f"yb_loaded{l}_{b}", 16 * (t // 2 + 1)))
                    link(V.tensor_scalar(ya[b], ya[b], r_whi[:, t:t + 1], None, ALU.mult))
                    link(V.scalar_tensor_tensor(ya[b], yb[b], r_wlo[:, t:t + 1], ya[b], ALU.mult, ALU.add))
                    link(V.tensor_tensor(ya[b], ya[b], bc[t // LT], ALU.mult))
                    V.tensor_tensor(xt[:, t, :], xt[:, t, :], ya[b], ALU.add).then_inc(sem(f"x_moe{l}"), 1)

            modulation0()
            norm(0)
            projected(0, E0, EV_CH, z)

            rms(rstd[:, 0:4], 4)
            rms(rstd[:, 4:8], 4, 4)
            for t in range(NT):
                V.tensor_scalar(z[:, t, 0:QL], z[:, t, 0:QL], rstd[:, t:t + 1], None, ALU.mult)
                V.tensor_scalar(z[:, t, QL:QL + KVL], z[:, t, QL:QL + KVL], rstd[:, 4 + t:5 + t], None, ALU.mult)\
                 .then_inc(sem("cn_ready"), 1)
            for t in range(LT):
                rope(z[:, t, QL + KVL:QL + KVL + RD], const("cos32")[:, t * RD:(t + 1) * RD], const("sin32")[:, t * RD:(t + 1) * RD],
                     1, RD, rh[:, 3584 + 32 * t:3616 + 32 * t], None).then_inc(sem("krope_done"), 1)
            ve.wait_ge(sem("kr_mm"), at("kr_mm", 1))
            V.tensor_copy(kT[64:96, 0, :], bank[5][64:96, :]).then_inc(sem("kT_rope"), 1)
            for g in range(0, 20, 2):
                latent_done(ve, g)
                if g < MH:
                    V.tensor_scalar(qT[0:QD, g, :], bank[g % 4][0:QD, :], MLA_SCALE, None, ALU.mult).then_inc(sem("lat_v"), 1)
                elif g < 2 * MH:
                    V.tensor_copy(kT[0:NOPE, g - MH, :], bank[g % 4][0:NOPE, :]).then_inc(sem("lat_v"), 1)
                else:
                    V.tensor_copy(z[:, g - 2 * MH, 0:MH * MV], bank[g % 4][:, :]).then_inc(sem("lat_v"), 1)
            ve.wait_ge(sem("lat_v"), at("lat_v", 10))
            ve.wait_ge(sem("lat_a"), at("lat_a", 10))
            ve.wait_ge(sem("krope_done"), at("krope_done", LT))
            for i in range(4):
                ve.wait_ge(sem("qrot_mm"), at("qrot_mm", i + 1))
                t1 = rh[64:96, 3584:4096].rearrange("p (h n) -> p h n", h=2)
                if i:
                    ve.wait_ge(sem("qT_ready"), at("qT_ready", i))
                V.tensor_tensor(t1, bank[6 + i % 2][64:96, :].rearrange("p (h n) -> p h n", h=2),
                                const("sinT")[64:96, :].unsqueeze(1).to_broadcast([32, 2, SEQ]), ALU.mult).then_inc(sem("qrot_read"), 1)
                ve.wait_ge(sem("qrot_read"), at("qrot_read", i + 1))
                qr = qT[64:96, 2 * i:2 * i + 2, 0:SEQ]
                link(V.tensor_tensor(qr, qr, const("cosT")[64:96, :].unsqueeze(1).to_broadcast([32, 2, SEQ]), ALU.mult))
                V.tensor_tensor(qr, qr, t1, ALU.add).then_inc(sem("qT_ready"), 1)
            ve.wait_ge(sem("lam_exp"), at("lam_exp", 1))
            link(V.tensor_scalar(lamv[:, 3:4], lamv[:, 1:2], -1.0, LAM_INIT, ALU.mult, ALU.add))
            link(V.tensor_tensor(lamv[:, 2:3], lamv[:, 0:1], lamv[:, 3:4], ALU.add))

            attend(0, 0)
            link(V.reciprocal(rinv[:, 0:32], rsum[:, 0:32]))
            arrived(ve, SEL)
            V.tensor_copy(slot_r[SEL % SLOTS][:, 2048:4096], slot[SEL % SLOTS][:, 0:2048]).then_inc(sem("sel_ready"), 1)
            rv = rinv[:, 0:32].rearrange("p (h t) -> p t h", t=NT)
            for t in range(NT):
                V.tensor_tensor(heads(z[:, t, 0:512]), heads(bank[4 + t][:, :]), per_head(rv[:, t, :]), ALU.mult)\
                 .then_inc(sem("o_mla"), 1)
            ve.wait_ge(sem("o_mla"), at("o_mla", NT))
            V.tensor_copy(rstd[:, 0:1], rstd[:, 1:2]).then_inc(sem("o_read0"), 4)

            def low_part(i):
                ve.wait_ge(sem("split_hi"), i + 1)
                V.tensor_tensor(d_lo[:, i, :], bank[4 + i % 2][:, :], d_hi[:, i, :].bitcast(f32), ALU.subtract).then_inc(sem("split_lo"), 1)
            low_part(0)
            low_part(1)
            for g in range(0, 32, 2):
                ve.wait_ge(sem("dT_tr"), at("dT_tr", g + 1))
                V.tensor_copy(dops[g // 16][g % 16], bank[g % 4][:, :]).then_inc(sem("dT_v"), 1)
                if g % 4 == 2 and g // 4 + 2 < 8:
                    low_part(g // 4 + 2)
            for gi in (1, 2):
                attend(0, gi)
                c0 = (gi % 2) * 32
                link(V.reciprocal(rinv[:, c0:c0 + 32], rsum[:, c0:c0 + 32]))
                rv = rinv[:, c0:c0 + 32].rearrange("p (h c i) -> p c i h", c=2, i=2)
                for i in range(2):
                    t = i if gi == 1 else LT + i
                    link(V.tensor_scalar(rv[:, 1, i, :], rv[:, 1, i, :], lamv[:, 2:3], None, ALU.mult))
                    V.tensor_tensor(heads(tmp[0]), heads(bank[4 + i][:, :]), per_head(rv[:, 0, i, :]), ALU.mult)
                    link(V.tensor_tensor(heads(tmp[1]), heads(bank[6 + i][:, :]), per_head(rv[:, 1, i, :]), ALU.mult))
                    ob = z[:, t, ZQ:ZQ + 512]
                    V.tensor_tensor(ob, tmp[0], tmp[1], ALU.subtract).then_inc(sem("o_read0"), 2)
                    ve.wait_ge(sem("o_read0"), at("o_read0", 4 * gi + 2 * (i + 1)))
                    link(V.tensor_tensor(tmp[0], ob, ob, ALU.mult))
                    sums_done(V.tensor_reduce(stat[:, 0:8], heads(tmp[0]), AX, ALU.add))
                    rms(rstd[:, 0:8], 8)
                    link(V.tensor_tensor(heads(ob), heads(ob), per_head(rstd[:, 0:8]), ALU.mult))
                    V.tensor_tensor(heads(ob), heads(ob), subln_b.unsqueeze(1).to_broadcast([P, 8, DV]), ALU.mult)\
                     .then_inc(sem("o_ready0"), 2)
            transposed("oT0", KD, lambda g: oT[:, g, :], NTOK)
            broadcast("bc0", bc_list(0))
            out_project(0)
            experts(0)

            norm(1)
            projected(1, E1, OD_CH, zo)
            ve.wait_ge(sem("z_v1"), at("z_v1", 6))
            ve.wait_ge(sem("z_a1"), at("z_a1", 6))
            t1, t2 = rq[:, 2048:2048 + 640], rq[:, 2688:2688 + 640]
            for t in range(NT):
                h0, nh = (0, 10) if t < LT else (8, 2)
                src = zo[:, t, 768 + 64 * h0:768 + 640]
                n = 64 * nh
                sv = src.rearrange("p (h d) -> p h d", h=nh)
                link(V.tensor_tensor(t1[:, 0:n], src, src, ALU.mult))
                sums_done(V.tensor_reduce(nrm[:, 0:nh], t1[:, 0:n].rearrange("p (h d) -> p h d", h=nh), AX, ALU.add))
                rms(nrm[:, 0:nh], nh)
                link(V.tensor_tensor(sv, sv, nrm[:, 0:nh].unsqueeze(2).to_broadcast([P, nh, HD]), ALU.mult))
                if t < LT:
                    qv = src[:, 0:512].rearrange("p (h d) -> p h d", h=8)
                    link(V.tensor_tensor(qv, qv, qk_b[:, 0:64].unsqueeze(1).to_broadcast([P, 8, HD]), ALU.mult))
                kv = zo[:, t, 1280:1408].rearrange("p (h d) -> p h d", h=2)
                link(V.tensor_tensor(kv, kv, qk_b[:, 64:128].unsqueeze(1).to_broadcast([P, 2, HD]), ALU.mult))
                if t < LT:
                    link(rope(src, const("cos64")[:, t * 64:(t + 1) * 64], const("sin64")[:, t * 64:(t + 1) * 64], 10, 64, t1, t2))
            V.tensor_scalar(nsink, sink_b, -1.0, None, ALU.mult).then_inc(sem("odd_rope_d"), 1)
            ve.wait_ge(sem("odd_rope_d"), at("odd_rope_d", 1))
            modulation1(2)
            for g in range(0, 8, 2):
                ve.wait_ge(sem("gT_tr"), at("gT_tr", g + 1))
                V.tensor_scalar(goT[:, g, :], bank[g % 4][:, 0:SEQ], ATT_SCALE, None, ALU.mult).then_inc(sem("gT_v"), 1)
            for g in (0, 2):
                ve.wait_ge(sem("gk_tr"), at("gk_tr", g + 1))
                V.tensor_copy(gkT[:, g, :], bank[g][:, :]).then_inc(sem("gk_v"), 1)
            attend(1, 0)
            nw = nmx[:, 0:32].rearrange("p (h c) -> p h c", c=4)[:, :, 0:2]
            sk = nsk.rearrange("p (h c) -> p h c", c=2)
            V.tensor_tensor(sk, nw, sink_b.unsqueeze(2).to_broadcast([P, 8, 2]), ALU.add).then_inc(sem("sink_arg"), 1)
            ve.wait_ge(sem("sink_exp"), at("sink_exp", 1))
            rw = rsum[:, 0:32].rearrange("p (h c) -> p h c", c=4)[:, :, 0:2]
            link(V.tensor_tensor(rw, rw, sk, ALU.add))
            link(V.reciprocal(rinv[:, 0:32], rsum[:, 0:32]))
            rv = rinv[:, 0:32].rearrange("p (h c t) -> p c t h", c=2, t=2)
            for c in range(2):
                for t in range(2):
                    V.tensor_tensor(heads(zo[:, t, 512 * c:512 * c + 512]), heads(bank[4 + 2 * c + t][:, :]), per_head(rv[:, c, t, :]),
                                    ALU.mult).then_inc(sem("o_ready1"), 1)
            transposed("oT1", KD, lambda g: oT[:, g, 0:SEQ], SEQ)
            broadcast("bc1", bc_list(1))
            out_project(1)
            experts(1)

            rms(rstd[:, 0:LT], LT)
            ve.wait_ge(sem("nf_loaded"), at("nf_loaded", 16))
            for t in range(LT):
                V.scalar_tensor_tensor(ya[t], xt[:, t, :], rstd[:, t:t + 1], xt[:, LT, :], ALU.mult, ALU.mult)\
                 .then_inc(sem("out_ready"), 1)

        @block.scalar
        def _(ac):
            A = nc.scalar.activation
            ac.wait_ge(sem("zero_list"), at("zero_list", 1))
            for l in range(DEPTH):
                ac.dma_start(list_dram[l].rearrange("(p n) o -> p (n o)", p=P), zeros_i).then_inc(sem("list_zeroed"), 16)
            ac.wait_ge(sem("vec_sb"), at("vec_sb", 2))
            A(silu, colv[:, 0:16], ACT.Silu).then_inc(sem("silu_c"), 1)
            ac.wait_ge(sem("lam_sums"), at("lam_sums", 1))
            A(lamv[:, 0:2], lamv[:, 0:2], ACT.Exp).then_inc(sem("lam_exp"), 1)

            def sumsq(tiles, name, junk, waits):
                for t in range(tiles):
                    s_, v_ = waits(t)
                    ac.wait_ge(sem(s_), at(s_, v_))
                    if t:
                        ac.wait_ge(sem(name), at(name, t))
                    A(junk, xt[:, t, :], ACT.Square, accum_out=stat[:, t:t + 1]).then_inc(sem(name), 1)

            def modulation_rows(part, js, base):
                c0 = PARTS[part][0]
                for j in js:
                    ac.wait_ge(chunks_used, base + j + 1)
                    if c0 + j >= 2:
                        ac.wait_ge(sem("mod1_cols"), c0 + j - 1)
                    A(modrow1[(c0 + j) % 2], bank[2 + j % 2][0:2, :], ACT.Copy).then_inc(sem("mod1_row"), 1)

            def root(sums, n, of, o=0):
                A(roots[:, o:o + n], sums, ACT.Sqrt, scale=1.0 / of, bias=const("eps")).then_inc(sem("root_ready"), 1)

            sums_n = [0]

            def root_of_sums(sums, n, of):
                sums_n[0] += 1
                ac.wait_ge(sem("sums_ready"), at("sums_ready", sums_n[0]))
                root(sums, n, of)

            def weight_hi(l, base, chunks, i, half):
                n, w, k = base + i, chunks[i][1], slice(4 * half, 4 * half + 4)
                arrived(ac, n)
                if i:
                    if half == 0:
                        ac.wait_ge(sem(f"w_half{l}"), at(f"w_half{l}", i))
                    else:
                        ac.wait_ge(chunks_used, base + i)
                A(w_hi[:, k, 0:w], slotk[n % SLOTS][:, k, 0:w], ACT.Copy).then_inc(sem(f"w_hi{l}"), 1)

            def norm(l):
                ac.wait_ge(sem(f"sumsq{l}"), at(f"sumsq{l}", NT))
                root(stat[:, 0:NT], NT, D)
                if l == 0:
                    ac.wait_ge(sem("mod_cols"), MODC)
                for half in range(2):
                    weight_hi(l, E0 if l == 0 else E1, EV_CH if l == 0 else OD_CH, 0, half)
                for k in range(KD):
                    ac.wait_ge(sem(f"xT1_{l}"), at(f"xT1_{l}", k // 2 + 1))
                    ac.wait_ge(sem(f"scol{l}"), at(f"scol{l}", 2))
                    A(hT[:, k, SEQ:NTOK], bank[6 + (k // 2) % 2][:, (k % 2) * 256:(k % 2 + 1) * 256], ACT.Identity,
                      scale=scols[l][:, 8 + k:9 + k], bias=mod(l, 0, 1)[:, k:k + 1]).then_inc(sem(f"hT1_{l}"), 1)
                    ac.wait_ge(sem(f"hT0_{l}"), at(f"hT0_{l}", k + 1))
                    ac.wait_ge(sem(f"hT1_{l}"), at(f"hT1_{l}", k + 1))
                    A(hT_hi[:, k, :], hT[:, k, :], ACT.Copy).then_inc(sem(f"h_part{l}"), 1)

            def projected(l, base, chunks, zz):
                g = 0
                for i, (o, w, tiles) in enumerate(chunks):
                    if i + 1 < len(chunks):
                        weight_hi(l, base, chunks, i + 1, 0)
                    for t in range(tiles):
                        if g % 2 == 1:
                            product_done(ac, f"z_mm{l}", base, [c[2] for c in chunks], i, t)
                            A(zz[:, t, o:o + w], bank[4 * (i % 2) + t][:, 0:w], ACT.Copy).then_inc(sem(f"z_a{l}"), 1)
                        g += 1
                    if i + 1 < len(chunks):
                        weight_hi(l, base, chunks, i + 1, 1)

            def attend(l, gi):
                units, b = GROUPS[l][gi], GBASE[l][gi]
                for u in range(len(units)):
                    n = b + u
                    ac.wait_ge(sem(f"max_ready{l}"), at(f"max_ready{l}", n + 1))
                    if n >= 4:
                        ac.wait_ge(sem(f"t_ready{l}"), at(f"t_ready{l}", n - 3))
                    nk = units[u][2]
                    c = (gi % 2) * 32 + u
                    A(probs[n % 4][:, 0:nk], bank[n % 2][:, 0:nk], ACT.Exp, bias=nmx[:, n % 64:n % 64 + 1],
                      accum_out=rsum[:, c:c + 1]).then_inc(sem(f"p_ready{l}"), 1)

            def transposed(name, blocks, dst, n, scale=1.0):
                for g in range(1, blocks, 2):
                    ac.wait_ge(sem(f"{name}_tr"), at(f"{name}_tr", g + 1))
                    A(dst(g), bank[g % 4][:, 0:n], ACT.Copy, scale=scale).then_inc(sem(f"{name}_a"), 1)

            def broadcast(name, cols):
                for i in range(len(cols)):
                    ac.wait_ge(sem(f"{name}_mm"), at(f"{name}_mm", i + 1))
                    A(bc[cols[i][0]][:, 512:1024], bank[5 + 2 * (i % 2)][:, :], ACT.Copy).then_inc(sem(f"{name}_a"), 1)

            def experts(l):
                T = TL[l]
                def token_cols(t):
                    ac.wait_ge(sem(f"h_hi{l}"), at(f"h_hi{l}", t + 1))
                    A(hT[:, 4:8, t * P:(t + 1) * P], bank[5 + 2 * (t % 2)][:, :].rearrange("p (k n) -> p k n", k=4), ACT.Copy)\
                     .then_inc(sem(f"h_a{l}"), 1)

                def token_store(t):
                    ac.wait_ge(sem(f"h_ready{l}"), at(f"h_ready{l}", t + 1))
                    ac.dma_start(h_dram[l][t * P:(t + 1) * P, :], htok[t % 2]).then_inc(sem(f"h_stored{l}_{t % 2}"), 16)
                for t in range(T):
                    ac.wait_ge(sem(f"x_add{l}"), at(f"x_add{l}", T + t + 1))
                    A(junk, xt[:, t, :], ACT.Square, accum_out=stat[:, t:t + 1]).then_inc(sem(f"sumsq_f{l}"), 1)
                    ac.wait_ge(sem(f"sumsq_f{l}"), at(f"sumsq_f{l}", t + 1))
                    root(stat[:, t:t + 1], 1, D, t)
                    if t >= 1:
                        token_store(t - 1)
                    if t >= 3:
                        token_cols(t - 3)
                for t in range(max(0, T - 3), T):
                    if t == T - 1:
                        token_store(t)
                    token_cols(t)
                ac.wait_ge(sem(f"logits{l}"), at(f"logits{l}", 1))
                A(r_s[:, 0:T * NE], bank[0][:, 0:T * NE], ACT.Sigmoid).then_inc(sem(f"sig{l}"), 1)
                if l == 0:
                    modulation_rows(0, [0, 1], MA)
                broadcast(f"gf{l}", gate_list(l))
                if l == 0:
                    modulation_rows(0, [2, 3], MA)

                def rows_hi(buf, e):
                    for h in range(2):
                        name = ("xT_lo", "xT_hi")[h] + str(l)
                        ac.wait_ge(sem(name), at(name, e + 1))
                        A(xg_hi[buf][:, 4 * h:4 * h + 4, :], bank[h][:, :].rearrange("p (k n) -> p k n", k=4), ACT.Copy)\
                         .then_inc(sem(f"xgT_a{l}"), 1)

                def quarter_hi(u, it, e, q):
                    base = X0 if l == 0 else X1
                    n = base + 3 * u + q // 2
                    if q % 2 == 0:
                        arrived(ac, n, it)
                    if q == 0:
                        ac.wait_ge(chunks_used, e * 3 + base - 1)
                    if q == 3:
                        ac.wait_ge(sem(f"gate_half{l}"), at(f"gate_half{l}", e + 1))
                    k = 4 * (q % 2)
                    for part in quarter[q]:
                        m = part.shape[1]
                        ins = A(part, slotk[n % SLOTS][:, k:k + m, :], ACT.Copy)
                        k += m
                    ins.then_inc(sem(f"ex_hi{l}"), 1)

                def pair(it, last_pair):
                    for u in range(2):
                        e = it * 2 + u
                        quarter_hi(u, it, e, 3)
                        ac.wait_ge(chunks_used, e * 3 + (X0 if l == 0 else X1) + 1)
                        ac.wait_ge(sem(f"act_ready{l}"), at(f"act_ready{l}", e))
                        A(sg[u], bank[2][:, :], ACT.Silu).then_inc(sem(f"silu_ready{l}"), 1)
                        if not (last_pair and u == 1):
                            rows_hi(1 - u, e + 1)
                        ac.wait_ge(sem(f"act_tr{l}"), at(f"act_tr{l}", e + 1))
                        A(actT[u], bank[4][:, :].rearrange("p (j n) -> p j n", j=4), ACT.Copy).then_inc(sem(f"actT_ready{l}"), 1)
                        if not (last_pair and u == 1):
                            for q in range(3):
                                quarter_hi(1 - u, it + u, e + 1, q)
                        ac.wait_ge(chunks_used, e * 3 + (X0 if l == 0 else X1) + 3)
                        ac.wait_ge(sem(f"y_stored{l}_{u}"), at(f"y_stored{l}_{u}", it * 16))
                        A(ybuf[u][:, 512:1024], bank[6][:, :], ACT.Copy).then_inc(sem(f"y_a{l}"), 1)
                        ac.wait_ge(sem(f"y_v{l}"), at(f"y_v{l}", e + 1))
                        ac.wait_ge(sem(f"y_a{l}"), at(f"y_a{l}", e + 1))
                        dst = y_dram[l][0:P * NE, :].rearrange("(s e) d -> s e d", e=NE)
                        if isinstance(e, int):
                            dst = dst[:, e, :]
                        else:
                            dst = dst[:, ds(e, 1), :].rearrange("s e d -> s (e d)")
                        ac.dma_start(dst, ybuf[u]).then_inc(sem(f"y_stored{l}_{u}"), 16)
                rows_hi(0, 0)
                if l == 0:
                    ac.wait_ge(sem("mod1_cols"), PARTS[0][1])
                for q in range(3):
                    quarter_hi(0, 0, 0, q)
                pair(0, False)
                with ac.Fori(1, NE // 2 - 1) as it:
                    pair(it, False)
                pair(NE // 2 - 1, True)

                ac.wait_ge(sem(f"flag_set{l}"), at(f"flag_set{l}", 1))
                over = ac.value_load(flag_i[l][0:1, :], min_val=0, max_val=1)
                with ac.If(over > 0):
                    with ac.Fori(0, ROUNDS[l]) as r:
                        with ac.Fori(0, NE) as e:
                            i = r * NE + e
                            ac.wait_ge(sem(f"over_used{l}"), at(f"over_used{l}", i * 3 + 2))
                            A(sg[0], bank[2][:, :], ACT.Silu).then_inc(sem(f"over_silu{l}"), 1)
                            ac.wait_ge(sem(f"over_act_tr{l}"), at(f"over_act_tr{l}", i + 1))
                            A(actT[0], bank[4][:, :].rearrange("p (j n) -> p j n", j=4), ACT.Copy).then_inc(sem(f"over_actT{l}"), 1)
                            ac.wait_ge(sem(f"over_y{l}"), at(f"over_y{l}", i * 2 + 2))
                            dst = y_dram[l][ds(r * (P * NE) + P * NE, P * NE), :].rearrange("(s e) d -> s e d", e=NE)
                            ac.dma_start(dst[:, ds(e, 1), :].rearrange("s e d -> s (e d)"), ybuf[0]).then_inc(sem(f"over_stored{l}"), 16)
                ac.nop()

            ac.wait_ge(sem("x_loaded"), at("x_loaded", 32))
            sumsq(NT, "sumsq0", rh[:, 0:D], lambda t: ("x_loaded", 32))
            norm(0)
            projected(0, E0, EV_CH, z)
            ac.wait_ge(chunks_used, U0)
            ac.wait_ge(sem("z_v0"), at("z_v0", 10))
            ac.wait_ge(sem("z_a0"), at("z_a0", 10))
            for t in range(NT):
                if t:
                    ac.wait_ge(sem("lat_sums"), at("lat_sums", 2 * t))
                A(rh[:, 0:QL], z[:, t, 0:QL], ACT.Square, accum_out=stat[:, t:t + 1]).then_inc(sem("lat_sums"), 1)
                A(rh[:, QL:QL + KVL], z[:, t, QL:QL + KVL], ACT.Square, accum_out=stat[:, 4 + t:5 + t]).then_inc(sem("lat_sums"), 1)
            ac.wait_ge(sem("lat_sums"), at("lat_sums", 2 * NT))
            root(stat[:, 0:4], 4, QL)
            A(roots[:, 4:8], stat[:, 4:8], ACT.Sqrt, scale=1.0 / KVL, bias=const("eps")).then_inc(sem("root_ready"), 1)
            for b in range(5):
                ac.wait_ge(sem("ct_tr"), at("ct_tr", b + 1))
                A(cT[:, b, :], bank[4 + b % 4][:, :], ACT.Copy, scale=colv[:, C_NQ + b:C_NQ + b + 1]).then_inc(sem("ct_ready"), 1)
            for g in range(1, 20, 2):
                latent_done(ac, g)
                if g < MH:
                    ins = A(qT[0:QD, g, :], bank[g % 4][0:QD, :], ACT.Copy, scale=MLA_SCALE)
                elif g < 2 * MH:
                    ins = A(kT[0:NOPE, g - MH, :], bank[g % 4][0:NOPE, :], ACT.Copy)
                else:
                    ins = A(z[:, g - 2 * MH, 0:MH * MV], bank[g % 4][:, :], ACT.Copy)
                ins.then_inc(sem("lat_a"), 1)
            attend(0, 0)

            def high_part(i):
                ac.wait_ge(sem("diff_tr"), i + 1)
                A(d_hi[:, i, :], bank[4 + i % 2][:, :], ACT.Copy).then_inc(sem("split_hi"), 1)
            high_part(0)
            high_part(1)
            for g in range(1, 32, 2):
                ac.wait_ge(sem("dT_tr"), at("dT_tr", g + 1))
                A(dops[g // 16][g % 16], bank[g % 4][:, :], ACT.Copy).then_inc(sem("dT_a"), 1)
                if g % 4 == 3 and g // 4 + 2 < 8:
                    high_part(g // 4 + 2)
            for gi in (1, 2):
                attend(0, gi)
                for i in range(2):
                    root_of_sums(stat[:, 0:8], 8, DV)
            transposed("oT0", KD, lambda g: oT[:, g, :], NTOK)
            broadcast("bc0", bc_list(0))
            experts(0)
            modulation_rows(1, [0, 1, 2, 3], MB)
            for t in range(NT):
                ac.wait_ge(sem("x_moe0"), at("x_moe0", t + 1))
                if t:
                    ac.wait_ge(sem("sumsq1"), at("sumsq1", t))
                A(rh[:, 0:D], xt[:, t, :], ACT.Square, accum_out=stat[:, t:t + 1]).then_inc(sem("sumsq1"), 1)
                if t < 2:
                    modulation_rows(1, [4 + t], MB)
            norm(1)
            projected(1, E1, OD_CH, zo)
            for t in range(NT):
                if t >= 2:
                    modulation_rows(2, [t - 2], MC_)
                root_of_sums(nrm[:, 0:10 if t < LT else 2], 10 if t < LT else 2, HD)
            transposed("gT", 8, lambda g: goT[:, g, :], SEQ, ATT_SCALE)
            for g in (1, 3):
                ac.wait_ge(sem("gk_tr"), at("gk_tr", g + 1))
                A(gkT[:, g, :], bank[g][:, :], ACT.Copy).then_inc(sem("gk_a"), 1)
            attend(1, 0)
            ac.wait_ge(sem("sink_arg"), at("sink_arg", 1))
            A(nsk, nsk, ACT.Exp).then_inc(sem("sink_exp"), 1)
            transposed("oT1", KD, lambda g: oT[:, g, 0:SEQ], SEQ)
            broadcast("bc1", bc_list(1))
            experts(1)
            sumsq(LT, "sumsq_out", rh[:, 0:D], lambda t: ("x_moe1", t + 1))
            ac.wait_ge(sem("sumsq_out"), at("sumsq_out", LT))
            root(stat[:, 0:LT], LT, D)
            for t in range(LT):
                ac.wait_ge(sem("out_ready"), at("out_ready", t + 1))
                ac.dma_start(out_dram[0, t * P:(t + 1) * P, :], ya[t]).then_inc(sem("out_stored"), 16)
            ac.wait_ge(sem("out_stored"), at("out_stored", 16 * LT))

        @block.gpsimd
        def _(gp):
            G = nc.gpsimd
            n_done = [0]

            def link(ins):
                n_done[0] += 1
                ins.then_inc(sem("g_chain"), 1)
                gp.wait_ge(sem("g_chain"), at("g_chain", n_done[0]))
            G.memset(zeros_i, 0).then_inc(sem("zero_list"), 1)

            def rope(src, cos, sin, heads, d, t1):
                q = d // 4
                s4 = src.rearrange("p (h x a q) -> p h x a q", h=heads, x=2, a=2)
                t4 = t1.rearrange("p (h x a q) -> p h x a q", h=heads, x=2, a=2)
                n4 = sin.rearrange("p (x a q) -> p x a q", x=2, a=2)
                for i in range(2):
                    link(G.tensor_tensor(t4[:, :, :, i, :], s4[:, :, :, 1 - i, :],
                                         n4[:, :, i, :].unsqueeze(1).to_broadcast([P, heads, 2, q]), ALU.mult))
                s2 = src.rearrange("p (h d) -> p h d", h=heads)
                link(G.tensor_tensor(s2, s2, cos.unsqueeze(1).to_broadcast([P, heads, d]), ALU.mult))
                return G.tensor_tensor(src, src, t1, ALU.add)

            def experts(l):
                T = TL[l]
                gp.wait_ge(sem(f"idx{l}"), at(f"idx{l}", 2))
                gp.wait_ge(sem("list_zeroed"), at("list_zeroed", 32))
                for t in range(T):
                    for idx in (idx_hi, idx_lo):
                        gp.indirect_dma_start(out=list_dram[l], out_offset=bass.IndirectOffsetOnAxis(idx[:, t:t + 1], 0),
                                              in_=tokid_i[:, t:t + 1], in_offset=None).then_inc(sem(f"listed{l}"), 16)
                gp.wait_ge(sem(f"listed{l}"), at(f"listed{l}", 32 * T))
                gp.dma_start(slots_i, list_dram[l][0:P * NE, :].rearrange("(s e) o -> s (e o)", e=NE)).then_inc(sem(f"slots{l}"), 16)
                gp.wait_ge(sem(f"slots{l}"), at(f"slots{l}", 16))
                for b in range(2):
                    gp.wait_ge(sem(f"h_stored{l}_{b}"), at(f"h_stored{l}_{b}", 8 * T))
                for e in range(NE):
                    if e >= 2:
                        gp.wait_ge(sem(f"xT_hi{l}"), at(f"xT_hi{l}", e - 1))
                    gp.indirect_dma_start(out=xg[e % 2], out_offset=None, in_=h_dram[l],
                                          in_offset=bass.IndirectOffsetOnAxis(slots_i[:, e:e + 1], 0)).then_inc(sem(f"xg_loaded{l}_{e % 2}"), 16)
                over = gp.value_load(flag_i[l][0:1, :], min_val=0, max_val=1)
                with gp.If(over > 0):
                    gp.wait_ge(sem(f"xT_hi{l}"), at(f"xT_hi{l}", NE))
                    for i in range(ROUNDS[l] * NE):
                        r, e = i // NE + 1, i % NE
                        if i:
                            gp.wait_ge(sem(f"over_stored{l}"), at(f"over_stored{l}", 16 * i))
                        if e == 0:
                            gp.dma_start(slots_i, list_dram[l][r * P * NE:(r + 1) * P * NE, :].rearrange("(s e) o -> s (e o)", e=NE))\
                              .then_inc(sem(f"over_idx{l}"), 16)
                            gp.wait_ge(sem(f"over_idx{l}"), at(f"over_idx{l}", 16 * r))
                        gp.indirect_dma_start(out=xg[0], out_offset=None, in_=h_dram[l],
                                              in_offset=bass.IndirectOffsetOnAxis(slots_i[:, e:e + 1], 0)).then_inc(sem(f"over_xg{l}"), 16)
                    gp.wait_ge(sem(f"over_stored{l}"), at(f"over_stored{l}", 16 * ROUNDS[l] * NE))
                gp.nop()
                for b in range(2):
                    gp.wait_ge(sem(f"y_stored{l}_{b}"), at(f"y_stored{l}_{b}", 8 * NE))

                def result_rows(rows):
                    for t in range(T):
                        if t >= 2:
                            gp.wait_ge(sem(f"x_moe{l}"), at(f"x_moe{l}", t - 1))
                        for buf, idx, name in ((ya, idx_hi, "ya"), (yb, idx_lo, "yb")):
                            gp.indirect_dma_start(out=buf[t % 2], out_offset=None, in_=rows,
                                                  in_offset=bass.IndirectOffsetOnAxis(idx[:, t:t + 1], 0))\
                              .then_inc(sem(f"{name}_loaded{l}_{t % 2}"), 16)
                with gp.If(over > 0):
                    result_rows(y_dram[l])
                gp.nop()
                with gp.If(over < 1):
                    result_rows(y_dram[l][0:P * NE, :])
                gp.nop()

            gp.wait_ge(chunks_used, U0)
            gp.wait_ge(sem("z_v0"), at("z_v0", 10))
            gp.wait_ge(sem("z_a0"), at("z_a0", 10))
            gp.wait_ge(sem("small_loaded"), at("small_loaded", 16 * SMALL_LOADS))
            for t in range(LT):
                ins = rope(z[:, t, ZQ:ZQ + 1024], const("cos32")[:, t * RD:(t + 1) * RD], const("sin32")[:, t * RD:(t + 1) * RD],
                           32, 32, rh[:, 2560:3584])
                link(ins)
            for t in range(NT):
                G.tensor_scalar(z[:, t, ZQ:ZQ + 512], z[:, t, ZQ:ZQ + 512], DIFF_SCALE, None, ALU.mult)\
                 .then_inc(sem("diff_rope"), 1)
            gp.wait_ge(sem("kT_rope"), at("kT_rope", 1))
            gp.wait_ge(sem("diff_rope"), at("diff_rope", NT))
            G.tensor_copy(kT[64:96, 1:MH, :], kT[64:96, 0:1, :].to_broadcast([32, MH - 1, NTOK])).then_inc(sem("kT_ready"), 1)
            experts(0)
            gp.wait_ge(sem("z_v1"), at("z_v1", 6))
            gp.wait_ge(sem("z_a1"), at("z_a1", 6))
            for t in range(LT):
                ins = rope(zo[:, t, 0:640], const("cos64")[:, t * 64:(t + 1) * 64], const("sin64")[:, t * 64:(t + 1) * 64],
                           10, 64, rq[:, 3328:3968])
                link(ins)
            gp.wait_ge(sem("odd_rope_d"), at("odd_rope_d", 1))
            for g in range(4):
                o = (512 if g < 2 else 1280) + (g % 2) * HD
                for t in range(NT):
                    kd = kdup[:, (g * NT + t) * P:(g * NT + t + 1) * P].rearrange("p (c d) -> p c d", c=2)
                    ins = G.tensor_copy(kd, zo[:, t, o:o + HD].unsqueeze(1).to_broadcast([P, 2, HD]))
            ins.then_inc(sem("odd_rope_w"), 1)
            experts(1)


_INS = ["x", "c", "ctx", "c_ctx", "w_mod", "b_mod", "norm_mix", "norm_ffn", "even_w_in", "even_norm_q", "even_norm_kv",
        "even_w_uq", "even_w_ukv", "even_lambda", "even_subln", "even_w_out", "odd_w_in", "odd_sink", "odd_q_norm",
        "odd_k_norm", "odd_w_out", "w_router", "b_router", "w_gate", "w_up", "w_down", "norm_final"]


def kernel(**inputs):
    import concourse.bacc as bacc
    from concourse.bass_utils import run_bass_kernel_spmd

    nc = bacc.Bacc("TRN2", target_bir_lowering=False, num_devices=1)
    arrays = {f"in_{n}": np.ascontiguousarray(inputs[n]) for n in _INS}
    arrays["shape_consts"] = shape_constants()
    aps = {n: nc.dram_tensor(n, v.shape, mybir.dt.from_np(v.dtype), kind="ExternalInput").ap() for n, v in arrays.items()}
    out = nc.dram_tensor("out", (1, SEQ, D), mybir.dt.float32, kind="ExternalOutput").ap()
    build(nc, {n: aps[f"in_{n}"] for n in _INS}, aps["shape_consts"], out)
    r = run_bass_kernel_spmd(nc, [arrays], core_ids=[0])
    return r.results[0]["out"]
```

```python
import math
from contextlib import ExitStack

import numpy as np

import concourse.bass as bass
from concourse import mybir

P = 128
D = 1024
KD = D // P
SEQ, CTX = 256, 256
NT = (SEQ + CTX) // P
LT = SEQ // P
NTOK = SEQ + CTX
DEPTH = 2
GRID_W = 64
EPS = 1e-6
CH = 512
SLOTS = 6
SLOT = KD * CH
MODC = 6 * D // CH
PARTS = [(0, 4), (4, 6), (10, 2)]
QL, KVL, RD, NOPE, MV, MH = 384, 256, 32, 64, 64, 8
QD = NOPE + RD
DH, DD, DV = 8, 32, 64
EV_IN = QL + KVL + RD + 2 * DH * 2 * DD + DH * DV
EV_CH = [(0, QL, NT), (QL, KVL + RD, NT), (672, 512, NT), (1184, 512, NT), (1696, 512, NT)]
ZQ, ZK, ZV = 672, 1184, 1696
HD = 64
OD_IN = 1536
OD_CH = [(0, 512, LT), (512, 256, NT), (768, 512, LT), (1280, 256, NT)]
LAM_INIT = 0.8 - 0.6 * math.exp(-0.3 * 0)
MLA_SCALE, DIFF_SCALE, ATT_SCALE = QD ** -0.5, DD ** -0.5, HD ** -0.5
NE, NG, EG, FF = 16, 4, 4, 512
TL = [NT, LT]
ROUNDS = [t - 1 for t in TL]
ROWS = NTOK * NE

CONSTS = [("ident", P), ("ones", P), ("tri", P), ("cos32", LT * 32), ("sin32", LT * 32),
          ("cosT", SEQ), ("sinT", SEQ), ("rot", 32),
          ("cos64", LT * 64), ("sin64", LT * 64), ("wmask", 2 * P), ("lower", EG * EG),
          ("eidx", NE), ("tokid", NT), ("eps", 1)]


def shape_constants():
    c = {}
    p = np.arange(P)
    c["ident"] = np.eye(P)
    c["ones"] = np.ones((P, P))
    c["tri"] = (p[:, None] < p[None, :])
    t = np.arange(SEQ)

    def tables(rot):
        half = rot // 2
        inv = (np.float32(10000.0) ** (-np.arange(0, half, 2, dtype=np.float32) / np.float32(half))).astype(np.float32)
        cos, sin = [], []
        for pos in (t // GRID_W, t % GRID_W):
            ang = pos.astype(np.float32)[:, None] * inv[None, :]
            cos += [np.cos(ang), np.cos(ang)]
            sin += [-np.sin(ang), np.sin(ang)]
        return np.concatenate(cos, 1), np.concatenate(sin, 1)
    for rot in (32, 64):
        cos, sin = tables(rot)
        c[f"cos{rot}"] = cos.reshape(LT, P, rot).transpose(1, 0, 2).reshape(P, -1)
        c[f"sin{rot}"] = sin.reshape(LT, P, rot).transpose(1, 0, 2).reshape(P, -1)
    cos, sin = tables(32)
    tall = np.zeros((P, SEQ)); tall[64:96] = cos.T; c["cosT"] = tall
    tall = np.zeros((P, SEQ)); tall[64:96] = sin.T; c["sinT"] = tall
    rot = np.zeros((P, 32))
    for m in range(32):
        rot[64 + (m // 16) * 16 + (m % 16 + 8) % 16, m] = 1.0
    c["rot"] = rot
    far = np.zeros((P, 2, P))
    far[:, 0][p[None, :] > p[:, None]] = -1e30
    far[:, 1][p[None, :] < p[:, None]] = -1e30
    c["wmask"] = far.reshape(P, -1)
    i = np.arange(EG)
    c["lower"] = np.broadcast_to((i[None, :] < i[:, None]).reshape(1, -1), (P, EG * EG))
    c["eidx"] = np.broadcast_to(np.arange(NE)[None], (P, NE))
    c["tokid"] = p[:, None] + P * np.arange(NT)[None, :]
    c["eps"] = np.full((P, 1), EPS)
    sel = np.zeros((P, 2, 2, 4, P))
    for kind, rows in enumerate(((0, 0, 1, 1), (0, 1, 0, 1))):
        for q, part in enumerate(rows):
            for j in range(4):
                for i in range(32):
                    sel[32 * j + i, kind, part, j, 32 * q + i] = 1.0
    return np.concatenate([np.asarray(c[n], np.float32).reshape(P, w) for n, w in CONSTS] +
                          [sel.reshape(P, 2048).astype(np.float32)], 1)


def build(nc, a, consts_dram, out_dram, dbg=None, cap=P):
    f32, i32, f32r = mybir.dt.float32, mybir.dt.int32, mybir.dt.float32r
    ALU = mybir.AluOpType
    ACT = mybir.ActivationFunctionType
    AX = mybir.AxisListType.X
    ds = bass.ds
    ctx = ExitStack()
    layer0_total = {
        "scol{}": 4, "sumsq{}": NT, "xn_ready{}": NT,
        "xT0_{}": KD // 2, "xT1_{}": KD // 2, "hT0_{}": KD, "hT1_{}": KD,
        "h_part{}": KD, "h_split{}": KD, "w_half{}": len(EV_CH), "w_hi{}": 2 * len(EV_CH), "w_lo{}": 2 * len(EV_CH),
        "z_v{}": 10, "z_a{}": 10, "z_mm{}": len(EV_CH) * (NT - 1),
        "s_ready{}": 96, "max_ready{}": 96, "p_ready{}": 96, "t_ready{}": 96, "pT_ready{}": 96, "pv_done{}": 96,
        "out_mm{}": 2 * (NT - 1), "out_v{}": 2 * NT, "x_add{}": 2 * NT,
        "sumsq_f{}": NT, "h_ready{}": NT, "h_stored{}_0": 8 * NT, "h_stored{}_1": 8 * NT,
        "h_lo{}": NT, "h_hi{}": NT, "h_v{}": NT, "h_a{}": NT,
        "logits{}": 1, "sig{}": 1, "mask{}": 1, "counts{}": 1, "idx{}": 2, "flag_set{}": 1, "listed{}": 32 * NT + 16, "slots{}": 32,
        "xg_loaded{}_0": 8 * NE + 16, "xg_loaded{}_1": 8 * NE + 16, "xT_lo{}": NE, "xT_hi{}": NE, "xgT_v{}": 2 * NE, "xgT_a{}": 2 * NE,
        "ex_hi{}": 4 * NE, "ex_lo{}": 4 * NE, "gate_half{}": NE,
        "silu_ready{}": NE, "act_ready{}": NE, "act_tr{}": NE, "actT_ready{}": NE, "y_mm{}": NE, "y_v{}": NE, "y_a{}": NE,
        "y_stored{}_0": 8 * NE, "y_stored{}_1": 8 * NE,
        "ya_loaded{}_0": 16, "ya_loaded{}_1": 16, "yb_loaded{}_0": 16, "yb_loaded{}_1": 16, "y_sum{}": NT, "x_moe{}": NT,
    }
    sems, alias = {}, {}
    for n, total in layer0_total.items():
        for l in range(DEPTH):
            alias[n.format(l)] = (n.format(""), l * total)
    for kind, stages in (("blocks", [("dT", 32), ("oT0", 8), ("g_q", 8), ("oT1", 8)]),
                         ("rows", [("bc0", 6), ("gf0", 2), ("bc1", 3), ("gf1", 1)])):
        at = 0
        for n, count in stages:
            for part, share in ((("tr", 1), ("v", 2), ("a", 2)) if kind == "blocks" else
                                (("mm", 1), ("v", 1), ("a", 1))):
                alias[f"{n}_{part}"] = (f"{kind}_{part}", at // share)
            at += count

    for n, of, seen in (("ya_loaded0_2", "xg_loaded_0", 8 * NE), ("yb_loaded0_2", "xg_loaded_1", 8 * NE),
                        ("ya_loaded0_3", "listed", 32 * NT), ("yb_loaded0_3", "slots", 16)):
        alias[n] = (of, seen)
    for part in ("tr", "hi", "lo"):
        for n, at_ in ((("diff_tr" if part == "tr" else f"split_{part}"), 0), (f"gx_{part}", 8), (f"gk_{part}", 16)):
            alias[n] = (f"parts_{part}", at_)

    def sem(name):
        n = alias.get(name, (name, 0))[0]
        if n not in sems:
            sems[n] = ctx.enter_context(nc.semaphore(n))
        return sems[n]

    def at(name, value):
        return value + alias.get(name, (name, 0))[1]

    def sb(name, shape, dt=f32):
        return ctx.enter_context(nc.sbuf_tensor(name, shape, dt))

    h_dram = [nc.dram_tensor(f"h_rows{l}", [(NT if l == 0 else LT) * P, D], f32).ap() for l in range(DEPTH)]
    list_dram = [nc.dram_tensor(f"slot_list{l}", [ROWS, 1], i32).ap() for l in range(DEPTH)]
    y_dram = [nc.dram_tensor(f"y_rows{l}", [TL[l] * P * NE, D], f32).ap() for l in range(DEPTH)]

    with ctx:
        with ExitStack() as first_names:
            def named(name, cols):
                return first_names.enter_context(nc.sbuf_tensor(name, [P, cols], f32))
            ring = [named(f"ring{i}", SLOT) for i in range(SLOTS)]
            rq, rk, rh, rz = (named(f"region_{n}", cols) for n, cols in (("q", 4096), ("k", 4096), ("h", 4096), ("z", NT * EV_IN)))
        ring_r = [sb(f"ring{i}_r", [P, SLOT], f32r) for i in range(SLOTS)]
        rq_r = sb("region_q_r", [P, 4096], f32r)
        rk_r = sb("region_k_r", [P, 4096], f32r)
        rh_r = sb("region_h_r", [P, 4096], f32r)
        rz_r = sb("region_z_r", [P, NT * EV_IN], f32r)
        sel64 = sb("sel64", [P, 6 * 64], f32r)
        x = sb("x", [P, NT * D])
        NCON = sum(w for _, w in CONSTS)
        con = sb("con", [P, NCON])
        small = sb("small", [P, 1307])
        small_i = sb("small_i", [P, 96], i32)
        bank = [ctx.enter_context(nc.psum_tensor(f"bank{i}", [P, 512], f32)) for i in range(8)]

        off = {}
        o = 0
        for n, w in CONSTS:
            off[n] = (o, w)
            o += w

        def const(n):
            return con[:, off[n][0]:off[n][0] + off[n][1]]
        so = [0]

        def sm(w):
            so[0] += w
            assert so[0] <= 1307, so[0]
            return small[:, so[0] - w:so[0]]
        ident, ones, tri = const("ident"), const("ones"), const("tri")
        colv = sm(56)
        C_C, C_NM, C_NF, C_NQ, C_NKV = 0, 16, 32, 48, 51
        bmodT = sm(96)
        modT = sm(2 * 96)
        silu = sm(16)
        scols = [sm(32), sm(32)]
        stat = sm(16)
        rstd = sm(16)
        lamv = sm(4)
        nsink, nsk, nrm = sm(8), sm(16), sm(10)
        nmx = sm(64)
        roots = sm(18)
        rsum = sm(64)
        rinv = sm(64)
        tokid_i = small_i[:, 0:4]
        idx_hi = small_i[:, 4:8]
        idx_lo = small_i[:, 8:12]
        slots_i = small_i[:, 12:28]
        zeros_i = small_i[:, 32:96]
        kdup = rh[:, 0:2048]
        flag_i = [small_i[:, 30 + l:31 + l] for l in range(DEPTH)]

        def mod(l, s, r):
            return modT.rearrange("p (l s k r) -> p l s k r", l=2, s=6, r=2)[:, l, s, :, r]
        xt = x[:, :].rearrange("p (t d) -> p t d", t=NT)
        hT = rh[:, :].rearrange("p (k n) -> p k n", k=KD)
        xn = rz[:, 2 * D:6 * D].rearrange("p (t d) -> p t d", t=NT)
        slot = [r[:, :] for r in ring]
        slotk = [s.rearrange("p (k n) -> p k n", k=KD) for s in slot]
        bc = [rz[:, i * D:(i + 1) * D] for i in range(6)]

        modrow = [rk[0:2, i * CH:(i + 1) * CH] for i in range(2)]
        z = rz[:, :].rearrange("p (t n) -> p t n", t=NT)
        zo = rz[:, 0:NT * OD_IN].rearrange("p (t n) -> p t n", t=NT)
        cT = hT
        qT = rq[:, :].rearrange("p (h n) -> p h n", h=MH)
        kT = rk[:, :].rearrange("p (h n) -> p h n", h=MH)
        probs = [rh[:, i * 512:(i + 1) * 512] for i in range(4)]
        probsT = [rh[:, (4 + i) * 512:(5 + i) * 512] for i in range(2)]
        tmp = [rh[:, (6 + i) * 512:(7 + i) * 512] for i in range(2)]
        d_hi, d_lo = (r[:, :].rearrange("p (b n) -> p b n", b=8) for r in (rq_r, rk_r))
        hT_hi, hT_lo = (r[:, :].rearrange("p (k n) -> p k n", k=KD) for r in (rq_r, rh_r))
        w_hi = rk_r[:, :].rearrange("p (k n) -> p k n", k=KD)
        slot_r = [r[:, :] for r in ring_r]
        oT = rq[:, :].rearrange("p (k n) -> p k n", k=KD)
        g_q = rq_r[:, :].rearrange("p (h n) -> p h n", h=16)
        g_k = [[rk_r[:, g * 2 * NTOK + part * NTOK:g * 2 * NTOK + (part + 1) * NTOK] for part in range(2)] for g in range(4)]
        gx_hi, gx_lo = (r.rearrange("p (b n) -> p b n", b=8) for r in (rh_r[:, 2048:4096], rz_r[:, NT * OD_IN:NT * OD_IN + 2048]))
        htok = [rk[:, (2 + i) * D:(3 + i) * D] for i in range(2)]
        junk = rz[:, 6 * D:7 * D]
        modrow1 = [rz[0:2, 8832 - (2 - i) * CH:8832 - (1 - i) * CH] for i in range(2)]
        xg = [rk[:, i * D:(i + 1) * D] for i in range(2)]
        ybuf = [rk[:, (2 + i) * D:(3 + i) * D] for i in range(2)]
        xgT = [rq[:, i * D:(i + 1) * D].rearrange("p (k n) -> p k n", k=KD) for i in range(2)]
        sg = [rh[:, i * 512:(i + 1) * 512] for i in range(2)]
        act_ = [rh[:, (2 + i) * 512:(3 + i) * 512] for i in range(2)]
        actT = [rh[:, (4 + i) * 512:(5 + i) * 512].rearrange("p (j n) -> p j n", j=4) for i in range(2)]
        ya = [r[:, i * D:(i + 1) * D] for r in (rq, rk) for i in range(2)]
        yb = [r[:, (2 + i) * D:(3 + i) * D] for r in (rq, rk) for i in range(2)]
        ow = rz[:, 2 * D:2 * D + 4096]
        over_w = [ow.rearrange("p (k n) -> p k n", k=KD), ow.rearrange("p (k n) -> p k n", k=KD),
                  ow.rearrange("p (k n) -> p k n", k=4)]
        xg_hi, xg_lo = ([rq_r[:, (2 * j + i) * D:(2 * j + i + 1) * D].rearrange("p (k n) -> p k n", k=KD) for i in range(2)]
                        for j in range(2))

        def blocks_of(region, o, n):
            return region[:, o:o + n * CH].rearrange("p (k n) -> p k n", k=n)
        quarter = [[blocks_of(rz_r, 2 * D, 4)], [blocks_of(rz_r, 4 * D, 4)],
                   [blocks_of(rz_r, NT * EV_IN - 2 * CH, 2), blocks_of(rh_r, 3 * D, 2)]]
        quarter.append(quarter[0])
        ro = [6 * D]

        def rt(w):
            ro[0] += w
            assert ro[0] <= NT * EV_IN - 2 * CH
            return rz[:, ro[0] - w:ro[0]]
        r_s, r_sel, r_beat, r_eq = rt(64), rt(64), rt(256), rt(256)
        r_top, r_gs, r_mask, r_w, r_pos, r_val, r_t = rt(64), rt(16), rt(64), rt(64), rt(64), rt(64), rt(64)
        r_gb, r_hi, r_lo, r_whi, r_wlo, r_sum, r_cnt = rt(64), rt(4), rt(4), rt(4), rt(4), rt(4), rt(16)
        wr_sb, br_sb = sm(KD * NE), sm(NE)
        subln_b, lam_b = sm(64), sm(128)
        sink_b, qk_b = sm(8), sm(128)

        dops = []
        for kind in range(2):
            dops.append([slot_r[(19 + 2 * kind + c // 8) % SLOTS][:, (c % 8) * NTOK:(c % 8 + 1) * NTOK] for c in range(16)])

        slotk_r = [s.rearrange("p (k n) -> p k n", k=KD) for s in slot_r]

        M0 = 0
        E0 = M0 + MODC
        U0 = E0 + len(EV_CH)
        S0 = U0 + 2
        SEL = S0 + 4
        O0 = SEL + 1
        MA = O0 + 2
        X0 = MA + PARTS[0][1]
        MB = X0 + 3 * NE
        E1 = MB + PARTS[1][1]
        MC_ = E1 + len(OD_CH)
        O1 = MC_ + PARTS[2][1]
        X1 = O1 + 2
        END = X1 + 3 * NE

        def view(w, cols, o=0):
            return w[:, o:o + cols].rearrange("(k p) n -> p k n", p=P)
        assert S0 == 19
        chunks_used = sem("chunks_used")
        full = [sem(f"slot_full{i}") for i in range(SLOTS)]

        def arrived(eng, n, it=None, step=1):
            v = 16 * (n // SLOTS + 1)
            if n > SEL and n % SLOTS in [c % SLOTS for c in range(S0, SEL)]:
                v -= 16
            eng.wait_ge(full[n % SLOTS], v if it is None else it * (16 * step) + v)

        def product_done(eng, name, base, tiles, i, t):
            if t == tiles[i] - 1:
                eng.wait_ge(chunks_used, base + i + 1)
            else:
                eng.wait_ge(sem(name), at(name, sum(n - 1 for n in tiles[:i]) + t + 1))

        def latent_done(eng, g):
            if g in (MH - 1, 2 * MH + NT - 1):
                eng.wait_ge(chunks_used, U0 + (1 if g < MH else 2))
            else:
                eng.wait_ge(sem("lat_mm"), at("lat_mm", g + (1 if g < MH else 0)))

        block = ctx.enter_context(nc.Block())

        @block.sync
        def _(sp):
            def load(n, dst, src, it=None, step=1):
                if n >= SLOTS or it is not None:
                    v = n - SLOTS + 1
                    sp.wait_ge(chunks_used, v if it is None else it * (SLOTS * step) + v)
                sp.dma_start(dst, src).then_inc(full[n % SLOTS], 16)

            s_v = sem("small_loaded")
            sp.dma_start(con[:, :], consts_dram[:, 0:NCON]).then_inc(s_v, 16)
            vecs = rq[:, 0:P]
            rows = [(a["c"].rearrange("a (k p) -> (a k) p", p=P), 8),
                    (a["c_ctx"].rearrange("(k p) -> k p", p=P), 8),
                    (a["norm_mix"].rearrange("l (k p) -> (l k) p", p=P), 16),
                    (a["norm_ffn"].rearrange("l (k p) -> (l k) p", p=P), 16),
                    (a["even_norm_q"].rearrange("l (k p) -> (l k) p", p=P), 3),
                    (a["even_norm_kv"].rearrange("l (k p) -> (l k) p", p=P), 2)]
            wide = [(subln_b, a["even_subln"][0]), (lam_b, a["even_lambda"][0].rearrange("a b -> (a b)")),
                    (sink_b, a["odd_sink"][0]), (qk_b[:, 0:64], a["odd_q_norm"][0]), (qk_b[:, 64:128], a["odd_k_norm"][0]),
                    (br_sb, a["b_router"])]
            r = 0
            for src, n in rows:
                sp.dma_start(vecs[r:r + n, :], src).then_inc(s_v, 16)
                r += n
            sp.dma_start(rq[0:96, P:2 * P], a["b_mod"].rearrange("l (k p) -> (l k) p", p=P)).then_inc(s_v, 16)

            def modulation(base, l, c0, n):
                for j in range(n):
                    load(base + j, slotk[(base + j) % SLOTS], view(a["w_mod"][l], CH, (c0 + j) * CH))
            modulation(M0, 0, 0, 3)
            for dst, src in wide:
                sp.dma_start(dst, src.partition_broadcast(P)).then_inc(sem("wide_loaded"), 16)
            sp.dma_start(wr_sb.rearrange("p (k e) -> p k e", k=KD), a["w_router"].rearrange("(k p) e -> p k e", p=P)).then_inc(sem("wide_loaded"), 16)
            sp.dma_start(xt[:, 0:LT, :], a["x"].rearrange("a (t p) d -> p (a t) d", p=P)).then_inc(sem("x_loaded"), 16)
            sp.dma_start(xt[:, LT:NT, :], a["ctx"].rearrange("a (t p) d -> p (a t) d", p=P)).then_inc(sem("x_loaded"), 16)
            modulation(M0 + 3, 0, 3, MODC - 3)
            for i, (o, w, _) in enumerate(EV_CH):
                n = E0 + i
                load(n, slotk[n % SLOTS][:, :, 0:w], view(a["even_w_in"][0], w, o))
            load(U0, slot[U0 % SLOTS][:, 0:3 * 768].rearrange("p (k n) -> p k n", k=3), view(a["even_w_uq"][0], 768))
            load(U0 + 1, slot[(U0 + 1) % SLOTS][:, 0:2 * 1024].rearrange("p (k n) -> p k n", k=2), view(a["even_w_ukv"][0], 1024))
            load(SEL, slot[SEL % SLOTS][:, 0:2048], consts_dram[:, NCON:NCON + 2048])
            for i in range(2):
                n = O0 + i
                load(n, slotk[n % SLOTS], view(a["even_w_out"][0], CH, i * CH))

            def experts(base, l):
                gate = a["w_gate"][l].rearrange("e (k p) f -> e p k f", p=P)
                up = a["w_up"][l].rearrange("e (k p) f -> e p k f", p=P)
                down = a["w_down"][l].rearrange("e (j p) d -> e p j d", p=P)
                with sp.Fori(0, NE // 2) as it:
                    for u in range(2):
                        e = it * 2 + u
                        for j, w in enumerate((gate, up, down)):
                            n = base + 3 * u + j
                            s = slotk[n % SLOTS] if j < 2 else slot[n % SLOTS].rearrange("p (j n) -> p j n", j=4)
                            load(n, s, w[ds(e, 1)].rearrange("e p k f -> (e p) k f"), it=it)

            def overflow(l):
                sp.wait_ge(sem(f"flag_set{l}"), at(f"flag_set{l}", 1))
                over = sp.value_load(flag_i[l][0:1, :], min_val=0, max_val=1)
                with sp.If(over > 0):
                    mats = [(a["w_gate"][l], FF), (a["w_up"][l], FF), (a["w_down"][l], D)]
                    sp.wait_ge(sem(f"y_v{l}"), at(f"y_v{l}", NE))
                    with sp.Fori(0, ROUNDS[l]) as r:
                        with sp.Fori(0, NE) as e:
                            for j in range(3):
                                if j == 0:
                                    sp.wait_ge(sem(f"over_xT{l}"), at(f"over_xT{l}", r * NE + e + 1))
                                else:
                                    sp.wait_ge(sem(f"over_used{l}"), at(f"over_used{l}", (r * NE + e) * 3 + j))
                                sp.dma_start(over_w[j], mats[j][0][ds(e, 1)].rearrange(
                                    "a (k p) n -> p (a k) n", p=P)).then_inc(sem(f"over_loaded{l}"), 16)
                sp.nop()
            modulation(MA, 1, *PARTS[0])
            experts(X0, 0)
            overflow(0)
            modulation(MB, 1, *PARTS[1])
            for i, (o, w, _) in enumerate(OD_CH):
                n = E1 + i
                load(n, slotk[n % SLOTS][:, :, 0:w], view(a["odd_w_in"][0], w, o))
            modulation(MC_, 1, *PARTS[2])
            for i in range(2):
                n = O1 + i
                load(n, slotk[n % SLOTS], view(a["odd_w_out"][0], CH, i * CH))
            experts(X1, 1)
            overflow(1)
            sp.wait_ge(sem("sumsq1"), at("sumsq1", NT))
            sp.wait_ge(sem("xn_ready1"), at("xn_ready1", NT))
            sp.dma_start(xt[:, LT, :], a["norm_final"].partition_broadcast(P)).then_inc(sem("nf_loaded"), 16)
            sp.wait_ge(sem("out_stored"), at("out_stored", 16 * LT))

        SMALL_LOADS, WIDE_LOADS = 8, 7

        def even_group(gi):
            units = []
            if gi == 0:
                for h in range(MH):
                    for t in range(NT):
                        k0 = 0 if t < LT else SEQ
                        units.append((qT[0:QD, h, t * P:(t + 1) * P], [kT[0:QD, h, k0:NTOK]], NTOK - k0,
                                      [z[:, j, h * MV:(h + 1) * MV] for j in range(k0 // P, NT)],
                                      bank[4 + t][:, h * MV:(h + 1) * MV]))
            else:
                for h in range(DH):
                    for c in range(2):
                        for i in range(LT):
                            t = i if gi == 1 else LT + i
                            k0 = 0 if gi == 1 else SEQ
                            units.append((dops[0][2 * h + c][:, t * P:(t + 1) * P], [dops[1][2 * h + c][:, k0:NTOK]], NTOK - k0,
                                          [z[:, j, ZV + h * DV:ZV + (h + 1) * DV] for j in range(k0 // P, NT)],
                                          bank[4 + 2 * c + i][:, h * DV:(h + 1) * DV]))
            return units

        def odd_units():
            units = []
            for h in range(8):
                for kind in range(2):
                    for t in range(LT):
                        v0 = 640 if kind == 0 else 1408
                        units.append((g_q[:, 8 * kind + h, t * P:(t + 1) * P], g_k[2 * kind + h // 4], NTOK,
                                      [zo[:, j, v0 + (h // 4) * HD:v0 + (h // 4 + 1) * HD] for j in range(NT)],
                                      bank[4 + 2 * kind + t][:, h * HD:(h + 1) * HD]))
            return units
        GROUPS = [[even_group(0), even_group(1), even_group(2)], [odd_units()]]
        GBASE = [[0, 32, 64], [0]]

        def bc_list(l):
            rs = range(2) if l == 0 else range(1)
            return [(0 + r, mod(l, 2, r)) for r in rs] + [(2 + r, scols[l][:, 8 * r + 16:8 * r + 24]) for r in rs] + \
                   [(4 + r, mod(l, 3, r)) for r in rs]

        def gate_list(l):
            return [(r, mod(l, 5, r)) for r in (range(2) if l == 0 else range(1))]

        @block.tensor
        def _(pe):
            mm = nc.tensor.matmul
            tr = nc.tensor.transpose
            pe.wait_ge(sem("small_loaded"), at("small_loaded", 16 * SMALL_LOADS))
            tr(bank[0][:, 0:53], rq[0:53, 0:P], ident[0:53, 0:53])
            tr(bank[1][:, 0:96], rq[0:96, P:2 * P], ident[0:96, 0:96]).then_inc(sem("vec_cols"), 1)

            def modulation0():
                def to_cols(it, j):
                    pe.wait_ge(sem("mod_row"), it * SLOTS + j + 1)
                    if j >= 2:
                        pe.wait_ge(sem("mod_T"), it * SLOTS + j - 1)
                    for i in range(4):
                        last = mm(bank[2 + j % 2][:, 2 * i:2 * i + 2], modrow[j % 2][:, i * P:(i + 1) * P],
                                  ident[0:2, 0:2], start=True, stop=True)
                    last.then_inc(sem("mod_cols"), 1)
                with pe.Fori(0, MODC // SLOTS) as it:
                    for j in range(SLOTS):
                        arrived(pe, M0 + j, it)
                        if j >= 2:
                            pe.wait_ge(sem("mod_row"), it * SLOTS + j - 1)
                        for k in range(KD):
                            last = mm(bank[j % 2][0:2, :], silu.rearrange("p (r k) -> p k r", r=2)[:, k, :],
                                      slotk[(M0 + j) % SLOTS][:, k, :], start=k == 0, stop=k == KD - 1)
                        last.then_inc(chunks_used, 1)
                        if j > 0:
                            to_cols(it, j - 1)
                    to_cols(it, SLOTS - 1)
                    pe.wait_ge(sem("mod_T"), it * SLOTS + SLOTS)

            def modulation1_products(part, base, j, blocks, between={}):
                if blocks[0] == 0:
                    arrived(pe, base + j)
                    if j >= 2:
                        pe.wait_ge(sem("mod1_row"), PARTS[part][0] + j - 1)
                for k in blocks:
                    if (j, k) in between:
                        between[j, k]()
                    last = mm(bank[2 + j % 2][0:2, :], silu.rearrange("p (r k) -> p k r", r=2)[:, k, :],
                              slotk[(base + j) % SLOTS][:, k, :], start=k == 0, stop=k == KD - 1)
                if blocks[-1] == KD - 1:
                    last.then_inc(chunks_used, 1)

            def modulation1(part, base, between={}, first=(0, 0)):
                c0, n = PARTS[part]

                def to_cols(j):
                    pe.wait_ge(sem("mod1_row"), c0 + j + 1)
                    for i in range(4):
                        last = mm(bank[0][:, 8 * j + 2 * i:8 * j + 2 * i + 2], modrow1[(c0 + j) % 2][:, i * P:(i + 1) * P],
                                  ident[0:2, 0:2], start=True, stop=True)
                    last.then_inc(sem("mod1_cols"), 1)
                for j in range(first[0], n):
                    modulation1_products(part, base, j, range(first[1] if j == first[0] else 0, KD), between)
                    if j > 0:
                        to_cols(j - 1)
                to_cols(n - 1)

            def norm_T(l):
                for kp in range(KD // 2):
                    for grp in range(2):
                        if kp == 0:
                            pe.wait_ge(sem(f"xn_ready{l}"), at(f"xn_ready{l}", 2 * (grp + 1)))
                        if kp >= 2:
                            pe.wait_ge(sem(f"hT{grp}_{l}"), at(f"hT{grp}_{l}", 2 * (kp - 1)))
                        for kk in range(2):
                            for i in range(2):
                                k, t = 2 * kp + kk, 2 * grp + i
                                last = tr(bank[4 + 2 * grp + kp % 2][:, kk * 256 + i * P:kk * 256 + (i + 1) * P],
                                          xn[:, t, k * P:(k + 1) * P], ident)
                        last.then_inc(sem(f"xT{grp}_{l}"), 1)

            def project(l, base, chunks):
                first = [sum(c[2] for c in chunks[:i]) for i in range(len(chunks))]
                for i, (o, w, tiles) in enumerate(chunks):
                    n = base + i
                    for half in range(2):
                        pe.wait_ge(sem(f"w_lo{l}"), at(f"w_lo{l}", 2 * i + half + 1))
                        for t in range(tiles):
                            if half == 0 and i >= 2:
                                g = first[i - 2] + t
                                if t < chunks[i - 2][2]:
                                    pe.wait_ge(sem(f"z_{'va'[g % 2]}{l}"), at(f"z_{'va'[g % 2]}{l}", g // 2 + 1))
                            for k in range(4 * half, 4 * half + 4):
                                if i == 0 and t == 0:
                                    pe.wait_ge(sem(f"h_split{l}"), at(f"h_split{l}", k + 1))
                                hh, hl = hT_hi[:, k, t * P:(t + 1) * P], hT_lo[:, k, t * P:(t + 1) * P]
                                wh, wl = w_hi[:, k, 0:w], slotk_r[n % SLOTS][:, k, 0:w]
                                out = bank[4 * (i % 2) + t][:, 0:w]
                                mm(out, hh, wh, start=k == 0, stop=False)
                                mm(out, hh, wl, start=False, stop=False)
                                last = mm(out, hl, wh, start=False, stop=k == KD - 1)
                            if half == 1:
                                last.then_inc(chunks_used if t == tiles - 1 else sem(f"z_mm{l}"), 1)
                            elif t == tiles - 1:
                                last.then_inc(sem(f"w_half{l}"), 1)

            def attend(l, gi):
                units, b = GROUPS[l][gi], GBASE[l][gi]
                if gi > 0:
                    pe.wait_ge(sem(f"o_read{l}"), at(f"o_read{l}", 4 * gi))

                def scores(u):
                    q, k, nk, _, _ = units[u]
                    if b + u >= 2:
                        pe.wait_ge(sem(f"p_ready{l}"), at(f"p_ready{l}", b + u - 1))
                    for i, kk in enumerate(k):
                        last = mm(bank[(b + u) % 2][:, 0:nk], q, kk, start=i == 0, stop=i == len(k) - 1)
                    last.then_inc(sem(f"s_ready{l}"), 1)
                scores(0)
                scores(1)
                for u in range(len(units) + 1):
                    if u < len(units):
                        pe.wait_ge(sem(f"p_ready{l}"), at(f"p_ready{l}", b + u + 1))
                        if b + u >= 2:
                            pe.wait_ge(sem(f"pT_ready{l}"), at(f"pT_ready{l}", b + u - 1))
                        for j in range(units[u][2] // P):
                            last = tr(bank[2 + (b + u) % 2][:, j * P:(j + 1) * P], probs[(b + u) % 4][:, j * P:(j + 1) * P], ident)
                        last.then_inc(sem(f"t_ready{l}"), 1)
                    if u + 2 < len(units):
                        scores(u + 2)
                    if u >= 1:
                        _, _, nk, vs, out = units[u - 1]
                        pe.wait_ge(sem(f"pT_ready{l}"), at(f"pT_ready{l}", b + u))
                        for j, v in enumerate(vs):
                            last = mm(out, probsT[(b + u - 1) % 2][:, j * P:(j + 1) * P], v, start=j == 0, stop=j == len(vs) - 1)
                            if (l, gi, u, j) == (0, 2, len(units), 0):
                                last.then_inc(chunks_used, 5)
                        last.then_inc(sem(f"pv_done{l}"), 1)

            def block_T(name, blocks, ready):
                for g, tiles in enumerate(blocks):
                    if g in ready:
                        pe.wait_ge(sem(ready[g][0]), ready[g][1])
                    if g >= 4:
                        pe.wait_ge(sem(f"{name}_{'va'[g % 2]}"), at(f"{name}_{'va'[g % 2]}", (g - 4) // 2 + 1))
                    for i, src in enumerate(tiles):
                        last = tr(bank[g % 4][:, i * P:(i + 1) * P], src, ident)
                    last.then_inc(sem(f"{name}_tr"), 1)

            def broadcast(name, cols, rows=None):
                for i in range(len(cols)) if rows is None else rows:
                    if i >= 2:
                        pe.wait_ge(sem(f"{name}_v"), at(f"{name}_v", i - 1))
                        pe.wait_ge(sem(f"{name}_a"), at(f"{name}_a", i - 1))
                    for k in range(KD):
                        last = mm(bank[4 + 2 * (i % 2) + k // 4][:, (k % 4) * P:(k % 4 + 1) * P],
                                  cols[i][1][:, k:k + 1].to_broadcast([P, P]), ident, start=True, stop=True)
                    last.then_inc(sem(f"{name}_mm"), 1)

            def out_project(l, base):
                T = TL[l]

                def token_T(t):
                    pe.wait_ge(sem(f"h_ready{l}"), at(f"h_ready{l}", t + 1))
                    if t >= 2:
                        pe.wait_ge(sem(f"h_v{l}"), at(f"h_v{l}", t - 1))
                        pe.wait_ge(sem(f"h_a{l}"), at(f"h_a{l}", t - 1))
                    for k in range(KD):
                        ins = tr(bank[4 + 2 * (t % 2) + k // 4][:, (k % 4) * P:(k % 4 + 1) * P], htok[t % 2][:, k * P:(k + 1) * P], ident)
                        if k % 4 == 3:
                            ins.then_inc(sem(f"h_lo{l}") if k == 3 else sem(f"h_hi{l}"), 1)

                def router(t):
                    pe.wait_ge(sem(f"h_v{l}"), at(f"h_v{l}", t + 1))
                    pe.wait_ge(sem(f"h_a{l}"), at(f"h_a{l}", t + 1))
                    for k in range(KD):
                        last = mm(bank[0][:, t * NE:(t + 1) * NE], hT[:, k, t * P:(t + 1) * P],
                                  wr_sb[:, k * NE:(k + 1) * NE], start=k == 0, stop=k == KD - 1)
                    if t == T - 1:
                        last.then_inc(sem(f"logits{l}"), 1)
                pe.wait_ge(sem("wide_loaded"), 16 * WIDE_LOADS)
                pe.wait_ge(sem(f"oT{l}_v"), at(f"oT{l}_v", 4))
                pe.wait_ge(sem(f"oT{l}_a"), at(f"oT{l}_a", 4))
                g = 0
                for i in range(2):
                    n = base + i
                    arrived(pe, n)
                    for t in range(T):
                        if g >= 4:
                            pe.wait_ge(sem(f"out_v{l}"), at(f"out_v{l}", g - 3))
                        for k in range(KD):
                            last = mm(bank[g % 4][:, :], oT[:, k, t * P:(t + 1) * P], slotk[n % SLOTS][:, k, :],
                                      start=k == 0, stop=k == KD - 1)
                        last.then_inc(chunks_used if t == T - 1 else sem(f"out_mm{l}"), 1)
                        g += 1
                        if i == 0:
                            r = len(gate_list(l)) + t
                            broadcast(f"bc{l}", bc_list(l), range(r, r + 1))
                        if i == 1 and t >= 1:
                            token_T(t - 1)
                            if t >= 2:
                                router(t - 2)
                if l == 0:
                    modulation1_products(0, MA, 0, range(0, KD))
                router(T - 2)
                token_T(T - 1)
                if l == 0:
                    modulation1_products(0, MA, 1, range(0, 4))
                router(T - 1)

            def experts(l, base):
                T = TL[l]
                m = r_mask.rearrange("p (t e) -> p t e", e=NE)

                def counts():
                    pe.wait_ge(sem(f"mask{l}"), at(f"mask{l}", 1))
                    later = lambda b: m[:, b:b + 1, :].to_broadcast([P, T - b, NE])
                    out = lambda b: bank[1][:, b * NE:(T + 1) * NE].rearrange("p (t e) -> p t e", e=NE)
                    mm(bank[1][:, 0:NE], tri, m[:, 0, :], start=True, stop=True)
                    mm(out(1), ones, later(0), start=True, stop=False)
                    mm(bank[1][:, NE:T * NE], tri, r_mask[:, NE:T * NE], start=False, stop=False)
                    for b in range(1, T):
                        last = mm(out(b + 1), ones, later(b), start=False, stop=b == T - 1)
                    last.then_inc(sem(f"counts{l}"), 1)

                def gates():
                    broadcast(f"gf{l}", gate_list(l))
                if l == 0:
                    pe.wait_ge(sem(f"sig{l}"), at(f"sig{l}", 1))
                    modulation1(0, MA, {(2, 0): counts, (3, 7): gates}, first=(1, 4))
                else:
                    counts()
                    gates()

                def rows_T(buf, when, loaded):
                    pe.wait_ge(sem(loaded), at(loaded, when))
                    for k in range(KD):
                        last = tr(bank[k // 4][:, (k % 4) * P:(k % 4 + 1) * P], xg[buf][:, k * P:(k + 1) * P], ident)
                        if k == 3:
                            last.then_inc(sem(f"xT_lo{l}"), 1)
                    last.then_inc(sem(f"xT_hi{l}"), 1)

                def pair(it, last_pair):
                    for u in range(2):
                        e = it * 2 + u
                        n = base + 3 * u
                        pe.wait_ge(sem(f"xgT_v{l}"), at(f"xgT_v{l}", e * 2 + 2))
                        pe.wait_ge(sem(f"act_ready{l}"), at(f"act_ready{l}", e))
                        for q in range(4):
                            j = q // 2
                            pe.wait_ge(sem(f"ex_lo{l}"), at(f"ex_lo{l}", e * 4 + q + 1))
                            k = 4 * (q % 2)
                            for part in quarter[q]:
                                for kk in range(part.shape[1]):
                                    wh, wl = part[:, kk, :], slotk_r[(n + j) % SLOTS][:, k, :]
                                    mm(bank[2 + j][:, :], xg_hi[u][:, k, :], wh, start=k == 0, stop=False)
                                    mm(bank[2 + j][:, :], xg_hi[u][:, k, :], wl, start=False, stop=False)
                                    last = mm(bank[2 + j][:, :], xg_lo[u][:, k, :], wh, start=False, stop=k == KD - 1)
                                    k += 1
                            if q == 0:
                                last.then_inc(sem(f"gate_half{l}"), 1)
                            elif q % 2:
                                last.then_inc(chunks_used, 1)
                        if not (last_pair and u == 1):
                            rows_T(1 - u, it * 16 + 16 * (1 + u), f"xg_loaded{l}_{1 - u}")
                        pe.wait_ge(sem(f"act_ready{l}"), at(f"act_ready{l}", e + 1))
                        for j in range(4):
                            last = tr(bank[4][:, j * P:(j + 1) * P], act_[u][:, j * P:(j + 1) * P], ident)
                        last.then_inc(sem(f"act_tr{l}"), 1)
                        pe.wait_ge(sem(f"actT_ready{l}"), at(f"actT_ready{l}", e + 1))
                        pe.wait_ge(sem(f"y_v{l}"), at(f"y_v{l}", e))
                        pe.wait_ge(sem(f"y_a{l}"), at(f"y_a{l}", e))
                        arrived(pe, n + 2, it)
                        w = slot[(n + 2) % SLOTS].rearrange("p (j n) -> p j n", j=4)
                        for h in range(2):
                            for j in range(4):
                                last = mm(bank[5 + h][:, :], actT[u][:, j, :], w[:, j, h * 512:(h + 1) * 512],
                                          start=j == 0, stop=j == 3)
                            last.then_inc(sem(f"y_mm{l}") if h == 0 else chunks_used, 1)
                pe.wait_ge(sem(f"flag_set{l}"), at(f"flag_set{l}", 1))
                if l == 0:
                    pe.wait_ge(sem("mod1_T"), 1)
                rows_T(0, 16, f"xg_loaded{l}_0")
                pair(0, False)
                with pe.Fori(1, NE // 2 - 1) as it:
                    pair(it, False)
                pair(NE // 2 - 1, True)

                pe.wait_ge(sem(f"flag_set{l}"), at(f"flag_set{l}", 1))
                over = pe.value_load(flag_i[l][0:1, :], min_val=0, max_val=1)
                with pe.If(over > 0):
                    pe.wait_ge(sem(f"y_v{l}"), at(f"y_v{l}", NE))
                    pe.wait_ge(sem(f"y_a{l}"), at(f"y_a{l}", NE))
                    with pe.Fori(0, ROUNDS[l] * NE) as i:
                        loaded, used = sem(f"over_loaded{l}"), sem(f"over_used{l}")
                        pe.wait_ge(sem(f"over_xg{l}"), at(f"over_xg{l}", i * 16 + 16))
                        for k in range(KD):
                            last = tr(bank[k // 4][:, (k % 4) * P:(k % 4 + 1) * P], xg[0][:, k * P:(k + 1) * P], ident)
                        last.then_inc(sem(f"over_xT{l}"), 1)
                        pe.wait_ge(sem(f"over_xgT{l}"), at(f"over_xgT{l}", i * 2 + 2))
                        for j in range(2):
                            pe.wait_ge(loaded, i * 48 + 16 * (j + 1))
                            for k in range(KD):
                                last = mm(bank[2 + j][:, :], xgT[0][:, k, :], over_w[j][:, k, :], start=k == 0, stop=k == KD - 1)
                            last.then_inc(used, 1)
                        pe.wait_ge(sem(f"over_act{l}"), at(f"over_act{l}", i + 1))
                        for j in range(4):
                            last = tr(bank[4][:, j * P:(j + 1) * P], act_[0][:, j * P:(j + 1) * P], ident)
                        last.then_inc(sem(f"over_act_tr{l}"), 1)
                        pe.wait_ge(sem(f"over_actT{l}"), at(f"over_actT{l}", i + 1))
                        pe.wait_ge(loaded, i * 48 + 48)
                        for h in range(2):
                            for j in range(4):
                                last = mm(bank[5 + h][:, :], actT[0][:, j, :], over_w[2][:, j, h * 512:(h + 1) * 512],
                                          start=j == 0, stop=j == 3)
                        last.then_inc(used, 1)
                pe.nop()

            pe.wait_ge(sem("silu_c"), at("silu_c", 1))
            modulation0()
            norm_T(0)
            project(0, E0, EV_CH)
            pe.wait_ge(sem("z_v0"), at("z_v0", 10))
            pe.wait_ge(sem("z_a0"), at("z_a0", 10))

            pe.wait_ge(sem("cn_ready"), at("cn_ready", NT))
            for b in range(5):
                if b == 4:
                    pe.wait_ge(sem("ct_ready"), at("ct_ready", 1))
                for t in range(NT):
                    last = tr(bank[4 + b % 4][:, t * P:(t + 1) * P], z[:, t, b * P:(b + 1) * P], ident)
                last.then_inc(sem("ct_tr"), 1)
            pe.wait_ge(sem("ct_ready"), at("ct_ready", 5))
            pe.wait_ge(sem("krope_done"), at("krope_done", LT))
            for t in range(NT):
                last = mm(bank[5][64:96, t * P:(t + 1) * P], z[:, t, QL + KVL:QL + KVL + RD], ident, start=True, stop=True)
            last.then_inc(sem("kr_mm"), 1)
            uq = slot[U0 % SLOTS][:, 0:3 * 768].rearrange("p (k n) -> p k n", k=3)
            ukv = slot[(U0 + 1) % SLOTS][:, 0:2 * 1024].rearrange("p (k n) -> p k n", k=2)
            arrived(pe, U0)
            for g in range(20):
                if g >= 4:
                    pe.wait_ge(sem(f"lat_{'va'[g % 2]}"), at(f"lat_{'va'[g % 2]}", (g - 4) // 2 + 1))
                if g == MH:
                    arrived(pe, U0 + 1)
                if g < MH:
                    for k in range(3):
                        last = mm(bank[g % 4][0:QD, :], uq[:, k, g * QD:(g + 1) * QD], cT[:, k, :], start=k == 0, stop=k == 2)
                elif g < 2 * MH:
                    h = g - MH
                    for k in range(2):
                        last = mm(bank[g % 4][0:NOPE, :], ukv[:, k, h * P:h * P + NOPE], cT[:, 3 + k, :], start=k == 0, stop=k == 1)
                else:
                    t = g - 2 * MH
                    for k in range(2):
                        last = mm(bank[g % 4][:, :], cT[:, 3 + k, t * P:(t + 1) * P],
                                  ukv[:, k, :].rearrange("p (h c) -> p h c", h=MH)[:, :, NOPE:P], start=k == 0, stop=k == 1)
                last.then_inc(chunks_used if g in (MH - 1, 2 * MH + NT - 1) else sem("lat_mm"), 1)
            pe.wait_ge(sem("lat_v"), at("lat_v", 10))
            pe.wait_ge(sem("lat_a"), at("lat_a", 10))
            pe.wait_ge(sem("kT_rope"), at("kT_rope", 1))
            for i in range(4):
                if i >= 2:
                    pe.wait_ge(sem("qrot_read"), at("qrot_read", i - 1))
                mm(bank[6 + i % 2][64:96, :], const("rot")[64:96, :], qT[64:96, 2 * i:2 * i + 2, 0:SEQ],
                   start=True, stop=True).then_inc(sem("qrot_mm"), 1)
            pe.wait_ge(sem("qT_ready"), at("qT_ready", 4))
            pe.wait_ge(sem("kT_ready"), at("kT_ready", 1))
            attend(0, 0)
            pe.wait_ge(sem("diff_rope"), at("diff_rope", NT))
            pe.wait_ge(sem("o_read0"), at("o_read0", 4))
            sel = slot_r[SEL % SLOTS][:, 2048:4096].rearrange("p (k s j m) -> p k s j m", k=2, s=2, j=4)

            def diff_T(i):
                if i >= 2:
                    pe.wait_ge(sem("split_lo"), at("split_lo", i - 1))
                for t in range(NT):
                    o = (ZQ, ZK)[i // 4] + (i % 4) * P
                    last = tr(bank[4 + i % 2][:, t * P:(t + 1) * P], z[:, t, o:o + P], ident)
                last.then_inc(sem("diff_tr"), 1)
            diff_T(0)
            diff_T(1)
            pe.wait_ge(sem("sel_ready"), 1)
            for g in range(32):
                if g % 4 == 0:
                    pe.wait_ge(sem("split_lo"), at("split_lo", g // 4 + 1))
                if g >= 4:
                    pe.wait_ge(sem(f"dT_{'va'[g % 2]}"), at(f"dT_{'va'[g % 2]}", (g - 4) // 2 + 1))
                mm(bank[g % 4][:, :], sel[:, g // 16, 0, g % 4, :], d_hi[:, g // 4, :], start=True, stop=False)
                last = mm(bank[g % 4][:, :], sel[:, g // 16, 1, g % 4, :], d_lo[:, g // 4, :], start=False, stop=True)
                last.then_inc(sem("dT_tr"), 1)
                if g % 4 == 3 and g // 4 + 2 < 8:
                    diff_T(g // 4 + 2)
            pe.wait_ge(sem("dT_v"), at("dT_v", 16))
            pe.wait_ge(sem("dT_a"), at("dT_a", 16))
            attend(0, 1)
            attend(0, 2)

            def o_src(l, t, k):
                if l == 1:
                    return zo[:, t, k * P:(k + 1) * P]
                return z[:, t, k * P:(k + 1) * P] if k < 4 else z[:, t, ZQ + (k - 4) * P:ZQ + (k - 3) * P]
            block_T("oT0", [[o_src(0, t, k) for t in range(NT)] for k in range(KD)], {4: ("o_ready0", 8)})
            broadcast("bc0", bc_list(0), range(2))
            out_project(0, O0)
            experts(0, X0)
            modulation1(1, MB)
            norm_T(1)
            pe.wait_ge(sem("mod1_T"), 2)
            project(1, E1, OD_CH)
            pe.wait_ge(sem("z_v1"), at("z_v1", 6))
            pe.wait_ge(sem("z_a1"), at("z_a1", 6))
            modulation1(2, MC_)
            pe.wait_ge(sem("mod1_T"), 3)
            pe.wait_ge(sem("odd_rope_w"), 1)
            pe.wait_ge(sem("odd_rope_d"), 1)

            def query_T(b):
                if b >= 2:
                    pe.wait_ge(sem("gx_lo"), at("gx_lo", b - 1))
                for t in range(LT):
                    o = (b // 4) * 768 + (b % 4) * P
                    last = tr(bank[4 + b % 2][:, t * P:(t + 1) * P], zo[:, t, o:o + P], ident)
                last.then_inc(sem("gx_tr"), 1)
            query_T(0)
            query_T(1)
            for b in range(8):
                pe.wait_ge(sem("gx_lo"), at("gx_lo", b + 1))
                if b >= 2:
                    pe.wait_ge(sem(f"g_q_{'va'[b % 2]}"), at(f"g_q_{'va'[b % 2]}", (b - 2) // 2 + 1))
                for h in range(2):
                    out = bank[b % 2][:, h * SEQ:(h + 1) * SEQ]
                    mm(out, sel64[:, 192 * h + 64:192 * h + 192], gx_hi[:, b, :], start=True, stop=False)
                    last = mm(out, sel64[:, 192 * h:192 * h + 128], gx_lo[:, b, :], start=False, stop=True)
                last.then_inc(sem("g_q_tr"), 1)
                if b + 2 < 8:
                    query_T(b + 2)
            for g in range(4):
                if g >= 2:
                    pe.wait_ge(sem("gk_lo"), at("gk_lo", g - 1))
                for t in range(NT):
                    last = tr(bank[2 + g % 2][:, t * P:(t + 1) * P], kdup[:, (g * NT + t) * P:(g * NT + t + 1) * P], ident)
                last.then_inc(sem("gk_tr"), 1)
            pe.wait_ge(sem("gk_lo"), at("gk_lo", 4))
            pe.wait_ge(sem("g_q_v"), at("g_q_v", 4))
            pe.wait_ge(sem("g_q_a"), at("g_q_a", 4))
            attend(1, 0)
            block_T("oT1", [[o_src(1, t, k) for t in range(LT)] for k in range(KD)], {0: ("o_ready1", 4)})
            broadcast("bc1", bc_list(1), range(1))
            out_project(1, O1)
            experts(1, X1)

        @block.vector
        def _(ve):
            V = nc.vector
            done = [0]

            def link(ins):
                done[0] += 1
                ins.then_inc(sem("v_chain"), 1)
                ve.wait_ge(sem("v_chain"), at("v_chain", done[0]))

            sums_n, roots_n = [0], [0]

            def sums_done(ins):
                sums_n[0] += 1
                ins.then_inc(sem("sums_ready"), 1)
                ve.wait_ge(sem("sums_ready"), at("sums_ready", sums_n[0]))

            def rms(out, n, o=0):
                roots_n[0] += 1
                ve.wait_ge(sem("root_ready"), at("root_ready", roots_n[0]))
                link(V.reciprocal(out, roots[:, o:o + n]))

            ve.wait_ge(sem("vec_cols"), at("vec_cols", 1))
            V.tensor_copy(colv[:, 0:53], bank[0][:, 0:53]).then_inc(sem("vec_sb"), 1)
            V.tensor_copy(bmodT, bank[1][:, 0:96]).then_inc(sem("vec_sb"), 1)
            ve.wait_ge(sem("vec_sb"), at("vec_sb", 2))
            link(V.tensor_copy(tokid_i, const("tokid")))
            for h in range(2):
                half = ident[:, 64 * h:64 * h + 64]
                for i, factor in enumerate((0.0, 1.0, 0.0)):
                    ins = V.tensor_scalar(sel64[:, (3 * h + i) * 64:(3 * h + i + 1) * 64], half, factor, None, ALU.mult)
            link(ins)
            ve.wait_ge(sem("wide_loaded"), at("wide_loaded", 16 * WIDE_LOADS))
            lq = lam_b.rearrange("p (a b c) -> p a b c", a=2, b=2)
            link(V.tensor_tensor(lq[:, :, 0, :], lq[:, :, 0, :], lq[:, :, 1, :], ALU.mult))
            V.tensor_reduce(lamv[:, 0:2], lq[:, :, 0, :], AX, ALU.add).then_inc(sem("lam_sums"), 1)
            link(V.tensor_scalar(subln_b, subln_b, 1.0 - LAM_INIT, None, ALU.mult))

            def scale_cols(l, section, gain, o):
                for r in range(2):
                    V.scalar_tensor_tensor(scols[l][:, o + 8 * r:o + 8 * r + 8], mod(l, section, r), 1.0,
                                           colv[:, gain + 8 * l:gain + 8 * l + 8], ALU.add, ALU.mult).then_inc(sem(f"scol{l}"), 1)
                ve.wait_ge(sem(f"scol{l}"), at(f"scol{l}", 2 if section == 1 else 4))

            def modulation0():
                mT = modT.rearrange("p (l b r) -> p l b r", l=2, r=2)[:, 0]
                with ve.Fori(0, MODC // SLOTS) as it:
                    def to_T(j):
                        ve.wait_ge(sem("mod_cols"), it * SLOTS + j + 1)
                        c = it * (SLOTS * 4) + 4 * j
                        V.tensor_tensor(mT[:, ds(c, 4), :], bank[2 + j % 2][:, 0:8].rearrange("p (b r) -> p b r", r=2),
                                        bmodT[:, ds(c, 4)].unsqueeze(2).to_broadcast([P, 4, 2]), ALU.add).then_inc(sem("mod_T"), 1)
                    for j in range(SLOTS):
                        ve.wait_ge(chunks_used, it * SLOTS + M0 + j + 1)
                        V.tensor_copy(modrow[j % 2], bank[j % 2][0:2, :]).then_inc(sem("mod_row"), 1)
                        if j > 0:
                            to_T(j - 1)
                    to_T(SLOTS - 1)
                ve.wait_ge(sem("mod_T"), MODC)
                scale_cols(0, 1, C_NM, 0)
                scale_cols(0, 4, C_NF, 16)

            def modulation1(part):
                c0, n = PARTS[part]
                ve.wait_ge(sem("mod1_cols"), c0 + n)
                V.tensor_tensor(modT[:, 96 + 8 * c0:96 + 8 * (c0 + n)].rearrange("p (b r) -> p b r", r=2),
                                bank[0][:, 0:8 * n].rearrange("p (b r) -> p b r", r=2),
                                bmodT[:, 48 + 4 * c0:48 + 4 * (c0 + n)].unsqueeze(2).to_broadcast([P, 4 * n, 2]),
                                ALU.add).then_inc(sem("mod1_T"), 1)
                ve.wait_ge(sem("mod1_T"), part + 1)

            def norm_tile(l, t):
                rms(rstd[:, t:t + 1], 1, t)
                V.tensor_scalar(xn[:, t, :], xt[:, t, :], rstd[:, t:t + 1], None, ALU.mult).then_inc(sem(f"xn_ready{l}"), 1)

            def weight_lo(l, base, chunks, i, half):
                n, w, k = base + i, chunks[i][1], slice(4 * half, 4 * half + 4)
                ve.wait_ge(sem(f"w_hi{l}"), at(f"w_hi{l}", 2 * i + half + 1))
                V.tensor_tensor(slotk_r[n % SLOTS][:, k, 0:w], slotk[n % SLOTS][:, k, 0:w], w_hi[:, k, 0:w].bitcast(f32),
                                ALU.subtract).then_inc(sem(f"w_lo{l}"), 1)

            def norm(l):
                if l == 0:
                    for t in range(NT):
                        norm_tile(0, t)
                weight_lo(l, E0 if l == 0 else E1, EV_CH if l == 0 else OD_CH, 0, 0)
                if l == 1:
                    modulation1(1)
                    scale_cols(1, 4, C_NF, 16)
                for k in range(KD):
                    ve.wait_ge(sem(f"xT0_{l}"), at(f"xT0_{l}", k // 2 + 1))
                    V.tensor_scalar(hT[:, k, 0:SEQ], bank[4 + (k // 2) % 2][:, (k % 2) * 256:(k % 2 + 1) * 256],
                                    scols[l][:, k:k + 1], mod(l, 0, 0)[:, k:k + 1], ALU.mult, ALU.add).then_inc(sem(f"hT0_{l}"), 1)
                    if k >= 1:
                        token_lo(l, k - 1)
                token_lo(l, KD - 1)
                weight_lo(l, E0 if l == 0 else E1, EV_CH if l == 0 else OD_CH, 0, 1)

            def token_lo(l, k):
                ve.wait_ge(sem(f"h_part{l}"), at(f"h_part{l}", k + 1))
                V.tensor_tensor(hT_lo[:, k, :], hT[:, k, :], hT_hi[:, k, :].bitcast(f32), ALU.subtract).then_inc(sem(f"h_split{l}"), 1)

            def projected(l, base, chunks, zz):
                g = 0
                for i, (o, w, tiles) in enumerate(chunks):
                    if i + 1 < len(chunks):
                        weight_lo(l, base, chunks, i + 1, 0)
                    for t in range(tiles):
                        if g % 2 == 0:
                            product_done(ve, f"z_mm{l}", base, [c[2] for c in chunks], i, t)
                            V.tensor_copy(zz[:, t, o:o + w], bank[4 * (i % 2) + t][:, 0:w]).then_inc(sem(f"z_v{l}"), 1)
                        g += 1
                    if i + 1 < len(chunks):
                        weight_lo(l, base, chunks, i + 1, 1)

            def rope(src, cos, sin, heads, d, t1, t2):
                q = d // 4
                s4 = src.rearrange("p (h x a q) -> p h x a q", h=heads, x=2, a=2)
                t4 = t1.rearrange("p (h x a q) -> p h x a q", h=heads, x=2, a=2)
                n4 = sin.rearrange("p (x a q) -> p x a q", x=2, a=2)
                for i in range(2):
                    V.tensor_tensor(t4[:, :, :, i, :], s4[:, :, :, 1 - i, :],
                                    n4[:, :, i, :].unsqueeze(1).to_broadcast([P, heads, 2, q]), ALU.mult)\
                     .then_inc(sem("v_rope"), 1)
                    rope_n[0] += 1
                ve.wait_ge(sem("v_rope"), at("v_rope", rope_n[0]))
                s2 = src.rearrange("p (h d) -> p h d", h=heads)
                link(V.tensor_tensor(s2, s2, cos.unsqueeze(1).to_broadcast([P, heads, d]), ALU.mult))
                return V.tensor_tensor(src, src, t1, ALU.add)
            rope_n = [0]

            def attend(l, gi, between={}):
                units, b = GROUPS[l][gi], GBASE[l][gi]

                def maxima(u):
                    nk = units[u][2]
                    ve.wait_ge(sem(f"s_ready{l}"), at(f"s_ready{l}", b + u + 1))
                    s = bank[(b + u) % 2]
                    m = nmx[:, (b + u) % 64:(b + u) % 64 + 1]
                    if l == 1 and (u // 2) % 2 == 0:
                        t = u % 2
                        far = s[:, P:2 * P] if t == 0 else s[:, 0:P]
                        link(V.tensor_tensor(far, far, const("wmask")[:, t * P:(t + 1) * P], ALU.add))
                        link(V.tensor_reduce(m, s[:, 0:nk], AX, ALU.max, negate=True))
                        V.tensor_tensor(m, m, nsink[:, u // 4:u // 4 + 1], ALU.min).then_inc(sem(f"max_ready{l}"), 1)
                    else:
                        V.tensor_reduce(m, s[:, 0:nk], AX, ALU.max, negate=True).then_inc(sem(f"max_ready{l}"), 1)
                maxima(0)
                maxima(1)
                for u in range(len(units)):
                    ve.wait_ge(sem(f"t_ready{l}"), at(f"t_ready{l}", b + u + 1))
                    if b + u >= 2:
                        ve.wait_ge(sem(f"pv_done{l}"), at(f"pv_done{l}", b + u - 1))
                    nk = units[u][2]
                    V.tensor_copy(probsT[(b + u) % 2][:, 0:nk], bank[2 + (b + u) % 2][:, 0:nk]).then_inc(sem(f"pT_ready{l}"), 1)
                    if u + 2 < len(units):
                        maxima(u + 2)
                    if u in between:
                        between[u]()
                ve.wait_ge(sem(f"pv_done{l}"), at(f"pv_done{l}", b + len(units)))
                ve.wait_ge(sem(f"p_ready{l}"), at(f"p_ready{l}", b + len(units)))

            def heads(ap):
                return ap.rearrange("p (h d) -> p h d", h=8)

            def per_head(v):
                return v.unsqueeze(2).to_broadcast([P, 8, 64])

            def transposed(name, blocks, dst, n):
                for g in range(0, blocks, 2):
                    ve.wait_ge(sem(f"{name}_tr"), at(f"{name}_tr", g + 1))
                    V.tensor_copy(dst(g), bank[g % 4][:, 0:n]).then_inc(sem(f"{name}_v"), 1)

            def broadcast(name, cols, rows=None):
                for i in range(len(cols)) if rows is None else rows:
                    ve.wait_ge(sem(f"{name}_mm"), at(f"{name}_mm", i + 1))
                    V.tensor_copy(bc[cols[i][0]][:, 0:512], bank[4 + 2 * (i % 2)][:, :]).then_inc(sem(f"{name}_v"), 1)
                    if rows is not None or i == len(cols) - 1:
                        ve.wait_ge(sem(f"{name}_v"), at(f"{name}_v", i + 1))
                        ve.wait_ge(sem(f"{name}_a"), at(f"{name}_a", i + 1))

            def out_project(l):
                g = 0
                T = TL[l]

                def token_rows(t):
                    rms(rstd[:, t:t + 1], 1, t)
                    if t >= 2:
                        ve.wait_ge(sem(f"h_hi{l}"), at(f"h_hi{l}", t - 1))
                        ve.wait_ge(sem(f"h_stored{l}_{t % 2}"), at(f"h_stored{l}_{t % 2}", 16 * (t // 2)))
                    link(V.scalar_tensor_tensor(htok[t % 2], xt[:, t, :], rstd[:, t:t + 1], bc[2 + t // LT], ALU.mult, ALU.mult))
                    V.tensor_tensor(htok[t % 2], htok[t % 2], bc[4 + t // LT], ALU.add).then_inc(sem(f"h_ready{l}"), 1)

                def token_cols(t):
                    ve.wait_ge(sem(f"h_lo{l}"), at(f"h_lo{l}", t + 1))
                    V.tensor_copy(hT[:, 0:4, t * P:(t + 1) * P], bank[4 + 2 * (t % 2)][:, :].rearrange("p (k n) -> p k n", k=4))\
                     .then_inc(sem(f"h_v{l}"), 1)
                for i in range(2):
                    for t in range(T):
                        product_done(ve, f"out_mm{l}", O0 if l == 0 else O1, [T, T], i, t)
                        tm = rk[:, (g % 4) * 512:(g % 4 + 1) * 512]
                        ins = V.tensor_tensor(tm, bank[g % 4][:, :], bc[t // LT][:, i * 512:(i + 1) * 512], ALU.mult)
                        ins.then_inc(sem(f"out_v{l}"), 1)
                        g += 1
                        ve.wait_ge(sem(f"out_v{l}"), at(f"out_v{l}", g))
                        xs = xt[:, t, i * 512:(i + 1) * 512]
                        V.tensor_tensor(xs, xs, tm, ALU.add).then_inc(sem(f"x_add{l}"), 1)
                        if i == 0:
                            r = len(gate_list(l)) + t
                            broadcast(f"bc{l}", bc_list(l), range(r, r + 1))
                        if i == 1:
                            if t >= 1:
                                token_cols(t - 1)
                            token_rows(t)
                token_cols(T - 1)

            def experts(l):
                T = TL[l]
                W = T * NE
                G = T * NG
                s, sel, top, mask, w = r_s[:, 0:W], r_sel[:, 0:W], r_top[:, 0:W], r_mask[:, 0:W], r_w[:, 0:W]
                te = lambda v: v.rearrange("p (t e) -> p t e", e=NE)
                ge = lambda v: v.rearrange("p (g e) -> p g e", e=EG)
                ve.wait_ge(sem(f"sig{l}"), at(f"sig{l}", 1))
                link(V.tensor_tensor(te(sel), te(s), br_sb.unsqueeze(1).to_broadcast([P, T, NE]), ALU.add))

                def outranked(v, groups, n):
                    vv = v.rearrange("p (g e) -> p g e", e=n)
                    by, of = vv.unsqueeze(2).to_broadcast([P, groups, n, n]), vv.unsqueeze(3).to_broadcast([P, groups, n, n])
                    beat = r_beat[:, 0:groups * n * n].rearrange("p (g i j) -> p g i j", i=n, j=n)
                    eq = r_eq[:, 0:groups * n * n].rearrange("p (g i j) -> p g i j", i=n, j=n)
                    V.tensor_tensor(beat, by, of, ALU.is_gt)
                    link(V.tensor_tensor(eq, by, of, ALU.is_equal))
                    eqf = r_eq[:, 0:groups * n * n].rearrange("p (g m) -> p g m", m=n * n)
                    link(V.tensor_tensor(eqf, eqf, const("lower").unsqueeze(1).to_broadcast([P, groups, n * n]), ALU.mult))
                    link(V.tensor_tensor(r_beat[:, 0:groups * n * n], r_beat[:, 0:groups * n * n], r_eq[:, 0:groups * n * n], ALU.add))
                    return beat
                beat = outranked(sel, G, EG)
                link(V.tensor_reduce(top, beat, AX, ALU.add))
                link(V.tensor_scalar(top, top, 1.5, None, ALU.is_lt))
                link(V.tensor_tensor(r_t[:, 0:W], sel, top, ALU.mult))
                link(V.tensor_reduce(r_gs[:, 0:G], ge(r_t[:, 0:W]), AX, ALU.add))
                beat = outranked(r_gs[:, 0:G], T, NG)
                link(V.tensor_reduce(r_gb[:, 0:G], beat, AX, ALU.add))
                link(V.tensor_scalar(r_gb[:, 0:G], r_gb[:, 0:G], 0.5, None, ALU.is_lt))
                V.tensor_tensor(ge(mask), ge(top), r_gb[:, 0:G].unsqueeze(2).to_broadcast([P, G, EG]), ALU.mult)\
                 .then_inc(sem(f"mask{l}"), 1)
                ve.wait_ge(sem(f"mask{l}"), at(f"mask{l}", 1))
                link(V.tensor_tensor(w, s, mask, ALU.mult))
                link(V.tensor_reduce(r_sum[:, 0:T], te(w), AX, ALU.add))
                link(V.reciprocal(r_sum[:, 0:T], r_sum[:, 0:T]))
                link(V.tensor_tensor(te(w), te(w), r_sum[:, 0:T].unsqueeze(2).to_broadcast([P, T, NE]), ALU.mult))
                ve.wait_ge(sem(f"counts{l}"), at(f"counts{l}", 1))
                val = r_val[:, 0:W]
                link(V.tensor_scalar(r_pos[:, 0:W], bank[1][:, 0:W], float(NE), None, ALU.mult))
                link(V.tensor_tensor(te(val), te(r_pos[:, 0:W]), const("eidx").unsqueeze(1).to_broadcast([P, T, NE]), ALU.add))
                link(V.tensor_scalar(r_t[:, 0:W], val, 1.0, None, ALU.add))
                link(V.tensor_tensor(r_t[:, 0:W], r_t[:, 0:W], mask, ALU.mult))
                link(V.tensor_reduce(r_hi[:, 0:T], te(r_t[:, 0:W]), AX, ALU.max))
                link(V.tensor_scalar(r_hi[:, 0:T], r_hi[:, 0:T], -1.0, None, ALU.add))
                link(V.tensor_scalar(r_t[:, 0:W], val, -1.0, float(ROWS), ALU.mult, ALU.add))
                link(V.tensor_tensor(r_t[:, 0:W], r_t[:, 0:W], mask, ALU.mult))
                link(V.tensor_reduce(r_lo[:, 0:T], te(r_t[:, 0:W]), AX, ALU.max))
                link(V.tensor_scalar(r_lo[:, 0:T], r_lo[:, 0:T], -1.0, float(ROWS), ALU.mult, ALU.add))
                V.tensor_copy(idx_hi[:, 0:T], r_hi[:, 0:T]).then_inc(sem(f"idx{l}"), 1)
                V.tensor_copy(idx_lo[:, 0:T], r_lo[:, 0:T]).then_inc(sem(f"idx{l}"), 1)
                link(V.tensor_reduce(r_cnt[:, 0:1], bank[1][:, W:W + NE], AX, ALU.max))
                V.tensor_scalar(flag_i[l], r_cnt[:, 0:1], cap + 0.5, None, ALU.is_gt).then_inc(sem(f"flag_set{l}"), 1)
                for sel_idx, wsel in ((r_hi, r_whi), (r_lo, r_wlo)):
                    link(V.tensor_tensor(te(r_t[:, 0:W]), te(val), sel_idx[:, 0:T].unsqueeze(2).to_broadcast([P, T, NE]), ALU.is_equal))
                    link(V.tensor_tensor(r_t[:, 0:W], r_t[:, 0:W], w, ALU.mult))
                    link(V.tensor_reduce(wsel[:, 0:T], te(r_t[:, 0:W]), AX, ALU.add))

                broadcast(f"gf{l}", gate_list(l))
                if l == 0:
                    modulation1(0)
                    scale_cols(1, 1, C_NM, 0)

                def rows_lo(buf, e):
                    for h in range(2):
                        ve.wait_ge(sem(f"xgT_a{l}"), at(f"xgT_a{l}", e * 2 + h + 1))
                        V.tensor_tensor(xg_lo[buf][:, 4 * h:4 * h + 4, :], bank[h][:, :].rearrange("p (k n) -> p k n", k=4),
                                        xg_hi[buf][:, 4 * h:4 * h + 4, :].bitcast(f32), ALU.subtract).then_inc(sem(f"xgT_v{l}"), 1)

                def quarter_lo(u, e, q):
                    ve.wait_ge(sem(f"ex_hi{l}"), at(f"ex_hi{l}", e * 4 + q + 1))
                    k, s_ = 4 * (q % 2), ((X0 if l == 0 else X1) + 3 * u + q // 2) % SLOTS
                    for part in quarter[q]:
                        n = part.shape[1]
                        ins = V.tensor_tensor(slotk_r[s_][:, k:k + n, :], slotk[s_][:, k:k + n, :], part.bitcast(f32), ALU.subtract)
                        k += n
                    ins.then_inc(sem(f"ex_lo{l}"), 1)

                def pair(it, last_pair):
                    for u in range(2):
                        e = it * 2 + u
                        quarter_lo(u, e, 3)
                        ve.wait_ge(sem(f"silu_ready{l}"), at(f"silu_ready{l}", e + 1))
                        ve.wait_ge(chunks_used, e * 3 + (X0 if l == 0 else X1) + 2)
                        V.tensor_tensor(act_[u], sg[u], bank[3][:, :], ALU.mult).then_inc(sem(f"act_ready{l}"), 1)
                        if not (last_pair and u == 1):
                            rows_lo(1 - u, e + 1)
                            for q in range(3):
                                quarter_lo(1 - u, e + 1, q)
                        ve.wait_ge(sem(f"y_mm{l}"), at(f"y_mm{l}", e + 1))
                        ve.wait_ge(sem(f"y_stored{l}_{u}"), at(f"y_stored{l}_{u}", it * 16))
                        V.tensor_copy(ybuf[u][:, 0:512], bank[5][:, :]).then_inc(sem(f"y_v{l}"), 1)
                for b in range(2):
                    ve.wait_ge(sem(f"h_stored{l}_{b}"), at(f"h_stored{l}_{b}", 8 * T))
                for q in range(3):
                    quarter_lo(0, 0, q)
                rows_lo(0, 0)
                pair(0, False)
                with ve.Fori(1, NE // 2 - 1) as it:
                    pair(it, False)
                pair(NE // 2 - 1, True)

                over = ve.value_load(flag_i[l][0:1, :], min_val=0, max_val=1)
                with ve.If(over > 0):
                    ve.wait_ge(sem(f"y_stored{l}_0"), at(f"y_stored{l}_0", 8 * NE))
                    with ve.Fori(0, ROUNDS[l] * NE) as i:
                        ve.wait_ge(sem(f"over_xT{l}"), at(f"over_xT{l}", i + 1))
                        for h in range(2):
                            V.tensor_copy(xgT[0][:, 4 * h:4 * h + 4, :], bank[h][:, :].rearrange("p (k n) -> p k n", k=4))\
                             .then_inc(sem(f"over_xgT{l}"), 1)
                        ve.wait_ge(sem(f"over_silu{l}"), at(f"over_silu{l}", i + 1))
                        V.tensor_tensor(act_[0], sg[0], bank[3][:, :], ALU.mult).then_inc(sem(f"over_act{l}"), 1)
                        ve.wait_ge(sem(f"over_used{l}"), at(f"over_used{l}", i * 3 + 3))
                        for h in range(2):
                            V.tensor_copy(ybuf[0][:, 512 * h:512 * h + 512], bank[5 + h][:, :]).then_inc(sem(f"over_y{l}"), 1)
                ve.nop()

                for t in range(T):
                    ve.wait_ge(sem(f"yb_loaded{l}_{t}"), at(f"yb_loaded{l}_{t}", 16))
                    V.scalar_tensor_tensor(yb[t], yb[t], r_wlo[:, t:t + 1], bc[t // LT], ALU.mult, ALU.mult)
                    ve.wait_ge(sem(f"ya_loaded{l}_{t}"), at(f"ya_loaded{l}_{t}", 16))
                    link(V.scalar_tensor_tensor(ya[t], ya[t], r_whi[:, t:t + 1], bc[t // LT], ALU.mult, ALU.mult))
                    V.tensor_tensor(ya[t], ya[t], yb[t], ALU.add).then_inc(sem(f"y_sum{l}"), 1)
                    if l == 0 and t >= 2:
                        norm_tile(1, t - 2)
                if l == 0:
                    for t in (NT - 2, NT - 1):
                        norm_tile(1, t)

            modulation0()
            norm(0)
            projected(0, E0, EV_CH, z)

            rms(rstd[:, 0:4], 4)
            rms(rstd[:, 4:8], 4, 4)
            for t in range(NT):
                V.tensor_scalar(z[:, t, 0:QL], z[:, t, 0:QL], rstd[:, t:t + 1], None, ALU.mult)
                V.tensor_scalar(z[:, t, QL:QL + KVL], z[:, t, QL:QL + KVL], rstd[:, 4 + t:5 + t], None, ALU.mult)\
                 .then_inc(sem("cn_ready"), 1)
            for t in range(LT):
                rope(z[:, t, QL + KVL:QL + KVL + RD], const("cos32")[:, t * RD:(t + 1) * RD], const("sin32")[:, t * RD:(t + 1) * RD],
                     1, RD, rh[:, 3584 + 32 * t:3616 + 32 * t], None).then_inc(sem("krope_done"), 1)
            ve.wait_ge(sem("kr_mm"), at("kr_mm", 1))
            V.tensor_copy(kT[64:96, 0, :], bank[5][64:96, :]).then_inc(sem("kT_rope"), 1)
            for g in range(0, 20, 2):
                latent_done(ve, g)
                if g < MH:
                    V.tensor_scalar(qT[0:QD, g, :], bank[g % 4][0:QD, :], MLA_SCALE, None, ALU.mult).then_inc(sem("lat_v"), 1)
                elif g < 2 * MH:
                    V.tensor_copy(kT[0:NOPE, g - MH, :], bank[g % 4][0:NOPE, :]).then_inc(sem("lat_v"), 1)
                else:
                    V.tensor_copy(z[:, g - 2 * MH, 0:MH * MV], bank[g % 4][:, :]).then_inc(sem("lat_v"), 1)
            ve.wait_ge(sem("lat_v"), at("lat_v", 10))
            ve.wait_ge(sem("lat_a"), at("lat_a", 10))
            ve.wait_ge(sem("krope_done"), at("krope_done", LT))
            for i in range(4):
                ve.wait_ge(sem("qrot_mm"), at("qrot_mm", i + 1))
                t1 = rh[64:96, 3584:4096].rearrange("p (h n) -> p h n", h=2)
                if i:
                    ve.wait_ge(sem("qT_ready"), at("qT_ready", i))
                V.tensor_tensor(t1, bank[6 + i % 2][64:96, :].rearrange("p (h n) -> p h n", h=2),
                                const("sinT")[64:96, :].unsqueeze(1).to_broadcast([32, 2, SEQ]), ALU.mult).then_inc(sem("qrot_read"), 1)
                ve.wait_ge(sem("qrot_read"), at("qrot_read", i + 1))
                qr = qT[64:96, 2 * i:2 * i + 2, 0:SEQ]
                link(V.tensor_tensor(qr, qr, const("cosT")[64:96, :].unsqueeze(1).to_broadcast([32, 2, SEQ]), ALU.mult))
                V.tensor_tensor(qr, qr, t1, ALU.add).then_inc(sem("qT_ready"), 1)
            ve.wait_ge(sem("lam_exp"), at("lam_exp", 1))
            link(V.tensor_scalar(lamv[:, 3:4], lamv[:, 1:2], -1.0, LAM_INIT, ALU.mult, ALU.add))
            link(V.tensor_tensor(lamv[:, 2:3], lamv[:, 0:1], lamv[:, 3:4], ALU.add))

            attend(0, 0)
            link(V.reciprocal(rinv[:, 0:32], rsum[:, 0:32]))
            arrived(ve, SEL)
            V.tensor_copy(slot_r[SEL % SLOTS][:, 2048:4096], slot[SEL % SLOTS][:, 0:2048]).then_inc(sem("sel_ready"), 1)
            rv = rinv[:, 0:32].rearrange("p (h t) -> p t h", t=NT)
            for t in range(NT):
                V.tensor_tensor(heads(z[:, t, 0:512]), heads(bank[4 + t][:, :]), per_head(rv[:, t, :]), ALU.mult)\
                 .then_inc(sem("o_mla"), 1)
            ve.wait_ge(sem("o_mla"), at("o_mla", NT))
            V.tensor_copy(rstd[:, 0:1], rstd[:, 1:2]).then_inc(sem("o_read0"), 4)

            def low_part(i):
                ve.wait_ge(sem("split_hi"), at("split_hi", i + 1))
                V.tensor_tensor(d_lo[:, i, :], bank[4 + i % 2][:, :], d_hi[:, i, :].bitcast(f32), ALU.subtract).then_inc(sem("split_lo"), 1)
            low_part(0)
            low_part(1)
            for g in range(0, 32, 2):
                ve.wait_ge(sem("dT_tr"), at("dT_tr", g + 1))
                V.tensor_copy(dops[g // 16][g % 16], bank[g % 4][:, :]).then_inc(sem("dT_v"), 1)
                if g % 4 == 2 and g // 4 + 2 < 8:
                    low_part(g // 4 + 2)

            def diff_out(gi):
                c0 = (gi % 2) * 32
                link(V.reciprocal(rinv[:, c0:c0 + 32], rsum[:, c0:c0 + 32]))
                rv = rinv[:, c0:c0 + 32].rearrange("p (h c i) -> p c i h", c=2, i=2)
                for i in range(2):
                    link(V.tensor_scalar(rv[:, 1, i, :], rv[:, 1, i, :], lamv[:, 2:3], None, ALU.mult))
                    V.tensor_tensor(heads(tmp[0]), heads(bank[4 + i][:, :]), per_head(rv[:, 0, i, :]), ALU.mult)
                    link(V.tensor_tensor(heads(tmp[1]), heads(bank[6 + i][:, :]), per_head(rv[:, 1, i, :]), ALU.mult))
                    V.tensor_tensor(diff_o(gi, i), tmp[0], tmp[1], ALU.subtract).then_inc(sem("o_read0"), 2)
                    ve.wait_ge(sem("o_read0"), at("o_read0", 4 * gi + 2 * (i + 1)))

            def diff_o(gi, i):
                t = LT * (gi - 1) + i
                return z[:, t, ZQ:ZQ + 512]

            def diff_squares(gi, i):
                link(V.tensor_tensor(tmp[i], diff_o(gi, i), diff_o(gi, i), ALU.mult))
                V.tensor_reduce(stat[:, 8 * i:8 * i + 8], heads(tmp[i]), AX, ALU.add).then_inc(sem("sums_ready"), 1)
                sums_n[0] += 1

            def diff_norm(gi, i):
                ob = diff_o(gi, i)
                rms(rstd[:, 8 * i:8 * i + 8], 8, 8 * i)
                link(V.tensor_tensor(heads(ob), heads(ob), per_head(rstd[:, 8 * i:8 * i + 8]), ALU.mult))
                V.tensor_tensor(heads(ob), heads(ob), subln_b.unsqueeze(1).to_broadcast([P, 8, DV]), ALU.mult)\
                 .then_inc(sem("o_ready0"), 2)
            attend(0, 1)
            diff_out(1)
            attend(0, 2, {4: lambda: diff_squares(1, 0), 8: lambda: diff_squares(1, 1),
                          16: lambda: diff_norm(1, 0), 20: lambda: diff_norm(1, 1)})
            diff_out(2)
            for g in range(0, KD, 2):
                if g == 4:
                    for i in range(2):
                        diff_squares(2, i)
                    for i in range(2):
                        diff_norm(2, i)
                ve.wait_ge(sem("oT0_tr"), at("oT0_tr", g + 1))
                V.tensor_copy(oT[:, g, :], bank[g % 4][:, 0:NTOK]).then_inc(sem("oT0_v"), 1)
            broadcast("bc0", bc_list(0), range(2))
            out_project(0)
            experts(0)

            norm(1)
            projected(1, E1, OD_CH, zo)
            ve.wait_ge(sem("z_v1"), at("z_v1", 6))
            ve.wait_ge(sem("z_a1"), at("z_a1", 6))
            t1, t2 = rq[:, 2048:2048 + 640], rq[:, 2688:2688 + 640]
            for t in range(NT):
                h0, nh = (0, 10) if t < LT else (8, 2)
                src = zo[:, t, 768 + 64 * h0:768 + 640]
                n = 64 * nh
                sv = src.rearrange("p (h d) -> p h d", h=nh)
                link(V.tensor_tensor(t1[:, 0:n], src, src, ALU.mult))
                sums_done(V.tensor_reduce(nrm[:, 0:nh], t1[:, 0:n].rearrange("p (h d) -> p h d", h=nh), AX, ALU.add))
                rms(nrm[:, 0:nh], nh)
                link(V.tensor_tensor(sv, sv, nrm[:, 0:nh].unsqueeze(2).to_broadcast([P, nh, HD]), ALU.mult))
                if t < LT:
                    qv = src[:, 0:512].rearrange("p (h d) -> p h d", h=8)
                    link(V.tensor_tensor(qv, qv, qk_b[:, 0:64].unsqueeze(1).to_broadcast([P, 8, HD]), ALU.mult))
                kv = zo[:, t, 1280:1408].rearrange("p (h d) -> p h d", h=2)
                link(V.tensor_tensor(kv, kv, qk_b[:, 64:128].unsqueeze(1).to_broadcast([P, 2, HD]), ALU.mult))
                if t < LT:
                    link(rope(src, const("cos64")[:, t * 64:(t + 1) * 64], const("sin64")[:, t * 64:(t + 1) * 64], 10, 64, t1, t2))
            V.tensor_scalar(nsink, sink_b, -1.0, None, ALU.mult).then_inc(sem("odd_rope_d"), 1)
            ve.wait_ge(sem("odd_rope_d"), at("odd_rope_d", 1))
            modulation1(2)

            def query_lo(b):
                ve.wait_ge(sem("gx_hi"), at("gx_hi", b + 1))
                V.scalar_tensor_tensor(gx_lo[:, b, :], bank[4 + b % 2][:, 0:SEQ], ATT_SCALE, gx_hi[:, b, :].bitcast(f32),
                                       ALU.mult, ALU.subtract).then_inc(sem("gx_lo"), 1)
            query_lo(0)
            query_lo(1)
            for b in range(8):
                if b % 2 == 0:
                    ve.wait_ge(sem("g_q_tr"), at("g_q_tr", b + 1))
                    V.tensor_copy(g_q[:, 2 * b:2 * b + 2, :], bank[b % 2][:, :].rearrange("p (h n) -> p h n", h=2)).then_inc(sem("g_q_v"), 1)
                if b + 2 < 8:
                    query_lo(b + 2)
            for g in range(4):
                ve.wait_ge(sem("gk_hi"), at("gk_hi", g + 1))
                V.tensor_tensor(g_k[g][1], bank[2 + g % 2][:, :], g_k[g][0].bitcast(f32), ALU.subtract).then_inc(sem("gk_lo"), 1)
            attend(1, 0)
            nw = nmx[:, 0:32].rearrange("p (h c) -> p h c", c=4)[:, :, 0:2]
            sk = nsk.rearrange("p (h c) -> p h c", c=2)
            V.tensor_tensor(sk, nw, sink_b.unsqueeze(2).to_broadcast([P, 8, 2]), ALU.add).then_inc(sem("sink_arg"), 1)
            ve.wait_ge(sem("sink_exp"), at("sink_exp", 1))
            rw = rsum[:, 0:32].rearrange("p (h c) -> p h c", c=4)[:, :, 0:2]
            link(V.tensor_tensor(rw, rw, sk, ALU.add))
            link(V.reciprocal(rinv[:, 0:32], rsum[:, 0:32]))
            rv = rinv[:, 0:32].rearrange("p (h c t) -> p c t h", c=2, t=2)
            for c in range(2):
                for t in range(2):
                    V.tensor_tensor(heads(zo[:, t, 512 * c:512 * c + 512]), heads(bank[4 + 2 * c + t][:, :]), per_head(rv[:, c, t, :]),
                                    ALU.mult).then_inc(sem("o_ready1"), 1)
            transposed("oT1", KD, lambda g: oT[:, g, 0:SEQ], SEQ)
            broadcast("bc1", bc_list(1), range(1))
            out_project(1)
            experts(1)

            rms(rstd[:, 0:LT], LT)
            ve.wait_ge(sem("nf_loaded"), at("nf_loaded", 16))
            for t in range(LT):
                V.scalar_tensor_tensor(ya[t], xt[:, t, :], rstd[:, t:t + 1], xt[:, LT, :], ALU.mult, ALU.mult)\
                 .then_inc(sem("out_ready"), 1)

        @block.scalar
        def _(ac):
            A = nc.scalar.activation
            ac.wait_ge(sem("zero_list"), at("zero_list", 1))
            for l in range(DEPTH):
                ac.dma_start(list_dram[l].rearrange("(p n) o -> p (n o)", p=P), zeros_i).then_inc(sem("list_zeroed"), 16)
            ac.wait_ge(sem("vec_sb"), at("vec_sb", 2))
            A(silu, colv[:, 0:16], ACT.Silu).then_inc(sem("silu_c"), 1)
            ac.wait_ge(sem("lam_sums"), at("lam_sums", 1))
            A(lamv[:, 0:2], lamv[:, 0:2], ACT.Exp).then_inc(sem("lam_exp"), 1)

            def sumsq(tiles, name, junk, waits):
                for t in range(tiles):
                    s_, v_ = waits(t)
                    ac.wait_ge(sem(s_), at(s_, v_))
                    if t:
                        ac.wait_ge(sem(name), at(name, t))
                    A(junk, xt[:, t, :], ACT.Square, accum_out=stat[:, t:t + 1]).then_inc(sem(name), 1)

            def modulation_rows(part, js, base):
                c0 = PARTS[part][0]
                for j in js:
                    ac.wait_ge(chunks_used, base + j + 1)
                    if c0 + j >= 2:
                        ac.wait_ge(sem("mod1_cols"), c0 + j - 1)
                    A(modrow1[(c0 + j) % 2], bank[2 + j % 2][0:2, :], ACT.Copy).then_inc(sem("mod1_row"), 1)

            def root(sums, n, of, o=0):
                A(roots[:, o:o + n], sums, ACT.Sqrt, scale=1.0 / of, bias=const("eps")).then_inc(sem("root_ready"), 1)

            sums_n = [0]

            def root_of_sums(sums, n, of, o=0):
                sums_n[0] += 1
                ac.wait_ge(sem("sums_ready"), at("sums_ready", sums_n[0]))
                root(sums, n, of, o)

            def weight_hi(l, base, chunks, i, half):
                n, w, k = base + i, chunks[i][1], slice(4 * half, 4 * half + 4)
                arrived(ac, n)
                if i:
                    if half == 0:
                        ac.wait_ge(sem(f"w_half{l}"), at(f"w_half{l}", i))
                    else:
                        ac.wait_ge(chunks_used, base + i)
                A(w_hi[:, k, 0:w], slotk[n % SLOTS][:, k, 0:w], ACT.Copy).then_inc(sem(f"w_hi{l}"), 1)

            def norm(l):
                if l == 0:
                    ac.wait_ge(sem("mod_cols"), MODC)
                for half in range(2):
                    weight_hi(l, E0 if l == 0 else E1, EV_CH if l == 0 else OD_CH, 0, half)
                for k in range(KD):
                    ac.wait_ge(sem(f"xT1_{l}"), at(f"xT1_{l}", k // 2 + 1))
                    ac.wait_ge(sem(f"scol{l}"), at(f"scol{l}", 2))
                    A(hT[:, k, SEQ:NTOK], bank[6 + (k // 2) % 2][:, (k % 2) * 256:(k % 2 + 1) * 256], ACT.Identity,
                      scale=scols[l][:, 8 + k:9 + k], bias=mod(l, 0, 1)[:, k:k + 1]).then_inc(sem(f"hT1_{l}"), 1)
                    ac.wait_ge(sem(f"hT0_{l}"), at(f"hT0_{l}", k + 1))
                    ac.wait_ge(sem(f"hT1_{l}"), at(f"hT1_{l}", k + 1))
                    A(hT_hi[:, k, :], hT[:, k, :], ACT.Copy).then_inc(sem(f"h_part{l}"), 1)

            def projected(l, base, chunks, zz):
                g = 0
                for i, (o, w, tiles) in enumerate(chunks):
                    if i + 1 < len(chunks):
                        weight_hi(l, base, chunks, i + 1, 0)
                    for t in range(tiles):
                        if g % 2 == 1:
                            product_done(ac, f"z_mm{l}", base, [c[2] for c in chunks], i, t)
                            A(zz[:, t, o:o + w], bank[4 * (i % 2) + t][:, 0:w], ACT.Copy).then_inc(sem(f"z_a{l}"), 1)
                        g += 1
                    if i + 1 < len(chunks):
                        weight_hi(l, base, chunks, i + 1, 1)

            def attend(l, gi, between={}):
                units, b = GROUPS[l][gi], GBASE[l][gi]
                for u in range(len(units)):
                    if u in between:
                        between[u]()
                    n = b + u
                    ac.wait_ge(sem(f"max_ready{l}"), at(f"max_ready{l}", n + 1))
                    if n >= 4:
                        ac.wait_ge(sem(f"t_ready{l}"), at(f"t_ready{l}", n - 3))
                    nk = units[u][2]
                    c = (gi % 2) * 32 + u
                    A(probs[n % 4][:, 0:nk], bank[n % 2][:, 0:nk], ACT.Exp, bias=nmx[:, n % 64:n % 64 + 1],
                      accum_out=rsum[:, c:c + 1]).then_inc(sem(f"p_ready{l}"), 1)

            def transposed(name, blocks, dst, n, scale=1.0):
                for g in range(1, blocks, 2):
                    ac.wait_ge(sem(f"{name}_tr"), at(f"{name}_tr", g + 1))
                    A(dst(g), bank[g % 4][:, 0:n], ACT.Copy, scale=scale).then_inc(sem(f"{name}_a"), 1)

            def broadcast(name, cols):
                for i in range(len(cols)):
                    ac.wait_ge(sem(f"{name}_mm"), at(f"{name}_mm", i + 1))
                    A(bc[cols[i][0]][:, 512:1024], bank[5 + 2 * (i % 2)][:, :], ACT.Copy).then_inc(sem(f"{name}_a"), 1)

            def experts(l):
                T = TL[l]
                def token_cols(t):
                    ac.wait_ge(sem(f"h_hi{l}"), at(f"h_hi{l}", t + 1))
                    A(hT[:, 4:8, t * P:(t + 1) * P], bank[5 + 2 * (t % 2)][:, :].rearrange("p (k n) -> p k n", k=4), ACT.Copy)\
                     .then_inc(sem(f"h_a{l}"), 1)

                def token_store(t):
                    ac.wait_ge(sem(f"h_ready{l}"), at(f"h_ready{l}", t + 1))
                    ac.dma_start(h_dram[l][t * P:(t + 1) * P, :], htok[t % 2]).then_inc(sem(f"h_stored{l}_{t % 2}"), 16)
                for t in range(T):
                    ac.wait_ge(sem(f"x_add{l}"), at(f"x_add{l}", T + t + 1))
                    A(junk, xt[:, t, :], ACT.Square, accum_out=stat[:, t:t + 1]).then_inc(sem(f"sumsq_f{l}"), 1)
                    ac.wait_ge(sem(f"sumsq_f{l}"), at(f"sumsq_f{l}", t + 1))
                    root(stat[:, t:t + 1], 1, D, t)
                    if t >= 1:
                        token_cols(t - 1)
                    token_store(t)
                token_cols(T - 1)
                ac.wait_ge(sem(f"logits{l}"), at(f"logits{l}", 1))
                A(r_s[:, 0:T * NE], bank[0][:, 0:T * NE], ACT.Sigmoid).then_inc(sem(f"sig{l}"), 1)
                if l == 0:
                    modulation_rows(0, [0, 1], MA)
                broadcast(f"gf{l}", gate_list(l))
                if l == 0:
                    modulation_rows(0, [2, 3], MA)

                def rows_hi(buf, e):
                    for h in range(2):
                        name = ("xT_lo", "xT_hi")[h] + str(l)
                        ac.wait_ge(sem(name), at(name, e + 1))
                        A(xg_hi[buf][:, 4 * h:4 * h + 4, :], bank[h][:, :].rearrange("p (k n) -> p k n", k=4), ACT.Copy)\
                         .then_inc(sem(f"xgT_a{l}"), 1)

                def quarter_hi(u, it, e, q):
                    base = X0 if l == 0 else X1
                    n = base + 3 * u + q // 2
                    if q % 2 == 0:
                        arrived(ac, n, it)
                    if q == 0:
                        ac.wait_ge(chunks_used, e * 3 + base - 1)
                    if q == 3:
                        ac.wait_ge(sem(f"gate_half{l}"), at(f"gate_half{l}", e + 1))
                    k = 4 * (q % 2)
                    for part in quarter[q]:
                        m = part.shape[1]
                        ins = A(part, slotk[n % SLOTS][:, k:k + m, :], ACT.Copy)
                        k += m
                    ins.then_inc(sem(f"ex_hi{l}"), 1)

                def pair(it, last_pair):
                    for u in range(2):
                        e = it * 2 + u
                        quarter_hi(u, it, e, 3)
                        ac.wait_ge(chunks_used, e * 3 + (X0 if l == 0 else X1) + 1)
                        ac.wait_ge(sem(f"act_ready{l}"), at(f"act_ready{l}", e))
                        A(sg[u], bank[2][:, :], ACT.Silu).then_inc(sem(f"silu_ready{l}"), 1)
                        if not (last_pair and u == 1):
                            rows_hi(1 - u, e + 1)
                        ac.wait_ge(sem(f"act_tr{l}"), at(f"act_tr{l}", e + 1))
                        A(actT[u], bank[4][:, :].rearrange("p (j n) -> p j n", j=4), ACT.Copy).then_inc(sem(f"actT_ready{l}"), 1)
                        if not (last_pair and u == 1):
                            for q in range(3):
                                quarter_hi(1 - u, it + u, e + 1, q)
                        ac.wait_ge(chunks_used, e * 3 + (X0 if l == 0 else X1) + 3)
                        ac.wait_ge(sem(f"y_stored{l}_{u}"), at(f"y_stored{l}_{u}", it * 16))
                        A(ybuf[u][:, 512:1024], bank[6][:, :], ACT.Copy).then_inc(sem(f"y_a{l}"), 1)
                        ac.wait_ge(sem(f"y_v{l}"), at(f"y_v{l}", e + 1))
                        ac.wait_ge(sem(f"y_a{l}"), at(f"y_a{l}", e + 1))
                        dst = y_dram[l][0:P * NE, :].rearrange("(s e) d -> s e d", e=NE)
                        if isinstance(e, int):
                            dst = dst[:, e, :]
                        else:
                            dst = dst[:, ds(e, 1), :].rearrange("s e d -> s (e d)")
                        ac.dma_start(dst, ybuf[u]).then_inc(sem(f"y_stored{l}_{u}"), 16)
                for q in range(3):
                    if l == 0 and q == 2:
                        ac.wait_ge(sem("mod1_cols"), PARTS[0][1])
                    quarter_hi(0, 0, 0, q)
                rows_hi(0, 0)
                pair(0, False)
                with ac.Fori(1, NE // 2 - 1) as it:
                    pair(it, False)
                pair(NE // 2 - 1, True)

                ac.wait_ge(sem(f"flag_set{l}"), at(f"flag_set{l}", 1))
                over = ac.value_load(flag_i[l][0:1, :], min_val=0, max_val=1)
                with ac.If(over > 0):
                    with ac.Fori(0, ROUNDS[l]) as r:
                        with ac.Fori(0, NE) as e:
                            i = r * NE + e
                            ac.wait_ge(sem(f"over_used{l}"), at(f"over_used{l}", i * 3 + 2))
                            A(sg[0], bank[2][:, :], ACT.Silu).then_inc(sem(f"over_silu{l}"), 1)
                            ac.wait_ge(sem(f"over_act_tr{l}"), at(f"over_act_tr{l}", i + 1))
                            A(actT[0], bank[4][:, :].rearrange("p (j n) -> p j n", j=4), ACT.Copy).then_inc(sem(f"over_actT{l}"), 1)
                            ac.wait_ge(sem(f"over_y{l}"), at(f"over_y{l}", i * 2 + 2))
                            dst = y_dram[l][ds(r * (P * NE) + P * NE, P * NE), :].rearrange("(s e) d -> s e d", e=NE)
                            ac.dma_start(dst[:, ds(e, 1), :].rearrange("s e d -> s (e d)"), ybuf[0]).then_inc(sem(f"over_stored{l}"), 16)
                ac.nop()

            ac.wait_ge(sem("x_loaded"), at("x_loaded", 32))
            for t in range(NT):
                A(rh[:, 0:D], xt[:, t, :], ACT.Square, accum_out=stat[:, t:t + 1]).then_inc(sem("sumsq0"), 1)
                ac.wait_ge(sem("sumsq0"), at("sumsq0", t + 1))
                root(stat[:, t:t + 1], 1, D, t)
            norm(0)
            projected(0, E0, EV_CH, z)
            ac.wait_ge(chunks_used, U0)
            ac.wait_ge(sem("z_v0"), at("z_v0", 10))
            ac.wait_ge(sem("z_a0"), at("z_a0", 10))
            for t in range(NT):
                if t:
                    ac.wait_ge(sem("lat_sums"), at("lat_sums", 2 * t))
                A(rh[:, 0:QL], z[:, t, 0:QL], ACT.Square, accum_out=stat[:, t:t + 1]).then_inc(sem("lat_sums"), 1)
                A(rh[:, QL:QL + KVL], z[:, t, QL:QL + KVL], ACT.Square, accum_out=stat[:, 4 + t:5 + t]).then_inc(sem("lat_sums"), 1)
            ac.wait_ge(sem("lat_sums"), at("lat_sums", 2 * NT))
            root(stat[:, 0:4], 4, QL)
            A(roots[:, 4:8], stat[:, 4:8], ACT.Sqrt, scale=1.0 / KVL, bias=const("eps")).then_inc(sem("root_ready"), 1)
            for b in range(5):
                ac.wait_ge(sem("ct_tr"), at("ct_tr", b + 1))
                A(cT[:, b, :], bank[4 + b % 4][:, :], ACT.Copy, scale=colv[:, C_NQ + b:C_NQ + b + 1]).then_inc(sem("ct_ready"), 1)
            for g in range(1, 20, 2):
                latent_done(ac, g)
                if g < MH:
                    ins = A(qT[0:QD, g, :], bank[g % 4][0:QD, :], ACT.Copy, scale=MLA_SCALE)
                elif g < 2 * MH:
                    ins = A(kT[0:NOPE, g - MH, :], bank[g % 4][0:NOPE, :], ACT.Copy)
                else:
                    ins = A(z[:, g - 2 * MH, 0:MH * MV], bank[g % 4][:, :], ACT.Copy)
                ins.then_inc(sem("lat_a"), 1)
            attend(0, 0)

            def high_part(i):
                ac.wait_ge(sem("diff_tr"), at("diff_tr", i + 1))
                A(d_hi[:, i, :], bank[4 + i % 2][:, :], ACT.Copy).then_inc(sem("split_hi"), 1)
            high_part(0)
            high_part(1)
            for g in range(1, 32, 2):
                ac.wait_ge(sem("dT_tr"), at("dT_tr", g + 1))
                A(dops[g // 16][g % 16], bank[g % 4][:, :], ACT.Copy).then_inc(sem("dT_a"), 1)
                if g % 4 == 3 and g // 4 + 2 < 8:
                    high_part(g // 4 + 2)
            diff_roots = lambda i: root_of_sums(stat[:, 8 * i:8 * i + 8], 8, DV, 8 * i)
            attend(0, 1)
            attend(0, 2, {12: lambda: diff_roots(0), 14: lambda: diff_roots(1)})
            for g in range(1, KD, 2):
                if g == 5:
                    diff_roots(0)
                    diff_roots(1)
                ac.wait_ge(sem("oT0_tr"), at("oT0_tr", g + 1))
                A(oT[:, g, :], bank[g % 4][:, 0:NTOK], ACT.Copy).then_inc(sem("oT0_a"), 1)
            broadcast("bc0", bc_list(0))
            experts(0)
            modulation_rows(1, [0, 1, 2, 3], MB)
            for t in range(NT):
                ac.wait_ge(sem("x_moe0"), at("x_moe0", t + 1))
                A(rh[:, 0:D], xt[:, t, :], ACT.Square, accum_out=stat[:, t:t + 1]).then_inc(sem("sumsq1"), 1)
                ac.wait_ge(sem("sumsq1"), at("sumsq1", t + 1))
                root(stat[:, t:t + 1], 1, D, t)
                if t < 2:
                    modulation_rows(1, [4 + t], MB)
            norm(1)
            projected(1, E1, OD_CH, zo)
            for t in range(NT):
                if t >= 2:
                    modulation_rows(2, [t - 2], MC_)
                root_of_sums(nrm[:, 0:10 if t < LT else 2], 10 if t < LT else 2, HD)

            def query_hi(b):
                ac.wait_ge(sem("gx_tr"), at("gx_tr", b + 1))
                A(gx_hi[:, b, :], bank[4 + b % 2][:, 0:SEQ], ACT.Copy, scale=ATT_SCALE).then_inc(sem("gx_hi"), 1)
            query_hi(0)
            query_hi(1)
            for b in range(8):
                if b % 2 == 1:
                    ac.wait_ge(sem("g_q_tr"), at("g_q_tr", b + 1))
                    A(g_q[:, 2 * b:2 * b + 2, :], bank[b % 2][:, :].rearrange("p (h n) -> p h n", h=2), ACT.Copy).then_inc(sem("g_q_a"), 1)
                if b + 2 < 8:
                    query_hi(b + 2)
            for g in range(4):
                ac.wait_ge(sem("gk_tr"), at("gk_tr", g + 1))
                A(g_k[g][0], bank[2 + g % 2][:, :], ACT.Copy).then_inc(sem("gk_hi"), 1)
            attend(1, 0)
            ac.wait_ge(sem("sink_arg"), at("sink_arg", 1))
            A(nsk, nsk, ACT.Exp).then_inc(sem("sink_exp"), 1)
            transposed("oT1", KD, lambda g: oT[:, g, 0:SEQ], SEQ)
            broadcast("bc1", bc_list(1))
            experts(1)
            sumsq(LT, "sumsq_out", rh[:, 0:D], lambda t: ("x_moe1", t + 1))
            ac.wait_ge(sem("sumsq_out"), at("sumsq_out", LT))
            root(stat[:, 0:LT], LT, D)
            for t in range(LT):
                ac.wait_ge(sem("out_ready"), at("out_ready", t + 1))
                ac.dma_start(out_dram[0, t * P:(t + 1) * P, :], ya[t]).then_inc(sem("out_stored"), 16)
            ac.wait_ge(sem("out_stored"), at("out_stored", 16 * LT))

        @block.gpsimd
        def _(gp):
            G = nc.gpsimd
            n_done = [0]

            def link(ins):
                n_done[0] += 1
                ins.then_inc(sem("g_chain"), 1)
                gp.wait_ge(sem("g_chain"), at("g_chain", n_done[0]))
            G.memset(zeros_i, 0).then_inc(sem("zero_list"), 1)

            def rope(src, cos, sin, heads, d, t1):
                q = d // 4
                s4 = src.rearrange("p (h x a q) -> p h x a q", h=heads, x=2, a=2)
                t4 = t1.rearrange("p (h x a q) -> p h x a q", h=heads, x=2, a=2)
                n4 = sin.rearrange("p (x a q) -> p x a q", x=2, a=2)
                for i in range(2):
                    link(G.tensor_tensor(t4[:, :, :, i, :], s4[:, :, :, 1 - i, :],
                                         n4[:, :, i, :].unsqueeze(1).to_broadcast([P, heads, 2, q]), ALU.mult))
                s2 = src.rearrange("p (h d) -> p h d", h=heads)
                link(G.tensor_tensor(s2, s2, cos.unsqueeze(1).to_broadcast([P, heads, d]), ALU.mult))
                return G.tensor_tensor(src, src, t1, ALU.add)

            def experts(l):
                T = TL[l]
                gp.wait_ge(sem(f"idx{l}"), at(f"idx{l}", 2))
                gp.wait_ge(sem("list_zeroed"), at("list_zeroed", 32))
                for t in range(T):
                    for idx in (idx_hi, idx_lo):
                        gp.indirect_dma_start(out=list_dram[l], out_offset=bass.IndirectOffsetOnAxis(idx[:, t:t + 1], 0),
                                              in_=tokid_i[:, t:t + 1], in_offset=None).then_inc(sem(f"listed{l}"), 16)
                gp.wait_ge(sem(f"listed{l}"), at(f"listed{l}", 32 * T))
                gp.dma_start(slots_i, list_dram[l][0:P * NE, :].rearrange("(s e) o -> s (e o)", e=NE)).then_inc(sem(f"slots{l}"), 16)
                gp.wait_ge(sem(f"slots{l}"), at(f"slots{l}", 16))
                for b in range(2):
                    gp.wait_ge(sem(f"h_stored{l}_{b}"), at(f"h_stored{l}_{b}", 8 * T))
                for e in range(NE):
                    if e >= 2:
                        gp.wait_ge(sem(f"xT_hi{l}"), at(f"xT_hi{l}", e - 1))
                    gp.indirect_dma_start(out=xg[e % 2], out_offset=None, in_=h_dram[l],
                                          in_offset=bass.IndirectOffsetOnAxis(slots_i[:, e:e + 1], 0)).then_inc(sem(f"xg_loaded{l}_{e % 2}"), 16)
                over = gp.value_load(flag_i[l][0:1, :], min_val=0, max_val=1)
                with gp.If(over > 0):
                    gp.wait_ge(sem(f"xT_hi{l}"), at(f"xT_hi{l}", NE))
                    for i in range(ROUNDS[l] * NE):
                        r, e = i // NE + 1, i % NE
                        if i:
                            gp.wait_ge(sem(f"over_stored{l}"), at(f"over_stored{l}", 16 * i))
                        if e == 0:
                            gp.dma_start(slots_i, list_dram[l][r * P * NE:(r + 1) * P * NE, :].rearrange("(s e) o -> s (e o)", e=NE))\
                              .then_inc(sem(f"over_idx{l}"), 16)
                            gp.wait_ge(sem(f"over_idx{l}"), at(f"over_idx{l}", 16 * r))
                        gp.indirect_dma_start(out=xg[0], out_offset=None, in_=h_dram[l],
                                              in_offset=bass.IndirectOffsetOnAxis(slots_i[:, e:e + 1], 0)).then_inc(sem(f"over_xg{l}"), 16)
                    gp.wait_ge(sem(f"over_stored{l}"), at(f"over_stored{l}", 16 * ROUNDS[l] * NE))
                gp.nop()
                for b in range(2):
                    gp.wait_ge(sem(f"y_stored{l}_{b}"), at(f"y_stored{l}_{b}", 8 * NE))

                def result_rows(rows):
                    for t in range(T):
                        for buf, idx, name in ((yb, idx_lo, "yb"), (ya, idx_hi, "ya")):
                            gp.indirect_dma_start(out=buf[t], out_offset=None, in_=rows,
                                                  in_offset=bass.IndirectOffsetOnAxis(idx[:, t:t + 1], 0))\
                              .then_inc(sem(f"{name}_loaded{l}_{t}"), 16)
                with gp.If(over > 0):
                    result_rows(y_dram[l])
                gp.nop()
                with gp.If(over < 1):
                    result_rows(y_dram[l][0:P * NE, :])
                gp.nop()
                for t in range(T):
                    gp.wait_ge(sem(f"y_sum{l}"), at(f"y_sum{l}", t + 1))
                    G.tensor_tensor(xt[:, t, :], xt[:, t, :], ya[t], ALU.add).then_inc(sem(f"x_moe{l}"), 1)

            gp.wait_ge(chunks_used, U0)
            gp.wait_ge(sem("z_v0"), at("z_v0", 10))
            gp.wait_ge(sem("z_a0"), at("z_a0", 10))
            gp.wait_ge(sem("small_loaded"), at("small_loaded", 16 * SMALL_LOADS))
            for t in range(LT):
                ins = rope(z[:, t, ZQ:ZQ + 1024], const("cos32")[:, t * RD:(t + 1) * RD], const("sin32")[:, t * RD:(t + 1) * RD],
                           32, 32, rh[:, 2560:3584])
                link(ins)
            for t in range(NT):
                G.tensor_scalar(z[:, t, ZQ:ZQ + 512], z[:, t, ZQ:ZQ + 512], DIFF_SCALE, None, ALU.mult)\
                 .then_inc(sem("diff_rope"), 1)
            gp.wait_ge(sem("kT_rope"), at("kT_rope", 1))
            gp.wait_ge(sem("diff_rope"), at("diff_rope", NT))
            G.tensor_copy(kT[64:96, 1:MH, :], kT[64:96, 0:1, :].to_broadcast([32, MH - 1, NTOK])).then_inc(sem("kT_ready"), 1)
            experts(0)
            gp.wait_ge(sem("z_v1"), at("z_v1", 6))
            gp.wait_ge(sem("z_a1"), at("z_a1", 6))
            for t in range(LT):
                ins = rope(zo[:, t, 0:640], const("cos64")[:, t * 64:(t + 1) * 64], const("sin64")[:, t * 64:(t + 1) * 64],
                           10, 64, rq[:, 3328:3968])
                link(ins)
            gp.wait_ge(sem("odd_rope_d"), at("odd_rope_d", 1))
            for g in range(4):
                o = (512 if g < 2 else 1280) + (g % 2) * HD
                for t in range(NT):
                    kd = kdup[:, (g * NT + t) * P:(g * NT + t + 1) * P].rearrange("p (c d) -> p c d", c=2)
                    ins = G.tensor_copy(kd, zo[:, t, o:o + HD].unsqueeze(1).to_broadcast([P, 2, HD]))
            ins.then_inc(sem("odd_rope_w"), 1)
            experts(1)


_INS = ["x", "c", "ctx", "c_ctx", "w_mod", "b_mod", "norm_mix", "norm_ffn", "even_w_in", "even_norm_q", "even_norm_kv",
        "even_w_uq", "even_w_ukv", "even_lambda", "even_subln", "even_w_out", "odd_w_in", "odd_sink", "odd_q_norm",
        "odd_k_norm", "odd_w_out", "w_router", "b_router", "w_gate", "w_up", "w_down", "norm_final"]


def kernel(**inputs):
    import concourse.bacc as bacc
    from concourse.bass_utils import run_bass_kernel_spmd

    nc = bacc.Bacc("TRN2", target_bir_lowering=False, num_devices=1)
    arrays = {f"in_{n}": np.ascontiguousarray(inputs[n]) for n in _INS}
    arrays["shape_consts"] = shape_constants()
    aps = {n: nc.dram_tensor(n, v.shape, mybir.dt.from_np(v.dtype), kind="ExternalInput").ap() for n, v in arrays.items()}
    out = nc.dram_tensor("out", (1, SEQ, D), mybir.dt.float32, kind="ExternalOutput").ap()
    build(nc, {n: aps[f"in_{n}"] for n in _INS}, aps["shape_consts"], out)
    r = run_bass_kernel_spmd(nc, [arrays], core_ids=[0])
    return r.results[0]["out"]
```
